# Optimizing a Trainium2 kernel written in Bass

```python
import jax, jax.numpy as jnp
from jax import lax
import numpy as np

D_MODEL = 1024
BATCH = 1
SEQ = 1024
DEPTH = 1
DEC_BATCH = 1
DEC_SEQ = 64
PAST_LEN = 2048

CHUNK = 64
D_MIX = D_MODEL
POOL_WIDTH = D_MIX // 2
POOL_WINDOWS = (2, 4, 8, 16)
N_POOL_GROUPS = len(POOL_WINDOWS)
POOL_GROUP_W = POOL_WIDTH // N_POOL_GROUPS
POOL_HIST = max(POOL_WINDOWS) - 1
HEAD_DIM = 64
N_HEADS = (D_MIX - POOL_WIDTH) // HEAD_DIM
N_KV_HEADS = 2
GQ = N_HEADS // N_KV_HEADS
ATTN_WIDTH = N_HEADS * HEAD_DIM
KV_WIDTH = N_KV_HEADS * HEAD_DIM
IN_WIDTH = POOL_WIDTH + ATTN_WIDTH + 2 * KV_WIDTH
WINDOW = 128
PREV_CHUNKS = WINDOW // CHUNK
N_EXPERTS = 64
TOP_K = 6
N_EXPERT_GROUPS = 8
TOPK_GROUPS = 4
D_EXPERT = 256
D_SHARED = 256
ROUTED_SCALE = 2.5
EXPERT_BLOCK = 128
NORM_EPS = 1e-6

kernel_name = 'streaming_pool_swa_sink_moe'

def rmsnorm(x, g):
    xf = x.astype(jnp.float32)
    y = xf * lax.rsqrt(jnp.mean(xf * xf, axis=-1, keepdims=True) + NORM_EPS) * g.astype(jnp.float32)
    return y.astype(x.dtype)

def adaln(c, w_ada, b_ada):
    m = (jax.nn.silu(c) @ w_ada + b_ada).reshape(c.shape[0], 6, 1, c.shape[-1])
    return m[:, 0], m[:, 1], m[:, 2], m[:, 3], m[:, 4], m[:, 5]

def pool_mixer(u_ext, n_new, w_pool, pool_scale):
    B, L, C = u_ext.shape
    uf = u_ext.astype(jnp.float32).reshape(B, L, N_POOL_GROUPS, POOL_GROUP_W)
    cs = jnp.concatenate([jnp.zeros((B, 1, N_POOL_GROUPS, POOL_GROUP_W), jnp.float32),
                          jnp.cumsum(uf, axis=1)], axis=1)
    j = np.arange(L - n_new, L)
    means = []
    for g, w in enumerate(POOL_WINDOWS):
        lo = np.maximum(j + 1 - w, 0)
        cnt = np.minimum(j + 1, w).astype(np.float32)
        means.append((cs[:, j + 1, g] - cs[:, lo, g]) / cnt[None, :, None])
    d = jnp.stack(means, axis=2) - uf[:, L - n_new:]
    y = jnp.einsum('btgc,gcd->btgd', d, w_pool.astype(jnp.float32)).reshape(B, n_new, C)
    return (y * pool_scale.astype(jnp.float32)).astype(u_ext.dtype)

def sink_probs(scores, sink):
    m = jnp.maximum(jnp.max(scores, axis=-1, keepdims=True), sink)
    p = jnp.exp(scores - m)
    return p / (jnp.sum(p, axis=-1, keepdims=True) + jnp.exp(sink - m))

def banded_window_attention(q, k, v, sinks):
    B, S = q.shape[0], q.shape[1]
    NC = S // CHUNK
    NK = (PREV_CHUNKS + 1) * CHUNK
    qb = q.reshape(B, NC, CHUNK, N_KV_HEADS, GQ, HEAD_DIM)
    pad = ((0, 0), (PREV_CHUNKS * CHUNK, 0), (0, 0), (0, 0))
    kp = jnp.pad(k, pad).reshape(B, NC + PREV_CHUNKS, CHUNK, N_KV_HEADS, HEAD_DIM)
    vp = jnp.pad(v, pad).reshape(B, NC + PREV_CHUNKS, CHUNK, N_KV_HEADS, HEAD_DIM)
    kb = jnp.concatenate([kp[:, i:i + NC] for i in range(PREV_CHUNKS + 1)], axis=2)
    vb = jnp.concatenate([vp[:, i:i + NC] for i in range(PREV_CHUNKS + 1)], axis=2)
    scores = jnp.einsum('bnqkgd,bnskd->bnkgqs', qb, kb).astype(jnp.float32) * (HEAD_DIM ** -0.5)
    key_pos = np.arange(NC)[:, None] * CHUNK + np.arange(NK)[None, :] - PREV_CHUNKS * CHUNK
    valid = (key_pos >= 0)[None, :, None, None, None, :]
    scores = jnp.where(valid, scores, -jnp.inf)
    sink = sinks.astype(jnp.float32).reshape(N_KV_HEADS, GQ)[None, None, :, :, None, None]
    p = sink_probs(scores, sink).astype(v.dtype)
    o = jnp.einsum('bnkgqs,bnskd->bnqkgd', p, vb)
    return o.reshape(B, S, ATTN_WIDTH)

def cached_window_attention(q, k_ext, v_ext, sinks):
    B, T = q.shape[0], q.shape[1]
    qs = q.reshape(B, T, N_KV_HEADS, GQ, HEAD_DIM)
    scores = jnp.einsum('btkgd,bskd->bkgts', qs, k_ext).astype(jnp.float32) * (HEAD_DIM ** -0.5)
    sink = sinks.astype(jnp.float32).reshape(N_KV_HEADS, GQ)[None, :, :, None, None]
    p = sink_probs(scores, sink).astype(v_ext.dtype)
    o = jnp.einsum('bkgts,bskd->btkgd', p, v_ext)
    return o.reshape(B, T, ATTN_WIDTH)

def swiglu(h, wg, wu, wd):
    return (jax.nn.silu(h @ wg) * (h @ wu)) @ wd

def routed_moe(h, w_router, router_bias, w_gate, w_up, w_down):
    N, D = h.shape
    scores = jax.nn.sigmoid((h @ w_router).astype(jnp.float32))
    sel = scores + router_bias.astype(jnp.float32)
    grp = sel.reshape(N, N_EXPERT_GROUPS, N_EXPERTS // N_EXPERT_GROUPS)
    group_score = jnp.sum(lax.top_k(grp, 2)[0], axis=-1)
    _, gidx = lax.top_k(group_score, TOPK_GROUPS)
    gmask = jnp.sum(jax.nn.one_hot(gidx, N_EXPERT_GROUPS, dtype=jnp.float32), axis=-2) > 0
    emask = jnp.repeat(gmask, N_EXPERTS // N_EXPERT_GROUPS, axis=-1)
    _, eidx = lax.top_k(jnp.where(emask, sel, -jnp.inf), TOP_K)
    wts = jnp.take_along_axis(scores, eidx, axis=-1)
    wts = wts / jnp.sum(wts, axis=-1, keepdims=True) * ROUTED_SCALE
    A = N * TOP_K
    flat_e = eidx.reshape(A)
    flat_t = jnp.repeat(jnp.arange(N, dtype=jnp.int32), TOP_K)
    flat_w = wts.reshape(A)
    order = jnp.argsort(flat_e)
    se = flat_e[order]
    counts = jnp.bincount(flat_e, length=N_EXPERTS)
    starts = jnp.cumsum(counts) - counts
    padded = (counts + EXPERT_BLOCK - 1) // EXPERT_BLOCK * EXPERT_BLOCK
    pstarts = jnp.cumsum(padded) - padded
    pends = pstarts + padded
    dest = pstarts[se] + jnp.arange(A) - starts[se]
    n_blocks = -(-(A + N_EXPERTS * (EXPERT_BLOCK - 1)) // EXPERT_BLOCK)
    P = n_blocks * EXPERT_BLOCK
    tok_buf = jnp.full((P,), N, jnp.int32).at[dest].set(flat_t[order])
    w_buf = jnp.zeros((P,), jnp.float32).at[dest].set(flat_w[order])
    block_start = jnp.arange(n_blocks) * EXPERT_BLOCK
    block_e = jnp.minimum(jnp.sum(block_start[:, None] >= pends[None, :], axis=-1), N_EXPERTS - 1)
    x_pad = jnp.concatenate([h, jnp.zeros((1, D), h.dtype)], axis=0)
    xb = x_pad[tok_buf].reshape(n_blocks, EXPERT_BLOCK, D)

    def expert_block(args):
        xblk, e = args
        return swiglu(xblk, w_gate[e], w_up[e], w_down[e])

    yb = lax.map(expert_block, (xb, block_e))
    y = jnp.zeros((N + 1, D), jnp.float32).at[tok_buf].add(
        yb.reshape(P, D).astype(jnp.float32) * w_buf[:, None])
    return y[:N].astype(h.dtype)

def trunk_layer(x, c, lp, pool_hist, k_hist, v_hist):
    (w_ada, b_ada, norm_gains, w_in, w_pool, pool_scale, attn_sinks, w_out,
     w_router, router_bias, w_gate, w_up, w_down, ws_gate, ws_up, ws_down) = lp
    B, T, D = x.shape
    sh_m, sc_m, gt_m, sh_f, sc_f, gt_f = adaln(c, w_ada, b_ada)
    h = rmsnorm(x, norm_gains[0]) * (1 + sc_m) + sh_m
    proj = h @ w_in
    u = proj[..., :POOL_WIDTH]
    q = proj[..., POOL_WIDTH:POOL_WIDTH + ATTN_WIDTH].reshape(B, T, N_HEADS, HEAD_DIM)
    o_k = POOL_WIDTH + ATTN_WIDTH
    k = proj[..., o_k:o_k + KV_WIDTH].reshape(B, T, N_KV_HEADS, HEAD_DIM)
    v = proj[..., o_k + KV_WIDTH:].reshape(B, T, N_KV_HEADS, HEAD_DIM)
    if pool_hist is None:
        u_ext, k_ext, v_ext = u, k, v
        attn = banded_window_attention(q, k, v, attn_sinks)
    else:
        u_ext = jnp.concatenate([pool_hist.astype(u.dtype), u], axis=1)
        k_ext = jnp.concatenate([k_hist.astype(k.dtype), k], axis=1)
        v_ext = jnp.concatenate([v_hist.astype(v.dtype), v], axis=1)
        attn = cached_window_attention(q, k_ext, v_ext, attn_sinks)
    pool = pool_mixer(u_ext, T, w_pool, pool_scale)
    mix = jnp.concatenate([pool, attn], axis=-1) @ w_out
    x = x + gt_m * rmsnorm(mix, norm_gains[1])
    h = (rmsnorm(x, norm_gains[2]) * (1 + sc_f) + sh_f).reshape(B * T, D)
    ffn = routed_moe(h, w_router, router_bias, w_gate, w_up, w_down) + swiglu(h, ws_gate, ws_up, ws_down)
    x = x + gt_f * rmsnorm(ffn.reshape(B, T, D), norm_gains[3])
    return x, u_ext[:, -POOL_HIST:], k_ext[:, -WINDOW:], v_ext[:, -WINDOW:]

def setup_inputs(seed: int = 0) -> dict:
    key = jax.random.key(seed)
    ks = jax.random.split(key, 24)

    def nrm(k, shape, scale):
        return jax.random.normal(k, shape, jnp.float32) * scale

    kv_rows = min(WINDOW, PAST_LEN)
    return {
        'x_prompt': nrm(ks[0], (BATCH, SEQ, D_MODEL), 1.0),
        'x_sample': nrm(ks[1], (DEC_BATCH, DEC_SEQ, D_MODEL), 1.0),
        'c_prompt': nrm(ks[2], (BATCH, D_MODEL), 1.0),
        'c_sample': nrm(ks[3], (DEC_BATCH, D_MODEL), 1.0),
        'state_pool': nrm(ks[4], (DEPTH, DEC_BATCH, POOL_HIST, POOL_WIDTH), 1.0),
        'cache_k': nrm(ks[5], (DEPTH, DEC_BATCH, kv_rows, N_KV_HEADS, HEAD_DIM), 1.0),
        'cache_v': nrm(ks[6], (DEPTH, DEC_BATCH, kv_rows, N_KV_HEADS, HEAD_DIM), 1.0),
        'w_ada': nrm(ks[7], (DEPTH, D_MODEL, 6 * D_MODEL), 0.5 * D_MODEL ** -0.5),
        'b_ada': nrm(ks[8], (DEPTH, 6 * D_MODEL), 0.02),
        'norm_gains': 1.0 + nrm(ks[9], (DEPTH, 4, D_MODEL), 0.05),
        'w_in': nrm(ks[10], (DEPTH, D_MODEL, IN_WIDTH), D_MODEL ** -0.5),
        'w_pool': nrm(ks[11], (DEPTH, N_POOL_GROUPS, POOL_GROUP_W, POOL_GROUP_W), POOL_GROUP_W ** -0.5),
        'pool_scale': 1.0 + nrm(ks[12], (DEPTH, POOL_WIDTH), 0.05),
        'attn_sinks': nrm(ks[13], (DEPTH, N_HEADS), 0.5),
        'w_out': nrm(ks[14], (DEPTH, D_MIX, D_MODEL), D_MIX ** -0.5),
        'w_router': nrm(ks[15], (DEPTH, D_MODEL, N_EXPERTS), D_MODEL ** -0.5),
        'router_bias': nrm(ks[16], (DEPTH, N_EXPERTS), 0.01),
        'w_gate': nrm(ks[17], (DEPTH, N_EXPERTS, D_MODEL, D_EXPERT), D_MODEL ** -0.5),
        'w_up': nrm(ks[18], (DEPTH, N_EXPERTS, D_MODEL, D_EXPERT), D_MODEL ** -0.5),
        'w_down': nrm(ks[19], (DEPTH, N_EXPERTS, D_EXPERT, D_MODEL), D_EXPERT ** -0.5),
        'ws_gate': nrm(ks[20], (DEPTH, D_MODEL, D_SHARED), D_MODEL ** -0.5),
        'ws_up': nrm(ks[21], (DEPTH, D_MODEL, D_SHARED), D_MODEL ** -0.5),
        'ws_down': nrm(ks[22], (DEPTH, D_SHARED, D_MODEL), D_SHARED ** -0.5),
    }

def reference(x_prompt, x_sample, c_prompt, c_sample, state_pool, cache_k, cache_v,
              w_ada, b_ada, norm_gains, w_in, w_pool, pool_scale, attn_sinks, w_out,
              w_router, router_bias, w_gate, w_up, w_down, ws_gate, ws_up, ws_down):
    yp, ys = x_prompt, x_sample
    pool_p, k_p, v_p, pool_s, k_s, v_s = [], [], [], [], [], []
    for l in range(DEPTH):
        lp = (w_ada[l], b_ada[l], norm_gains[l], w_in[l], w_pool[l], pool_scale[l], attn_sinks[l], w_out[l],
              w_router[l], router_bias[l], w_gate[l], w_up[l], w_down[l], ws_gate[l], ws_up[l], ws_down[l])
        yp, sp, kp, vp = trunk_layer(yp, c_prompt, lp, None, None, None)
        ys, ss, kss, vss = trunk_layer(ys, c_sample, lp, state_pool[l], cache_k[l], cache_v[l])
        pool_p.append(sp); k_p.append(kp); v_p.append(vp)
        pool_s.append(ss); k_s.append(kss); v_s.append(vss)
    new_pool_prompt = jnp.stack(pool_p)
    new_k_prompt = jnp.stack(k_p)
    new_v_prompt = jnp.stack(v_p)
    new_pool_sample = jnp.stack(pool_s)
    new_k_sample = jnp.stack(k_s)
    new_v_sample = jnp.stack(v_s)
    return (yp, ys, new_pool_prompt, new_k_prompt, new_v_prompt, new_pool_sample, new_k_sample, new_v_sample)


_drawn_inputs = setup_inputs


def setup_inputs(seed=0):
    import zlib

    import numpy as np

    out = dict(_drawn_inputs(seed))
    spreads = {}
    factors = {'attn_sinks': 8.0}
    for name, (base, spread) in spreads.items():
        noise = np.random.default_rng([zlib.crc32(name.encode()), seed]).standard_normal(out[name].shape)
        drawn = base * np.exp(spread * noise) if base else spread * noise
        out[name] = __import__('jax').numpy.asarray(drawn.astype(out[name].dtype))
    for name, factor in factors.items():
        out[name] = (out[name] * factor).astype(out[name].dtype)
    return out
```

```python
from contextlib import ExitStack

import concourse.bass as bass
from concourse import mybir

F32 = mybir.dt.float32
BF16 = mybir.dt.bfloat16
I32 = mybir.dt.int32
U32 = mybir.dt.uint32
ALU = mybir.AluOpType
ACT = mybir.ActivationFunctionType
AX = mybir.AxisListType

P = 128
D = 1024
KD = D // P
SEQ, DEC = 1024, 64
N = SEQ + DEC
NT = -(-N // P)
ROWS = [min(P, N - P * t) for t in range(NT)]
CHUNK = 64
PW = 512
WINDOWS = (2, 4, 8, 16)
NG = len(WINDOWS)
HIST = max(WINDOWS) - 1
HD = 64
NJ = 4
KV = 128
WIN = 128
INW = PW + 512 + 2 * KV
NE, TOPK, EG, TOPG = 64, 6, 8, 4
DE = 256
KF = DE // P
SCALE_R = 2.5
EPS = 1e-6
MAX_TILES = -(-(N * TOPK + NE * P) // P)
TAB = MAX_TILES + 4
RING = 4
WSLOT = KD * 2 * DE + KF * D

UL = HIST + SEQ + HIST + DEC
US = HIST + SEQ
KL = SEQ + WIN + DEC
BLOCKS = [(0, 512), (512, 512), (1024, DEC)]

CHUNKS = [(0, 0, 64, "v", -1), (64, 0, 128, "v", 0)]
for _c in range(2, SEQ // CHUNK):
    CHUNKS.append((64 * _c, 64 * (_c - 2), 192, "odd" if _c % 2 else "v", (_c - 2) // 2))
CHUNKS.append((SEQ, SEQ, 192, "v", SEQ // P))


def build(nc, x_prompt, x_sample, c_prompt, c_sample, state_pool, cache_k, cache_v, w_ada, b_ada,
          norm_gains, w_in, w_pool, pool_scale, attn_sinks, w_out, w_router, router_bias,
          w_gate, w_up, w_down, ws_gate, ws_up, ws_down,
          y_prompt, y_sample, pool_p, k_p, v_p, pool_s, k_s, v_s):
    with ExitStack() as ctx:
        def sb(name, shape, dt=F32):
            return ctx.enter_context(nc.sbuf_tensor(name, shape, dt))

        def sem(name):
            return ctx.enter_context(nc.semaphore(name))

        h2_rows = nc.dram_tensor("h2_rows", (N, D), F32, kind="Internal").ap()
        y_acc = nc.dram_tensor("y_acc", (N + P, D), F32, kind="Internal").ap()

        x = sb("x", [P, NT, D])
        rowsb = sb("rowsb", [P, 4, 2, D])
        tr = sb("tr", [P, KD * N])
        big = sb("big", [P, RING * WSLOT])
        colv = sb("colv", [P, 100])
        sil = sb("sil", [P, KD, 2])
        mods = sb("mods", [P, 48, 2])
        a1 = sb("a1", [P, KD, 2])
        rowsrc = sb("rowsrc", [P, 4, KD, 2])
        ident = sb("ident", [P, P])
        ones = sb("ones", [P, P])
        onesb = sb("onesb", [P, P], BF16)
        triub = sb("triub", [P, P], BF16)
        iota1 = sb("iota1", [P, P])
        base = sb("base", [P, TAB])
        padcol = sb("padcol", [P, 1])
        prow = sb("prow", [P, 1])
        iotae = sb("iotae", [P, NE])
        lower8 = sb("lower8", [P, EG, EG])
        rec = sb("rec", [P, 16])
        ss = sb("ss", [P, NT])
        rstd = sb("rstd", [P, NT])
        ss1 = sb("ss1", [P, NT])
        r1 = sb("r1", [P, NT])
        ss2 = sb("ss2", [P, NT])
        r2 = sb("r2", [P, NT])
        ss3 = sb("ss3", [P, NT])
        r3 = sb("r3", [P, NT])
        sink = sb("sink", [P, NJ])
        wrt = sb("wrt", [P, KD, NE])
        rbias = sb("rbias", [P, NE])
        wtab = sb("wtab", [P, TAB])
        itab = sb("itab", [P, TAB])
        idxg = sb("idxg", [P, 1], I32)
        idxs = sb("idxs", [P, 1], I32)
        sl = sb("sl", [P, 4])
        etab = sb("etab", [1, TAB], I32)
        lasti = sb("lasti", [1, NE], I32)

        hT = tr[:, :].rearrange("p (k n) -> p k n", k=KD)
        def tr_at(at, n):
            return tr[:, at:at + n]
        xg = tr_at(0, D)
        xT = tr_at(D, D).rearrange("p (k n) -> p k n", k=KD)
        yw = tr_at(2 * D, D)
        oh = tr_at(3 * D, NT * P // 2).bitcast(BF16).rearrange("p (t s) -> p t s", t=NT)
        sg = tr_at(4 * D, DE)
        act_m = tr_at(4 * D + DE, DE)
        actT_m = tr_at(4 * D + 2 * DE, DE).rearrange("p (k n) -> p k n", k=KF)

        def at(a, n):
            return big[:, a:a + n]
        ada = [at(KD * D * s, KD * D).rearrange("p (k n) -> p k n", k=KD) for s in range(3)]
        q = at(0, NJ * N).rearrange("p (j n) -> p j n", j=NJ)
        kT = at(NJ * N, KL)
        w1 = at(WSLOT, KD * INW).rearrange("p (k n) -> p k n", k=KD)
        wo = at(WSLOT, KD * D).rearrange("p (k n) -> p k n", k=KD)
        vat = WSLOT + KD * INW
        vt = at(vat, 10 * KV).rearrange("p (t n) -> p t n", n=KV)
        sF = WSLOT + KD * D
        tmpf = at(sF, D)
        junkf = at(sF + D, D)
        h2p = [at(sF + 2 * D, D), at(sF + 3 * D, D)]
        assert sF + 4 * D <= 3 * WSLOT and vat + 10 * KV <= 3 * WSLOT and NJ * N + KL <= WSLOT
        u = at(3 * WSLOT, NG * UL).rearrange("p (g n) -> p g n", g=NG)
        vodd = at(3 * WSLOT + NG * UL, 8 * KV).rearrange("p (t n) -> p t n", n=KV)
        assert NG * UL + 8 * KV <= WSLOT
        wpool = at(vat + 10 * KV, NG * P).rearrange("p (g n) -> p g n", g=NG)
        assert vat + 10 * KV + NG * P <= 3 * WSLOT
        diag = at(3 * WSLOT, 8 * P).rearrange("p (b k n) -> p b k n", b=2, k=4)
        at_g = [2 * WSLOT]
        def g_buf(n):
            at_g[0] += n
            assert at_g[0] <= sF + 2 * D
            return at(at_g[0] - n, n)
        shy = [g_buf(D), g_buf(D)]
        sgs, ups, acts = g_buf(DE), g_buf(DE), g_buf(DE)
        actTs = g_buf(KF * P).rearrange("p (k n) -> p k n", k=KF)
        def wslot(s):
            return at(WSLOT * s, WSLOT)
        wsh = wslot(3)

        def gate_up(w):
            return w[:, 0:KD * 2 * DE].rearrange("p (m k n) -> p m k n", m=2, k=KD)

        def down(w):
            return w[:, KD * 2 * DE:WSLOT].rearrange("p (k n) -> p k n", k=KF)

        def y_t(t):
            return at(D * t, D)

        scr = rowsb[:, 1:3, :, :].rearrange("p a b n -> p (a b n)")
        junk = scr[:, 0:D]
        xn = [scr[:, D:2 * D], scr[:, 2 * D:3 * D]]
        sums = [scr[:, 0:UL], scr[:, UL:2 * UL]]
        fix = scr[:, 2 * UL:2 * UL + 16]
        probs = [scr[:, 768 * b:768 * (b + 1)].rearrange("p (j n) -> p j n", j=NJ) for b in range(2)]
        pta = [scr[:, 1536 + 512 * b:2048 + 512 * b].rearrange("p (j n) -> p j n", j=NJ) for b in range(2)]
        ptb = [scr[0:64, 2560 + 512 * b:3072 + 512 * b].rearrange("p (j n) -> p j n", j=NJ) for b in range(2)]
        small = scr[:, 3584:3712].rearrange("p (b v j) -> p b v j", b=2, v=16)
        row0 = rowsb[:, 0, :, :].rearrange("p c n -> p (c n)")
        row3 = rowsb[:, 3, :, :].rearrange("p c n -> p (c n)")
        qbd = [row0[:, 512 * b:512 * (b + 1)].rearrange("p (j n) -> p j n", j=NJ) for b in range(2)]
        outst_p = row0[0:HIST, 1024:2048].rearrange("p (a n) -> p a n", a=2)
        outst_k = row3[:, 0:2 * KV].rearrange("p (a n) -> p a n", a=2)
        stin = row3[0:HIST, 256:256 + PW]
        ckin = row3[:, 768:768 + KV]
        stg = row3[0:100, 896:896 + P]

        hb = rowsb[:, 0:3, :, :].rearrange("p a b n -> p (a b n)")
        at_h = [0]
        def h_buf(n):
            at_h[0] += n
            assert at_h[0] <= 3 * 2 * D
            return hb[:, at_h[0] - n:at_h[0]]
        wp = h_buf(NT * NE * 5 // 2).bitcast(BF16).rearrange("p (t e c) -> p t e c", t=NT, e=NE)
        pos = h_buf(NT * NE).rearrange("p (e t) -> p e t", t=NT)
        score = h_buf(NT * NE).rearrange("p (t e) -> p t e", t=NT)
        rtmp = h_buf(NT * NE * TOPK // 2)
        sel = h_buf(NT * NE).rearrange("p (t e) -> p t e", t=NT)
        mask = h_buf(NT * NE).rearrange("p (t e) -> p t e", t=NT)
        g8 = h_buf(NT * EG * 8).rearrange("p (t g n) -> p t g n", t=NT, g=EG)
        def small_g(n, k=NT):
            return g_buf(n * k).rearrange("p (t n) -> p t n", t=k)
        maskb = g_buf(NT * NE // 2).bitcast(BF16).rearrange("p (t e) -> p t e", t=NT)
        gs, gm, top8, ixf = small_g(EG), small_g(EG), small_g(8), small_g(8)
        ix8 = g_buf(NT * 8).bitcast(U32).rearrange("p (t n) -> p t n", t=NT)
        cnt, ntl, tst = g_buf(NE), g_buf(NE), g_buf(NE)
        den = sb("den", [P, NT])
        tend = sb("tend", [P, NE])

        ps = ctx.enter_context(nc.psum_tensor("ps", [P, 8, 512], F32))

        def bank(b):
            return ps[:, b, :]

        def pair(b):
            return ps[:, b:b + 2, :].rearrange("p b n -> p (b n)")

        const_pool = sem("const_pool")
        small_in = sem("small_in")
        misc_in = sem("misc_in")
        ada_in = [sem(f"ada_in{s}") for s in range(3)]
        x_in = [sem(f"x_in{t}") for t in range(NT)]
        w_in_s = sem("w_in_s")
        w_out_s = sem("w_out_s")
        stg_t = sem("stg_t")
        colv_s = sem("colv_s")
        sil_s = sem("sil_s")
        ada_mm = sem("ada_mm")
        mods_s = sem("mods_s")
        diag_s = sem("diag_s")
        row_mm = sem("row_mm")
        row_s = sem("row_s")
        dchain = sem("dchain")
        achain = sem("achain")
        pchain = sem("pchain")
        ss_s = sem("ss_s")
        ms_s = sem("ms_s")
        sq_s = sem("sq_s")
        rstd_s = sem("rstd_s")
        xn_s = sem("xn_s")
        ht_mm = sem("ht_mm")
        ht_s = sem("ht_s")
        misc_mm = sem("misc_mm")
        misc_ev = sem("misc_ev")
        uz_s = sem("uz_s")
        proj_mm = sem("proj_mm")
        ev_act = sem("ev_act")
        ev_dve = sem("ev_dve")
        outs_mm = sem("outs_mm")
        outs_ev = sem("outs_ev")
        stored = sem("stored")
        outs_st = sem("outs_st")
        pool_st = sem("pool_st")
        wpool_s = sem("wpool_s")
        dstep = sem("dstep")
        pool_turn = sem("pool_turn")
        pooled = sem("pooled")
        vodd_s = sem("vodd_s")
        qbd_s = sem("qbd_s")
        sc_mm = sem("sc_mm")
        mx_s = sem("mx_s")
        ex_s = sem("ex_s")
        pr_s = sem("pr_s")
        pt_mm = sem("pt_mm")
        pta_s = sem("pta_s")
        ptb_s = sem("ptb_s")
        pv_mm = sem("pv_mm")
        o_s = sem("o_s")
        mix_mm = sem("mix_mm")
        ssm_s = sem("ssm_s")
        msm_s = sem("msm_s")
        sqm_s = sem("sqm_s")
        res_s = sem("res_s")
        x1_s = sem("x1_s")
        ssx_s = sem("ssx_s")
        msx_s = sem("msx_s")
        sqx_s = sem("sqx_s")
        h2a_s = sem("h2a_s")
        h2_s = sem("h2_s")
        h2_st = [sem(f"h2_st{b}") for b in range(2)]
        h2t_mm = sem("h2t_mm")
        h2t_s = sem("h2t_s")
        log_mm = sem("log_mm")
        score_s = sem("score_s")
        wsh_s = sem("wsh_s")
        shg_mm = sem("shg_mm")
        shs_s = sem("shs_s")
        sha_s = sem("sha_s")
        sht_mm = sem("sht_mm")
        sht_s = sem("sht_s")
        shd_mm = sem("shd_mm")
        shy_s = sem("shy_s")
        shy_st = [sem(f"shy_st{b}") for b in range(2)]
        maskb_s = sem("maskb_s")
        rank_mm = sem("rank_mm")
        tables = sem("tables")
        w_slot_s = [sem(f"w_slot{s}") for s in range(RING)]
        w_ready = sem("w_ready")
        oh_s = sem("oh_s")
        slot_mm = sem("slot_mm")
        idx_s = sem("idx_s")
        gathered = sem("gathered")
        xt_mm = sem("xt_mm")
        xt_s = sem("xt_s")
        gu_mm = sem("gu_mm")
        silu_s = sem("silu_s")
        act_s = sem("act_s")
        at_mm = sem("at_mm")
        at_s = sem("at_s")
        dn_mm = sem("dn_mm")
        yw_s = sem("yw_s")
        added = sem("added")
        y_in = [sem(f"y_in{t}") for t in range(NT)]
        fin_ss = sem("fin_ss")
        fin_ms = sem("fin_ms")
        fin_sq = sem("fin_sq")
        fin_g = sem("fin_g")
        fin_s = sem("fin_s")

        def chained(eng, s):
            n = [0]

            def link(ins):
                n[0] += 1
                ins.then_inc(s, 1)
                eng.wait_ge(s, n[0])
            return link

        def rows_of(prompt, sample, t):
            return prompt[0, P * t:P * (t + 1), :] if t < SEQ // P else sample[0, :, :]

        ada_view = w_ada[0].rearrange("(k p) n -> p k n", p=P)
        gate_v = w_gate[0].rearrange("e (p k) n -> e p (k n)", k=KD)
        up_v = w_up[0].rearrange("e (p k) n -> e p (k n)", k=KD)
        down_v = w_down[0].rearrange("e (k p) n -> e p k n", p=P)

        groups = []
        for ct in range(9):
            for a, n_ in BLOCKS:
                groups.append(("ct", ct, a, n_))
        for g in range(3):
            groups.append(("v", g, 0, 0))
        for g in range(NG):
            for a, n_ in BLOCKS:
                groups.append(("pool", g, a, n_))

        def evac_group(eng, n, kind, c, a, n_, scalar_engine):
            src = bank(n % 4)
            def copy(out, in_):
                if scalar_engine:
                    return eng.activation(out, in_, ACT.Copy)
                return eng.tensor_copy(out, in_)
            if kind == "v":
                if c < 2:
                    return copy(vt[:, 4 * c:4 * c + 4, :], src.rearrange("p (t n) -> p t n", t=4))
                return copy(vt[0:DEC, 9, :], src[0:DEC, 0:KV])
            if kind == "pool":
                out, sc = hT[:, c, a:a + n_], colv[:, 96 + c:97 + c]
                if scalar_engine:
                    return eng.activation(out, src[:, 0:n_], ACT.Copy, scale=sc)
                return eng.tensor_scalar(out, src[:, 0:n_], sc, None, ALU.mult)
            if c < NG:
                to = HIST + a if a < SEQ else US + HIST
                return copy(u[:, c, to:to + n_], src[:, 0:n_])
            if c < 8:
                return copy(q[:, c - 4, a:a + n_], src[:, 0:n_])
            to = a if a < SEQ else SEQ + WIN
            return copy(kT[:, to:to + n_], src[:, 0:n_])

        NCH = len(CHUNKS)
        N_PROJ = 30

        block = ctx.enter_context(nc.Block())

        @block.sync
        def _(sp):
            sp.dma_start(stg[0:48, :], b_ada[0].rearrange("(r n) -> r n", n=P)).then_inc(small_in, 16)
            sp.dma_start(stg[48:80, :], norm_gains[0].rearrange("g (r n) -> (g r) n", n=P)).then_inc(small_in, 16)
            sp.dma_start(stg[80:88, :], c_prompt[0].rearrange("(r n) -> r n", n=P)).then_inc(small_in, 16)
            sp.dma_start(stg[88:96, :], c_sample[0].rearrange("(r n) -> r n", n=P)).then_inc(small_in, 16)
            sp.dma_start(stg[96:100, :], pool_scale[0].rearrange("(r n) -> r n", n=P)).then_inc(small_in, 16)
            for v in range(6):
                if v >= 3:
                    sp.wait_ge(ada_mm, v - 2)
                sp.dma_start(ada[v % 3], ada_view[:, :, D * v:D * (v + 1)]).then_inc(ada_in[v % 3], 16)
                if v == 1:
                    for t in range(NT):
                        sp.dma_start(x[0:ROWS[t], t, :], rows_of(x_prompt, x_sample, t)).then_inc(x_in[t], 16)
            sp.wait_ge(ada_mm, 6)
            sp.dma_start(w1, w_in[0].rearrange("(k p) n -> p k n", p=P)).then_inc(w_in_s, 16)
            sp.dma_start(wpool, w_pool[0].rearrange("g c d -> c g d")).then_inc(wpool_s, 16)
            sp.dma_start(vt[:, 8, :], cache_v[0, 0].rearrange("s h d -> s (h d)")).then_inc(vodd_s, 16)
            sp.wait_ge(ev_act, 15)
            sp.wait_ge(ev_dve, 15)
            sp.dma_start(vodd[0:64, 0:8, :], vt[64:128, 0:8, :]).then_inc(vodd_s, 16)
            sp.dma_start(vodd[64:128, 0:7, :], vt[0:64, 1:8, :]).then_inc(vodd_s, 16)
            sp.dma_start(v_p[0, 0].rearrange("s h d -> s (h d)"), vt[:, 7, :]).then_inc(stored, 16)
            sp.dma_start(v_s[0, 0, DEC:WIN].rearrange("s h d -> s (h d)"), vt[0:DEC, 9, :]).then_inc(stored, 16)
            sp.wait_ge(proj_mm, N_PROJ)
            sp.dma_start(wo[:, 0:NG, :], w_out[0, 0:PW].rearrange("(k p) n -> p k n", p=P)).then_inc(w_out_s, 16)
            for h in range(2):
                src = w_out[0, PW + 256 * h:PW + 256 * (h + 1)].rearrange("(j d) n -> d j n", d=HD)
                sp.dma_start(wo[64 * h:64 * h + 64, NG:NG + NJ, :], src).then_inc(w_out_s, 16)
            def load_expert(g, s):
                w = gate_up(wslot(s))
                def of(v):
                    return v.rearrange("(g s) p n -> s g p n", s=RING)[s, bass.ds(g, 1)].rearrange("a p n -> (a p) n")
                sp.dma_start(w[:, 0].rearrange("p k n -> p (k n)"), of(gate_v)).then_inc(w_slot_s[s], 16)
                sp.dma_start(w[:, 1].rearrange("p k n -> p (k n)"), of(up_v)).then_inc(w_slot_s[s], 16)
                d = down_v.rearrange("(g s) p k n -> s g p k n", s=RING)[s, bass.ds(g, 1)]
                sp.dma_start(down(wslot(s)), d.rearrange("a p k n -> (a p) k n"))\
                  .then_inc(w_slot_s[s], 16)

            sp.wait_ge(pv_mm, NCH)
            load_expert(0, 0)
            sp.wait_ge(row_s, 16)
            gu = gate_up(wsh)
            sp.dma_start(gu[:, 0].rearrange("p k n -> p (k n)"), ws_gate[0].rearrange("(p k) n -> p (k n)", k=KD)).then_inc(wsh_s, 16)
            sp.dma_start(gu[:, 1].rearrange("p k n -> p (k n)"), ws_up[0].rearrange("(p k) n -> p (k n)", k=KD)).then_inc(wsh_s, 16)
            sp.dma_start(down(wsh), ws_down[0].rearrange("(k p) n -> p k n", p=P)).then_inc(wsh_s, 16)
            for t in range(NT):
                sp.wait_ge(h2_s, t + 1)
                sp.dma_start(h2_rows[P * t:P * t + ROWS[t], :], h2p[t % 2][0:ROWS[t], :]).then_inc(h2_st[t % 2], 16)
            sp.wait_ge(mix_mm, NT)
            sp.wait_ge(h2t_mm, NT)
            sp.wait_ge(h2_st[0], 16 * ((NT + 1) // 2))
            sp.wait_ge(h2_st[1], 16 * (NT // 2))
            sp.wait_ge(h2_s, NT)
            load_expert(0, 1)
            for t in range(NT):
                sp.wait_ge(shy_s, t + 1)
                sp.dma_start(y_acc[P * t:P * t + ROWS[t], :], shy[t % 2][0:ROWS[t], :]).then_inc(shy_st[t % 2], 16)
            load_expert(0, 3)
            for b in range(2):
                sp.wait_ge(shy_st[b], 16 * ((NT + 1 - b) // 2))
            sp.wait_ge(tables, 1)
            load_expert(0, 2)
            sp.wait_ge(w_slot_s[0], 48)
            sp.sem_inc(w_ready, 1)
            sp.wait_ge(w_slot_s[1], 48)
            sp.sem_inc(w_ready, 1)
            sp.wait_ge(w_slot_s[2], 48)
            sp.sem_inc(w_ready, 1)
            with sp.Fori(1, NE // RING) as g:
                for s in range(RING):
                    last_of = sp.value_load(lasti[0:1, :].rearrange("a (g s) -> a s g", s=RING)[:, s, bass.ds(g - 1, 1)], min_val=0, max_val=MAX_TILES - 1)
                    sp.wait_ge(dn_mm, last_of + 1)
                    load_expert(g, s)
                    if s == 0:
                        sp.wait_ge(w_slot_s[RING - 1], g * 48)
                    else:
                        sp.wait_ge(w_slot_s[s - 1], g * 48 + 48)
                    sp.sem_inc(w_ready, 1)
            sp.wait_ge(w_slot_s[RING - 1], 48 * NE // RING)
            sp.sem_inc(w_ready, 1)

            last = sp.value_load(lasti[0:1, NE - 1:NE], min_val=NE - 1, max_val=MAX_TILES - 1)
            sp.wait_ge(added, 16 * (last + 2))
            for t in range(NT):
                sp.dma_start(y_t(t)[0:ROWS[t], :], y_acc[P * t:P * t + ROWS[t], :]).then_inc(y_in[t], 16)
            for t in range(NT):
                sp.wait_ge(fin_s, t + 1)
                sp.dma_start(rows_of(y_prompt, y_sample, t), x[0:ROWS[t], t, :]).then_inc(stored, 16)
            sp.wait_ge(stored, 16 * (2 + NT))
            sp.wait_ge(outs_st, 64)
            sp.wait_ge(pool_st, 32)

        @block.gpsimd
        def _(pool):
            link = chained(pool, pchain)
            pool.dma_start(sink[0:64, :], attn_sinks[0:1, 0:NJ].to_broadcast([64, NJ])).then_inc(misc_in, 16)
            pool.dma_start(sink[64:128, :], attn_sinks[0:1, NJ:2 * NJ].to_broadcast([64, NJ])).then_inc(misc_in, 16)
            pool.dma_start(rbias[:, :], router_bias[0:1, :].to_broadcast([P, NE])).then_inc(misc_in, 16)
            pool.dma_start(wrt[:, :, :].rearrange("p k n -> p (k n)"), w_router[0].rearrange("(p k) n -> p (k n)", k=KD)).then_inc(misc_in, 16)
            pool.dma_start(stin[:, :], state_pool[0, 0]).then_inc(misc_in, 16)
            pool.dma_start(ckin[:, :], cache_k[0, 0].rearrange("s h d -> s (h d)")).then_inc(misc_in, 16)
            pool.dma_start(k_s[0, 0, 0:DEC], cache_k[0, 0, DEC:WIN]).then_inc(pool_st, 16)
            pool.dma_start(v_s[0, 0, 0:DEC], cache_v[0, 0, DEC:WIN]).then_inc(pool_st, 16)
            pool.dma_start(y_acc[N:N + P, :], x_prompt[0, 0:P, :]).then_inc(added, 16)
            link(pool.memset(ident[:, :], 0.0))
            pool.affine_select(out=ident[:, :], in_=ident[:, :], compare_op=ALU.not_equal, fill=1.0, base=0,
                               pattern=[[-1, P]], channel_multiplier=1).then_inc(const_pool, 1)
            pool.memset(ones[:, :], 1.0)
            pool.memset(onesb[:, :], 1.0)
            link(pool.memset(triub[:, :], 1.0))
            pool.affine_select(out=triub[:, :], in_=triub[:, :], compare_op=ALU.is_gt, fill=0.0, base=0,
                               pattern=[[1, P]], channel_multiplier=-1)
            low = dict(allow_small_or_imprecise_dtypes=True)
            pool.iota(iota1[:, :], [[1, P]], base=1, channel_multiplier=0, **low)
            pool.iota(base[:, :], [[P, TAB]], base=0, channel_multiplier=0, **low)
            pool.iota(padcol[:, :], [[0, 1]], base=N + 1, channel_multiplier=1, **low)
            pool.iota(prow[:, :], [[0, 1]], base=1, channel_multiplier=1, **low)
            pool.iota(iotae[:, :], [[1, NE]], base=0, channel_multiplier=0, **low)
            pool.iota(rec[:, :], [[1, 16]], base=1, channel_multiplier=0, **low)
            link(pool.memset(lower8[:, :, :], 1.0))
            pool.affine_select(out=lower8[:, :, :], in_=lower8[:, :, :], compare_op=ALU.is_gt, fill=0.0, base=0,
                               pattern=[[1, EG], [-1, EG]], channel_multiplier=0)
            for b in range(2):
                pool.memset(qbd[b], 0.0)
            pool.memset(wtab[:, :], 0.0).then_inc(const_pool, 1)
            pool.wait_ge(const_pool, 2)
            pool.wait_ge(ada_mm, 6)
            pool.memset(u[:, :, 0:HIST], 0.0).then_inc(uz_s, 1)

            pool.wait_ge(uz_s, 1)
            pool.wait_ge(ev_act, 12)
            pool.wait_ge(ev_dve, 12)
            for n, (qc, _, _, _, _) in enumerate(CHUNKS):
                if n >= 2:
                    pool.wait_ge(sc_mm, n - 1)
                for h in range(2):
                    r = slice(64 * h, 64 * h + 64)
                    pool.tensor_copy(qbd[n % 2][r, :, r], q[r, :, qc:qc + CHUNK]).then_inc(qbd_s, 1)
                    pool.wait_ge(qbd_s, 2 * n + h + 1)

            for t in range(NT):
                r, c = slice(0, ROWS[t]), t // (SEQ // P)
                pool.wait_ge(res_s, t + 1)
                pool.tensor_tensor(x[r, t, :], x[r, t, :], tmpf[r, :], ALU.add).then_inc(x1_s, 1)
                pool.wait_ge(h2a_s, t + 1)
                if t >= 2:
                    pool.wait_ge(h2_st[t % 2], 16 * (t // 2))
                    pool.wait_ge(h2t_mm, t - 1)
                pool.tensor_tensor(h2p[t % 2][r, :].rearrange("p (k q) -> p q k", k=KD),
                                   junkf[r, :].rearrange("p (q k) -> p q k", k=KD),
                                   rowsb[r, 2, c, :].rearrange("p (q k) -> p q k", k=KD), ALU.add).then_inc(h2_s, 1)

            for t in range(NT):
                pool.wait_ge(shs_s, 2 * (t + 1))
                if t >= 1:
                    pool.wait_ge(sht_mm, t)
                pool.tensor_tensor(acts[0:ROWS[t], :], sgs[0:ROWS[t], :], ups[0:ROWS[t], :], ALU.mult)\
                    .then_inc(sha_s, 1)

            for b in range(2):
                pool.wait_ge(shy_st[b], 16 * ((NT + 1 - b) // 2))
            pool.wait_ge(added, 16)

            gather_bound, add_bound = pool.to_reg(N - 1), pool.to_reg(N + P - 1)

            def gather(i):
                pool.wait_ge(idx_s, i + 1)
                pool.sem_inc(pool_turn, 1)
                pool.indirect_dma_start(out=xg, out_offset=None, in_=h2_rows,
                                        in_offset=bass.IndirectOffsetOnAxis(ap=idxg[:, 0:1], axis=0),
                                        bounds_check=gather_bound, oob_is_err=False).then_inc(gathered, 16)

            def scatter_add(i):
                pool.wait_ge(yw_s, i + 2)
                pool.sem_inc(pool_turn, 1)
                pool.indirect_dma_start(out=y_acc, out_offset=bass.IndirectOffsetOnAxis(ap=idxs[:, 0:1], axis=0),
                                        in_=yw, in_offset=None, bounds_check=add_bound,
                                        compute_op=ALU.add).then_inc(added, 16)

            pool.wait_ge(shd_mm, NT)
            pool.memset(xg, 0.0).then_inc(uz_s, 1)
            pool.wait_ge(uz_s, 2)
            gather(0)
            pool.wait_ge(xt_mm, 1)
            gather(1)
            pool.wait_ge(tables, 1)
            last = pool.value_load(lasti[0:1, NE - 1:NE], min_val=NE - 1, max_val=MAX_TILES - 1)
            pool.wait_ge(xt_mm, 2)
            gather(2)
            with pool.Fori(1, MAX_TILES) as i:
                with pool.If(i <= last):
                    pool.wait_ge(xt_mm, i + 2)
                    gather(i + 2)
                    scatter_add(i - 1)
            scatter_add(last)

        @block.scalar
        def _(act):
            link = chained(act, achain)
            act.wait_ge(colv_s, 1)
            act.activation(sil[:, :, :].rearrange("p k c -> p c k"), colv[:, 80:96].rearrange("p (c k) -> p c k", c=2),
                           ACT.Silu).then_inc(sil_s, 1)
            act.wait_ge(ms_s, 1)
            for t in range(NT):
                r = slice(0, ROWS[t])
                act.wait_ge(x_in[t], 16)
                ins = act.activation(junk[r, :], x[r, t, :], ACT.Square, accum_out=ss[r, t:t + 1])
                if t < NT - 1:
                    link(ins)
                else:
                    ins.then_inc(ss_s, 1)
            act.wait_ge(ms_s, 2)
            act.activation(rstd[:, :], ss[:, :], ACT.Sqrt).then_inc(sq_s, 1)
            act.wait_ge(rstd_s, 1)
            for t in range(NT):
                r = slice(0, ROWS[t])
                if t >= 2:
                    act.wait_ge(ht_mm, t - 1)
                act.activation(xn[t % 2][r, :], x[r, t, :], ACT.Copy, scale=rstd[r, t:t + 1]).then_inc(xn_s, 1)

            def row_copies(n0, kinds):
                n = n0
                for kind in kinds:
                    for c in range(2):
                        for half in range(2):
                            act.wait_ge(row_mm, n + 1)
                            act.activation(rowsb[:, kind, c, 512 * half:512 * half + 512], bank(6 + n % 2), ACT.Copy)\
                               .then_inc(row_s, 1)
                            n += 1

            act.wait_ge(ada_mm, 6)
            for n, (kind, c, a, n_) in enumerate(groups):
                if n % 2 == 0:
                    act.wait_ge(proj_mm, n + 1)
                    evac_group(act, n, kind, c, a, n_, True).then_inc(ev_act, 1)
                if n == N_PROJ - 1:
                    act.wait_ge(outs_mm, 1)
                    act.activation(outst_p[:, 0, :], bank(4)[0:HIST, :], ACT.Copy)
                    act.activation(outst_p[:, 1, :], bank(5)[0:HIST, :], ACT.Copy)
                    act.activation(outst_k[:, 0, :], bank(6)[:, 0:KV], ACT.Copy)
                    act.activation(outst_k[0:DEC, 1, :], bank(6)[0:DEC, KV:2 * KV], ACT.Copy).then_inc(outs_ev, 1)
                    act.wait_ge(outs_ev, 1)
                    act.dma_start(pool_p[0, 0], outst_p[:, 0, :]).then_inc(outs_st, 16)
                    act.dma_start(pool_s[0, 0], outst_p[:, 1, :]).then_inc(outs_st, 16)
                    act.dma_start(k_p[0, 0].rearrange("s h d -> s (h d)"), outst_k[:, 0, :]).then_inc(outs_st, 16)
                    act.dma_start(k_s[0, 0, DEC:WIN].rearrange("s h d -> s (h d)"), outst_k[0:DEC, 1, :]).then_inc(outs_st, 16)
            act.wait_ge(pooled, NG)

            def exps(n):
                b, nk = n % 2, CHUNKS[n][2]
                act.wait_ge(mx_s, n + 1)
                if n >= 2:
                    act.wait_ge(pt_mm, n - 1)
                act.activation(small[:, b, 3, :], small[:, b, 2, :], ACT.Exp)
                for j in range(NJ):
                    src = ps[:, 2 * b + j // 2, 192 * (j % 2):192 * (j % 2) + nk]
                    ins = act.activation(probs[b][:, j, 0:nk], src, ACT.Exp, bias=small[:, b, 1, j:j + 1],
                                         scale=HD ** -0.5, accum_out=small[:, b, 4, j:j + 1])
                ins.then_inc(ex_s, 1)

            def copy_pta(n):
                act.wait_ge(pt_mm, n + 1)
                if n >= 2:
                    act.wait_ge(pv_mm, n - 1)
                nk = CHUNKS[n][2]
                if nk >= 128:
                    act.activation(pta[n % 2], bank(4).rearrange("p (j n) -> p j n", j=NJ), ACT.Copy).then_inc(pta_s, 1)
                else:
                    act.sem_inc(pta_s, 1)

            for m in range(NCH + 1):
                if m < NCH:
                    exps(m)
                if m >= 1:
                    copy_pta(m - 1)
            act.wait_ge(pv_mm, NCH)
            act.wait_ge(outs_st, 64)
            row_copies(0, range(4))

            def h2t_copy(t):
                act.wait_ge(h2t_mm, t + 1)
                act.activation(hT[:, :, P * t:P * t + ROWS[t]],
                               pair(4).rearrange("p (k n) -> p k n", k=KD)[:, :, 0:ROWS[t]], ACT.Copy).then_inc(h2t_s, 1)

            for t in range(NT):
                r = slice(0, ROWS[t])
                act.wait_ge(mix_mm, t + 1)
                if t >= 1:
                    act.wait_ge(h2_s, t)
                act.activation(junkf[r, :], pair(2 * (t % 2))[r, :], ACT.Square, accum_out=ss1[r, t:t + 1]).then_inc(ssm_s, 1)
                if t >= 1:
                    h2t_copy(t - 1)
                act.wait_ge(msm_s, t + 1)
                act.activation(r1[r, t:t + 1], ss1[r, t:t + 1], ACT.Sqrt).then_inc(sqm_s, 1)
                act.wait_ge(x1_s, t + 1)
                act.activation(junkf[r, :], x[r, t, :], ACT.Square, accum_out=ss2[r, t:t + 1]).then_inc(ssx_s, 1)
                act.wait_ge(msx_s, t + 1)
                act.activation(r2[r, t:t + 1], ss2[r, t:t + 1], ACT.Sqrt).then_inc(sqx_s, 1)
            h2t_copy(NT - 1)
            act.wait_ge(log_mm, NT)
            act.wait_ge(misc_ev, 3)
            act.activation(score[:, 0:8, :], bank(6).rearrange("p (t e) -> p t e", e=NE), ACT.Sigmoid)
            act.activation(score[0:DEC, 8, :], bank(7)[0:DEC, 0:NE], ACT.Sigmoid).then_inc(score_s, 1)

            def sh_silu(t):
                r = slice(0, ROWS[t])
                act.wait_ge(shg_mm, t + 1)
                if t >= 1:
                    act.wait_ge(sha_s, t)
                act.activation(sgs[r, :], bank(4)[r, 0:DE], ACT.Silu).then_inc(shs_s, 1)
                act.activation(ups[r, :], bank(4)[r, DE:2 * DE], ACT.Copy).then_inc(shs_s, 1)

            def sh_tail(t):
                r = slice(0, ROWS[t])
                act.wait_ge(sht_mm, t + 1)
                act.activation(actTs[:, :, r], bank(5)[:, 0:DE].rearrange("p (k n) -> p k n", k=KF)[:, :, r], ACT.Copy)\
                    .then_inc(sht_s, 1)
                act.wait_ge(shd_mm, t + 1)
                if t >= 2:
                    act.wait_ge(shy_st[t % 2], 16 * (t // 2))
                act.activation(shy[t % 2][r, :], pair(0)[r, :], ACT.Copy).then_inc(shy_s, 1)

            for t in range(NT):
                sh_silu(t)
                if t >= 1:
                    sh_tail(t - 1)
            sh_tail(NT - 1)

            def xt_copy(i):
                act.wait_ge(xt_mm, i + 1)
                act.activation(xT, pair(0).rearrange("p (k n) -> p k n", k=KD), ACT.Copy).then_inc(xt_s, 1)

            def silu_of(i):
                act.wait_ge(gu_mm, i + 1)
                act.activation(sg, bank(4)[:, 0:DE], ACT.Silu).then_inc(silu_s, 1)

            xt_copy(0)
            silu_of(0)
            xt_copy(1)
            act.wait_ge(tables, 1)
            last = act.value_load(lasti[0:1, NE - 1:NE], min_val=NE - 1, max_val=MAX_TILES - 1)
            with act.Fori(1, MAX_TILES) as i:
                with act.If(i <= last):
                    act.wait_ge(gu_mm, i + 1)
                    act.wait_ge(act_s, i)
                    act.activation(sg, bank(4)[:, 0:DE], ACT.Silu).then_inc(silu_s, 1)
                    xt_copy(i + 1)

            for t in range(NT):
                r = slice(0, ROWS[t])
                act.wait_ge(y_in[t], 16)
                ins = act.activation(hb[r, 0:D], y_t(t)[r, :], ACT.Square, accum_out=ss3[r, t:t + 1])
                if t < NT - 1:
                    link(ins)
                else:
                    ins.then_inc(fin_ss, 1)
            act.wait_ge(fin_ms, 1)
            act.activation(r3[:, :], ss3[:, :], ACT.Sqrt).then_inc(fin_sq, 1)

        @block.vector
        def _(dve):
            link = chained(dve, dchain)
            dve.memset(ss1[:, :], 1.0)
            dve.memset(ss3[:, :], 1.0)
            dve.memset(ss2[:, :], 1.0)
            dve.memset(ss[:, :], 1.0).then_inc(ms_s, 1)
            dve.wait_ge(stg_t, 1)
            dve.tensor_copy(colv[:, :], bank(7)[:, 0:100]).then_inc(colv_s, 1)
            dve.wait_ge(const_pool, 2)
            link(dve.reciprocal(rec[:, :], rec[:, :]))
            def mean_eps(s):
                return dve.tensor_scalar(s, s, 1.0 / D, EPS, ALU.mult, ALU.add)
            dve.wait_ge(ss_s, 1)
            mean_eps(ss[:, :]).then_inc(ms_s, 1)
            dve.wait_ge(sq_s, 1)
            dve.reciprocal(rstd[:, :], rstd[:, :]).then_inc(rstd_s, 1)
            dve.wait_ge(ada_mm, 6)
            dve.wait_ge(colv_s, 1)
            link(dve.tensor_tensor(mods[:, :, :], bank(6)[:, 0:96].rearrange("p (r c) -> p r c", c=2),
                                   colv[:, 0:48].unsqueeze(2).to_broadcast([P, 48, 2]), ALU.add))

            def gain(g):
                return colv[:, 48 + KD * g:48 + KD * (g + 1)].unsqueeze(2).to_broadcast([P, KD, 2])
            dve.scalar_tensor_tensor(a1[:, :, :], mods[:, 8:16, :], 1.0, gain(0), ALU.add, ALU.mult)
            dve.tensor_tensor(rowsrc[:, 0], mods[:, 16:24, :], gain(1), ALU.mult)
            dve.scalar_tensor_tensor(rowsrc[:, 1], mods[:, 32:40, :], 1.0, gain(2), ALU.add, ALU.mult)
            dve.tensor_copy(rowsrc[:, 2], mods[:, 24:32, :])
            dve.tensor_tensor(rowsrc[:, 3], mods[:, 40:48, :], gain(3), ALU.mult).then_inc(mods_s, 1)
            dve.wait_ge(mods_s, 1)
            for t in range(NT):
                c = t // (SEQ // P)
                dve.wait_ge(ht_mm, t + 1)
                src = pair(2 * (t % 2))
                for k in range(KD):
                    ins = dve.tensor_scalar(hT[:, k, P * t:P * t + ROWS[t]], src[:, P * k:P * k + ROWS[t]],
                                            a1[:, k, c:c + 1], mods[:, k, c:c + 1], ALU.mult, ALU.add)
                ins.then_inc(ht_s, 1)
            dve.wait_ge(misc_mm, 1)
            dve.tensor_copy(u[:, :, US:US + HIST], bank(4)[:, 0:NG * HIST].rearrange("p (g n) -> p g n", g=NG))
            dve.tensor_copy(kT[:, SEQ:SEQ + WIN], bank(5)[:, 0:WIN]).then_inc(misc_ev, 1)

            def diags(n0, kinds):
                n = n0
                for kind in kinds:
                    for c in range(2):
                        for half in range(2):
                            if n >= 2:
                                dve.wait_ge(row_mm, n - 1)
                            dve.tensor_tensor(diag[:, n % 2, :, :], ident[:, :].unsqueeze(1).to_broadcast([P, 4, P]),
                                              rowsrc[:, kind, 4 * half:4 * half + 4, c].unsqueeze(2).to_broadcast([P, 4, P]),
                                              ALU.mult).then_inc(diag_s, 1)
                            n += 1

            def pooling():
                dve.wait_ge(outs_mm, 1)
                dve.wait_ge(uz_s, 1)
                for g, w in enumerate(WINDOWS):
                    cur, s = u[:, g, :], 1
                    for b in range(g + 1):
                        nxt, lo = sums[b % 2], 2 * s - 1
                        link(dve.tensor_tensor(nxt[:, lo:UL], cur[:, lo:UL], cur[:, lo - s:UL - s], ALU.add))
                        cur, s = nxt, 2 * s
                    first = slice(HIST, HIST + w - 1)
                    link(dve.tensor_tensor(fix[:, 0:w - 1], cur[:, first], rec[:, 0:w - 1], ALU.mult))
                    link(dve.tensor_tensor(fix[:, 0:w - 1], fix[:, 0:w - 1], u[:, g, first], ALU.subtract))
                    link(dve.scalar_tensor_tensor(u[:, g, HIST:UL], cur[:, HIST:UL], 1.0 / w, u[:, g, HIST:UL],
                                                  ALU.mult, ALU.subtract))
                    dve.tensor_copy(u[:, g, first], fix[:, 0:w - 1]).then_inc(pooled, 1)
                    dve.wait_ge(pooled, g + 1)

            for n, (kind, c, a, n_) in enumerate(groups):
                if n % 2 == 1:
                    dve.wait_ge(proj_mm, n + 1)
                    evac_group(dve, n, kind, c, a, n_, False).then_inc(ev_dve, 1)
                if n == N_PROJ - 1:
                    dve.wait_ge(ev_act, N_PROJ // 2)
                    dve.wait_ge(ev_dve, N_PROJ // 2)
                    pooling()

            def maxima(n):
                b, nk = n % 2, CHUNKS[n][2]
                dve.wait_ge(sc_mm, n + 1)
                if n >= 2:
                    dve.wait_ge(pr_s, n - 1)
                s = ps[:, 2 * b:2 * b + 2, 0:384].rearrange("p a (c n) -> p a c n", c=2)[:, :, :, 0:nk]
                v = small[:, b, :, :]
                link(dve.tensor_reduce(v[:, 0, :], s, AX.X, ALU.max))
                link(dve.scalar_tensor_tensor(v[:, 0, :], v[:, 0, :], HD ** -0.5, sink[:, :], ALU.mult, ALU.max))
                link(dve.tensor_scalar(v[:, 1, :], v[:, 0, :], -1.0, None, ALU.mult))
                dve.tensor_tensor(v[:, 2, :], sink[:, :], v[:, 1, :], ALU.add).then_inc(mx_s, 1)

            def normalise(n):
                b, nk = n % 2, CHUNKS[n][2]
                v = small[:, b, :, :]
                dve.wait_ge(ex_s, n + 1)
                link(dve.tensor_tensor(v[:, 5, :], v[:, 3, :], v[:, 4, :], ALU.add))
                link(dve.reciprocal(v[:, 6, :], v[:, 5, :]))
                dve.tensor_tensor(probs[b][:, :, 0:nk], probs[b][:, :, 0:nk],
                                  v[:, 6, :].unsqueeze(2).to_broadcast([P, NJ, nk]), ALU.mult).then_inc(pr_s, 1)

            def copy_ptb(n):
                dve.wait_ge(pt_mm, n + 1)
                if n >= 2:
                    dve.wait_ge(pv_mm, n - 1)
                if CHUNKS[n][2] % 128:
                    dve.tensor_copy(ptb[n % 2], bank(5)[0:64, :].rearrange("p (j n) -> p j n", j=NJ)).then_inc(ptb_s, 1)
                else:
                    dve.sem_inc(ptb_s, 1)

            def copy_o(n):
                dve.wait_ge(pv_mm, n + 1)
                qc = CHUNKS[n][0]
                dve.tensor_copy(hT[:, NG:NG + NJ, qc:qc + CHUNK],
                                bank(6 + n % 2)[:, 0:NJ * CHUNK].rearrange("p (j n) -> p j n", j=NJ)).then_inc(o_s, 1)

            dve.wait_ge(misc_in, 16 * 6)
            for m in range(NCH + 2):
                if m < NCH:
                    maxima(m)
                if 1 <= m <= NCH:
                    normalise(m - 1)
                    copy_ptb(m - 1)
                if m >= 2:
                    copy_o(m - 2)
            diags(0, range(4))

            dve.wait_ge(row_s, 16)
            for t in range(NT):
                r, c = slice(0, ROWS[t]), t // (SEQ // P)
                dve.wait_ge(ssm_s, t + 1)
                mean_eps(ss1[r, t:t + 1]).then_inc(msm_s, 1)
                dve.wait_ge(sqm_s, t + 1)
                link(dve.reciprocal(r1[r, t:t + 1], r1[r, t:t + 1]))
                dve.scalar_tensor_tensor(tmpf[r, :], pair(2 * (t % 2))[r, :], r1[r, t:t + 1], rowsb[r, 0, c, :],
                                         ALU.mult, ALU.mult).then_inc(res_s, 1)
                dve.wait_ge(ssx_s, t + 1)
                mean_eps(ss2[r, t:t + 1]).then_inc(msx_s, 1)
                dve.wait_ge(sqx_s, t + 1)
                link(dve.reciprocal(r2[r, t:t + 1], r2[r, t:t + 1]))
                dve.scalar_tensor_tensor(junkf[r, :], x[r, t, :], r2[r, t:t + 1], rowsb[r, 1, c, :],
                                         ALU.mult, ALU.mult).then_inc(h2a_s, 1)

            dve.wait_ge(h2_s, NT)
            dve.wait_ge(log_mm, NT)
            dve.memset(score[:, 8, :], 0.0).then_inc(misc_ev, 2)
            dve.wait_ge(score_s, 1)
            bias9 = rbias[:, :].unsqueeze(1).to_broadcast([P, NT, NE])
            link(dve.tensor_tensor(sel, score, bias9, ALU.add))
            for t in range(NT):
                for g in range(EG):
                    ins = dve.max(g8[:, t, g, :], sel[:, t, EG * g:EG * g + 8])
            link(ins)
            link(dve.tensor_tensor(gs[:, :, :], g8[:, :, :, 0], g8[:, :, :, 1], ALU.add))
            half = NT * EG * EG
            above = rtmp.bitcast(BF16)[:, 0:half].rearrange("p (t i j) -> p t i j", t=NT, i=EG)
            equal = rtmp.bitcast(BF16)[:, half:2 * half].rearrange("p (t i j) -> p t i j", t=NT, i=EG)
            of_j = gs[:, :, :].unsqueeze(2).to_broadcast([P, NT, EG, EG])
            of_i = gs[:, :, :].unsqueeze(3).to_broadcast([P, NT, EG, EG])
            dve.tensor_tensor(above, of_j, of_i, ALU.is_gt)
            link(dve.tensor_tensor(equal, of_j, of_i, ALU.is_equal))
            link(dve.tensor_tensor(equal, equal, lower8[:, :, :].unsqueeze(1).to_broadcast([P, NT, EG, EG]), ALU.mult))
            link(dve.tensor_tensor(above, above, equal, ALU.add))
            link(dve.tensor_reduce(gm[:, :, :], above, AX.X, ALU.add))
            link(dve.tensor_scalar(gm[:, :, :], gm[:, :, :], TOPG - 0.5, -1.0, ALU.is_lt, ALU.add))
            link(dve.tensor_scalar(gm[:, :, :], gm[:, :, :], 3.0e38, None, ALU.mult))
            link(dve.tensor_tensor(sel.rearrange("p t (g e) -> p t g e", g=EG), sel.rearrange("p t (g e) -> p t g e", g=EG),
                                   gm[:, :, :].unsqueeze(3).to_broadcast([P, NT, EG, 8]), ALU.add))
            for t in range(NT):
                ins = dve.max(top8[:, t, :], sel[:, t, :])
            link(ins)
            for t in range(NT):
                ins = dve.max_index(ix8[:, t, :], top8[:, t, :], sel[:, t, :])
            link(ins)
            link(dve.tensor_copy(ixf[:, :, :], ix8[:, :, :]))
            hit = rtmp.bitcast(BF16).rearrange("p (t e k) -> p t e k", t=NT, e=NE)
            link(dve.tensor_tensor(hit, iotae[:, :].unsqueeze(1).unsqueeze(3).to_broadcast([P, NT, NE, TOPK]),
                                   ixf[:, :, 0:TOPK].unsqueeze(2).to_broadcast([P, NT, NE, TOPK]), ALU.is_equal))
            link(dve.tensor_reduce(mask, hit, AX.X, ALU.add))
            link(dve.memset(mask[DEC:P, NT - 1, :], 0.0))
            dve.tensor_copy(maskb, mask).then_inc(maskb_s, 1)
            wn = sel
            link(dve.tensor_tensor(wn, mask, score, ALU.mult))
            link(dve.tensor_reduce(den[:, :], wn, AX.X, ALU.add))
            link(dve.memset(den[DEC:P, NT - 1:NT], 1.0))
            link(dve.reciprocal(den[:, :], den[:, :]))
            link(dve.scalar_tensor_tensor(wn, wn, SCALE_R, den[:, :].unsqueeze(2).to_broadcast([P, NT, NE]),
                                          ALU.mult, ALU.mult))
            link(dve.tensor_copy(wp[:, :, :, 2], wn))
            link(dve.tensor_tensor(wn, wn, wp[:, :, :, 2], ALU.subtract))
            link(dve.tensor_copy(wp[:, :, :, 3], wn))
            link(dve.tensor_tensor(wp[:, :, :, 4], wn, wp[:, :, :, 3], ALU.subtract))
            dve.tensor_copy(wp[:, :, :, 0], base[:, 0:NT].unsqueeze(2).to_broadcast([P, NT, NE]))
            link(dve.tensor_scalar(wp[:, :, :, 1], mask, 0.0, prow[:, 0:1], ALU.mult, ALU.add))
            dve.wait_ge(rank_mm, 1)
            dve.memset(ntl[:, :], 1.0)
            link(dve.tensor_copy(cnt[:, :], bank(7)[:, NE:2 * NE]))
            for j in range(1, NT):
                link(dve.scalar_tensor_tensor(ntl[:, :], cnt[:, :], float(P * j), ntl[:, :], ALU.is_gt, ALU.add))
            link(dve.tensor_tensor_scan(tend[:, :], ones[:, 0:NE], ntl[:, :], 0.0, ALU.mult, ALU.add))
            link(dve.tensor_tensor(tst[:, :], tend[:, :], ntl[:, :], ALU.subtract))
            link(dve.tensor_scalar(tst[:, :], tst[:, :], float(P), 1.0, ALU.mult, ALU.add))
            start9 = tst[:, :].unsqueeze(1).to_broadcast([P, NT, NE])
            dve.tensor_tensor(sel[:, 0:8, :], bank(6).rearrange("p (t e) -> p t e", e=NE), start9[:, 0:8, :], ALU.add)
            link(dve.tensor_tensor(sel[:, 8:9, :], bank(7)[:, 0:NE].unsqueeze(1), start9[:, 8:9, :], ALU.add))
            link(dve.tensor_tensor(pos.rearrange("p e t -> p t e"), sel, mask, ALU.mult))
            dve.tensor_scalar(lasti[:, :], tend[0:1, :], -1.0, None, ALU.add)
            link(dve.tensor_scalar(cnt, tend[:, :], float(P), None, ALU.mult))
            ef = score[0:1, 0:4, :].rearrange("p t e -> p (t e)")[:, 0:TAB]
            step = NT * NE * TOPK // NE
            for a in range(0, TAB, step):
                m = min(step, TAB - a)
                past = rtmp[0:1, :].bitcast(BF16)[:, 0:m * NE].rearrange("p (i e) -> p i e", e=NE)
                link(dve.tensor_tensor(past, cnt[0:1, :].unsqueeze(1).to_broadcast([1, m, NE]),
                                       base[0:1, a:a + m].unsqueeze(2).to_broadcast([1, m, NE]), ALU.is_le))
                link(dve.tensor_reduce(ef[:, a:a + m], past, AX.X, ALU.add))
            dve.tensor_scalar(etab[:, :], ef, float(NE - 1), None, ALU.min).then_inc(tables, 1)
            dve.wait_ge(tables, 1)
            dve.wait_ge(shd_mm, NT)

            def one_hot(i):
                e = dve.value_load(etab[0:1, bass.ds(i, 1)], min_val=0, max_val=NE - 1)
                dve.scalar_tensor_tensor(oh, pos[:, bass.ds(e, 1), :].rearrange("p a t -> p t a").to_broadcast([P, NT, P]),
                                         base[:, bass.ds(i, 1)], iota1[:, :].unsqueeze(1).to_broadcast([P, NT, P]),
                                         ALU.subtract, ALU.is_equal).then_inc(oh_s, 1)

            def slots(i):
                s = bank(6)
                dve.wait_ge(slot_mm, i + 1)
                dve.tensor_reduce(sl[:, 0:1], s[:, 0:2], AX.X, ALU.add)
                dve.tensor_reduce(wtab[:, bass.ds(i, 1)], s[:, 2:5], AX.X, ALU.add).then_inc(dstep, 1)
                dve.wait_ge(dstep, 2 * i + 1)
                dve.tensor_scalar(sl[:, 1:2], sl[:, 0:1], 0.0, padcol[:, 0:1], ALU.is_equal, ALU.mult).then_inc(dstep, 1)
                dve.wait_ge(dstep, 2 * i + 2)
                dve.scalar_tensor_tensor(itab[:, bass.ds(i, 1)], sl[:, 0:1], -1.0, sl[:, 1:2], ALU.add, ALU.add)
                dve.scalar_tensor_tensor(idxg[:, 0:1], sl[:, 0:1], -1.0, sl[:, 1:2], ALU.add, ALU.add).then_inc(idx_s, 1)

            def act_of(i):
                dve.wait_ge(silu_s, i + 1)
                dve.tensor_tensor(act_m, sg, bank(4)[:, DE:2 * DE], ALU.mult).then_inc(act_s, 1)

            def at_copy(i):
                dve.wait_ge(at_mm, i + 1)
                dve.tensor_copy(actT_m, bank(5)[:, 0:DE].rearrange("p (k n) -> p k n", k=KF)).then_inc(at_s, 1)

            def y_of(i):
                dve.wait_ge(dn_mm, i + 1)
                dve.tensor_copy(idxs[:, 0:1], itab[:, bass.ds(i, 1)])
                dve.tensor_scalar(yw, pair(2), wtab[:, bass.ds(i, 1)], None, ALU.mult).then_inc(yw_s, 1)

            dve.sem_inc(yw_s, 1)
            one_hot(0)
            slots(0)
            one_hot(1)
            dve.wait_ge(gathered, 16)
            slots(1)
            one_hot(2)
            act_of(0)
            dve.wait_ge(gathered, 32)
            slots(2)
            last = dve.value_load(lasti[0:1, NE - 1:NE], min_val=NE - 1, max_val=MAX_TILES - 1)
            with dve.Fori(1, MAX_TILES) as i:
                with dve.If(i <= last):
                    at_copy(i - 1)
                    one_hot(i + 2)
                    act_of(i)
                    dve.wait_ge(gathered, 16 * (i + 2))
                    slots(i + 2)
                    dve.wait_ge(added, 16 * i)
                    y_of(i - 1)
            at_copy(last)
            dve.wait_ge(added, 16 * (last + 1))
            y_of(last)

            dve.wait_ge(fin_ss, 1)
            mean_eps(ss3[:, :]).then_inc(fin_ms, 1)
            dve.wait_ge(fin_sq, 1)
            link(dve.reciprocal(r3[:, :], r3[:, :]))
            for t in range(NT):
                r, c = slice(0, ROWS[t]), t // (SEQ // P)
                link(dve.scalar_tensor_tensor(y_t(t)[r, :], y_t(t)[r, :], r3[r, t:t + 1], rowsb[r, 3, c, :],
                                              ALU.mult, ALU.mult))
                dve.tensor_tensor(x[r, t, :], x[r, t, :], y_t(t)[r, :], ALU.add).then_inc(fin_s, 1)

        @block.tensor
        def _(pe):
            pe.wait_ge(const_pool, 1)
            pe.wait_ge(small_in, 16 * 5)
            pe.transpose(bank(7)[:, 0:100], stg[:, :], ident[0:100, 0:100]).then_inc(stg_t, 1)

            def transposes(t):
                r = slice(0, ROWS[t])
                pe.wait_ge(xn_s, t + 1)
                if t >= 2:
                    pe.wait_ge(ht_s, t - 1)
                for k in range(KD):
                    ins = pe.transpose(pair(2 * (t % 2))[:, P * k:P * k + ROWS[t]], xn[t % 2][r, P * k:P * (k + 1)],
                                       ident[r, r])
                ins.then_inc(ht_mm, 1)

            pe.wait_ge(sil_s, 1)
            for v in range(6):
                pe.wait_ge(ada_in[v % 3], 16 * (v // 3 + 1))
                for j in range(KD):
                    for k in range(KD):
                        c0 = 2 * (KD * v + j)
                        ins = pe.matmul(bank(6)[:, c0:c0 + 2], ada[v % 3][:, k, P * j:P * (j + 1)], sil[:, k, :],
                                        start=(k == 0), stop=(k == KD - 1))
                ins.then_inc(ada_mm, 1)
            for t in range(NT):
                transposes(t)

            pe.wait_ge(misc_in, 16 * 6)
            for g in range(NG):
                pe.transpose(bank(4)[:, HIST * g:HIST * (g + 1)], stin[:, P * g:P * (g + 1)], ident[0:HIST, 0:HIST])
            pe.transpose(bank(5)[:, 0:WIN], ckin[:, :], ident[:, :]).then_inc(misc_mm, 1)

            def rows(n0, kinds):
                n = n0
                for _ in kinds:
                    for _ in range(4):
                        pe.wait_ge(diag_s, n + 1)
                        if n >= 2:
                            pe.wait_ge(row_s, n - 1)
                        pe.matmul(bank(6 + n % 2), ones[:, :], diag[:, n % 2, :, :].rearrange("p a b -> p (a b)"),
                                  start=True, stop=True).then_inc(row_mm, 1)
                        n += 1

            pe.wait_ge(w_in_s, 16)
            pe.wait_ge(ht_s, NT)
            for n, (kind, c, a, n_) in enumerate(groups):
                if n >= 4:
                    pe.wait_ge(ev_dve if n % 2 else ev_act, (n - 4) // 2 + 1)
                out = bank(n % 4)
                if kind == "ct":
                    for k in range(KD):
                        ins = pe.matmul(out[:, 0:n_], w1[:, k, P * c:P * (c + 1)], hT[:, k, a:a + n_], start=(k == 0), stop=(k == KD - 1))
                elif kind == "v":
                    for t in range(4 * c, min(4 * c + 4, NT)):
                        o = out[0:ROWS[t], P * (t % 4):P * (t % 4) + KV]
                        for k in range(KD):
                            ins = pe.matmul(o, hT[:, k, P * t:P * t + ROWS[t]], w1[:, k, INW - KV:INW],
                                            start=(k == 0), stop=(k == KD - 1))
                else:
                    pe.wait_ge(pooled, c + 1)
                    pe.wait_ge(wpool_s, 16)
                    o = HIST + a if a < SEQ else US + HIST
                    ins = pe.matmul(out[:, 0:n_], wpool[:, c, :], u[:, c, o:o + n_], start=True, stop=True)
                ins.then_inc(proj_mm, 1)
                if n == N_PROJ - 1:
                    pe.wait_ge(ev_act, 14)
                    pe.wait_ge(ev_dve, 13)
                    pe.wait_ge(misc_ev, 1)
                    for g in range(NG):
                        pe.transpose(bank(4)[0:HIST, P * g:P * (g + 1)], u[:, g, US - HIST:US], ident[:, :])
                        pe.transpose(bank(5)[0:HIST, P * g:P * (g + 1)], u[:, g, UL - HIST:UL], ident[:, :])
                    pe.transpose(bank(6)[:, 0:KV], kT[:, SEQ - WIN:SEQ], ident[:, :])
                    pe.transpose(bank(6)[0:DEC, KV:2 * KV], kT[:, SEQ + WIN:KL], ident[:, :]).then_inc(outs_mm, 1)

            def scores(n):
                b, (qc, kc, nk, _, _) = n % 2, CHUNKS[n]
                pe.wait_ge(qbd_s, 2 * (n + 1))
                if n >= 2:
                    pe.wait_ge(ex_s, n - 1)
                for j in range(NJ):
                    ins = pe.matmul(ps[:, 2 * b + j // 2, 192 * (j % 2):192 * (j % 2) + nk], qbd[b][:, j, :],
                                    kT[:, kc:kc + nk], start=True, stop=True)
                ins.then_inc(sc_mm, 1)

            def prob_t(n):
                b, nk = n % 2, CHUNKS[n][2]
                pe.wait_ge(pr_s, n + 1)
                if n >= 1:
                    pe.wait_ge(pta_s, n)
                    pe.wait_ge(ptb_s, n)
                for j in range(NJ):
                    if nk >= 128:
                        ins = pe.transpose(bank(4)[:, P * j:P * (j + 1)], probs[b][:, j, 0:128], ident[:, :])
                    if nk % 128:
                        ins = pe.transpose(bank(5)[0:64, P * j:P * (j + 1)], probs[b][:, j, nk - 64:nk], ident[:, :])
                ins.then_inc(pt_mm, 1)

            def pv(n):
                b, (_, _, nk, where, tile) = n % 2, CHUNKS[n]
                v = vodd if where == "odd" else vt
                pe.wait_ge(pta_s, n + 1)
                pe.wait_ge(ptb_s, n + 1)
                if n >= 2:
                    pe.wait_ge(o_s, n - 1)
                for h in range(2):
                    r = slice(64 * h, 64 * h + 64)
                    out = bank(6 + b)[r, 0:NJ * CHUNK]
                    if nk >= 128:
                        ins = pe.matmul(out, v[:, tile, r], pta[b][:, :, r], start=True, stop=(nk == 128))
                    if nk % 128:
                        ins = pe.matmul(out, v[0:64, tile + 1, r], ptb[b][:, :, r], start=(nk == 64), stop=True)
                ins.then_inc(pv_mm, 1)

            pe.wait_ge(ev_act, len(groups) // 2)
            pe.wait_ge(ev_dve, len(groups) // 2)
            pe.wait_ge(outs_ev, 1)
            pe.wait_ge(vodd_s, 48)
            for m in range(NCH + 2):
                if m < NCH:
                    scores(m)
                if 1 <= m <= NCH:
                    prob_t(m - 1)
                if m >= 2:
                    pv(m - 2)

            pe.wait_ge(o_s, NCH)
            rows(0, range(4))

            pe.wait_ge(w_out_s, 48)
            pe.wait_ge(row_s, 16)

            def mix(t):
                if t >= 2:
                    pe.wait_ge(res_s, t - 1)
                for half in range(2):
                    for k in range(KD):
                        ins = pe.matmul(bank(2 * (t % 2) + half)[0:ROWS[t], :], hT[:, k, P * t:P * t + ROWS[t]],
                                        wo[:, k, 512 * half:512 * half + 512], start=(k == 0), stop=(k == KD - 1))
                ins.then_inc(mix_mm, 1)

            def h2_t(t):
                r = slice(0, ROWS[t])
                pe.wait_ge(h2_s, t + 1)
                if t >= 1:
                    pe.wait_ge(h2t_s, t)
                for k in range(KD):
                    ins = pe.transpose(pair(4)[:, P * k:P * k + ROWS[t]], h2p[t % 2][r, P * k:P * (k + 1)], ident[r, r])
                ins.then_inc(h2t_mm, 1)

            def logits(t):
                pe.wait_ge(h2t_s, t + 1)
                out = bank(6 + t // 8)[0:ROWS[t], NE * (t % 8):NE * (t % 8 + 1)]
                for k in range(KD):
                    ins = pe.matmul(out, hT[:, k, P * t:P * t + ROWS[t]], wrt[:, k, :], start=(k == 0), stop=(k == KD - 1))
                ins.then_inc(log_mm, 1)

            for t in range(NT + 1):
                if t < NT:
                    mix(t)
                if t >= 1:
                    h2_t(t - 1)
                if t >= 2:
                    logits(t - 2)
            logits(NT - 1)

            def swiglu_in(xt, w, cols):
                gu = gate_up(w)
                for k in range(KD):
                    ins = pe.matmul(bank(4)[0:cols, :], xt[:, k, :], gu[:, :, k, :], start=(k == 0), stop=(k == KD - 1))
                return ins

            def swiglu_out(b, at_, w, cols):
                d = down(w)
                for half in range(2):
                    for k in range(KF):
                        ins = pe.matmul(bank(b + half)[0:cols, :], at_[:, k, 0:cols], d[:, k, 512 * half:512 * half + 512],
                                        start=(k == 0), stop=(k == KF - 1))
                return ins

            pe.wait_ge(wsh_s, 48)

            def sh_out(t):
                r = slice(0, ROWS[t])
                pe.wait_ge(sht_s, t + 1)
                if t >= 1:
                    pe.wait_ge(shy_s, t)
                swiglu_out(0, actTs, wsh, ROWS[t]).then_inc(shd_mm, 1)

            def sh_t(t):
                r = slice(0, ROWS[t])
                pe.wait_ge(sha_s, t + 1)
                if t >= 1:
                    pe.wait_ge(shd_mm, t)
                for k in range(KF):
                    ins = pe.transpose(bank(5)[:, P * k:P * k + ROWS[t]], acts[r, P * k:P * (k + 1)], ident[r, r])
                ins.then_inc(sht_mm, 1)

            for t in range(NT):
                if t >= 1:
                    sh_t(t - 1)
                swiglu_in(hT[:, :, P * t:P * t + ROWS[t]], wsh, ROWS[t]).then_inc(shg_mm, 1)
                if t >= 1:
                    sh_out(t - 1)
                if t == 6:
                    pe.wait_ge(maskb_s, 1)
                    for tt in range(NT + 1):
                        out = bank(6)[:, NE * tt:NE * (tt + 1)] if tt < 8 else bank(7)[:, NE * (tt - 8):NE * (tt - 7)]
                        for s in range(min(tt + 1, NT)):
                            ins = pe.matmul(out, (triub if s == tt else onesb)[:, :], maskb[:, s, :],
                                            start=(s == 0), stop=(s == min(tt, NT - 1)))
                    ins.then_inc(rank_mm, 1)
            sh_t(NT - 1)
            sh_out(NT - 1)

            def slots(i):
                e = pe.value_load(etab[0:1, bass.ds(i, 1)], min_val=0, max_val=NE - 1)
                pe.wait_ge(oh_s, i + 1)
                for t in range(NT):
                    ins = pe.matmul(bank(6)[:, 0:5], oh[:, t, :], wp[:, t, bass.ds(e, 1), :].rearrange("p a c -> p (a c)"),
                                    start=(t == 0), stop=(t == NT - 1))
                ins.then_inc(slot_mm, 1)

            def x_t(i):
                pe.wait_ge(gathered, 16 * (i + 1))
                for k in range(KD):
                    ins = pe.transpose(pair(0)[:, P * k:P * (k + 1)], xg[:, P * k:P * (k + 1)], ident[:, :])
                ins.then_inc(xt_mm, 1)

            def ring_slot(i):
                e = pe.value_load(etab[0:1, bass.ds(i, 1)], min_val=0, max_val=NE - 1)
                return e, (e & (RING - 1)) * WSLOT

            def expert_in(i):
                e, o = ring_slot(i)
                pe.wait_ge(w_ready, e + 1)
                pe.wait_ge(xt_s, i + 1)
                swiglu_in(xT, big[:, bass.ds(o, WSLOT)], P).then_inc(gu_mm, 1)

            def act_t(i):
                pe.wait_ge(act_s, i + 1)
                for k in range(KF):
                    ins = pe.transpose(bank(5)[:, P * k:P * (k + 1)], act_m[:, P * k:P * (k + 1)], ident[:, :])
                ins.then_inc(at_mm, 1)

            def expert_out(i):
                e, o = ring_slot(i)
                pe.wait_ge(at_s, i + 1)
                swiglu_out(2, actT_m, big[:, bass.ds(o, WSLOT)], P).then_inc(dn_mm, 1)

            pe.wait_ge(tables, 1)
            pe.wait_ge(shy_s, NT)
            slots(0)
            pe.wait_ge(idx_s, 1)
            slots(1)
            x_t(0)
            expert_in(0)
            pe.wait_ge(xt_s, 1)
            x_t(1)
            pe.wait_ge(idx_s, 2)
            slots(2)
            last = pe.value_load(lasti[0:1, NE - 1:NE], min_val=NE - 1, max_val=MAX_TILES - 1)
            with pe.Fori(1, MAX_TILES) as i:
                with pe.If(i <= last):
                    act_t(i - 1)
                    expert_in(i)
                    x_t(i + 1)
                    pe.wait_ge(idx_s, i + 2)
                    slots(i + 2)
                    pe.wait_ge(yw_s, i)
                    expert_out(i - 1)
            act_t(last)
            pe.wait_ge(yw_s, last + 1)
            expert_out(last)


_INS = ["x_prompt", "x_sample", "c_prompt", "c_sample", "state_pool", "cache_k", "cache_v", "w_ada", "b_ada",
        "norm_gains", "w_in", "w_pool", "pool_scale", "attn_sinks", "w_out", "w_router", "router_bias",
        "w_gate", "w_up", "w_down", "ws_gate", "ws_up", "ws_down"]
_OUTS = [(1, SEQ, D), (1, DEC, D), (1, 1, HIST, PW), (1, 1, WIN, 2, HD), (1, 1, WIN, 2, HD),
         (1, 1, HIST, PW), (1, 1, WIN, 2, HD), (1, 1, WIN, 2, HD)]


def kernel(**inputs):
    import numpy as _np
    import concourse.bacc as _bacc
    from concourse import mybir as _mybir
    from concourse.bass_utils import run_bass_kernel_spmd as _run

    nc = _bacc.Bacc("TRN2", target_bir_lowering=False, num_devices=1)
    arrays, args = {}, []
    for name in _INS:
        a = _np.asarray(inputs[name])
        if name == "w_in":
            qcols = a[..., PW:PW + 512].reshape(1, D, 2, NJ, HD).transpose(0, 1, 3, 2, 4).reshape(1, D, 512)
            a = _np.concatenate([a[..., :PW], qcols, a[..., PW + 512:]], axis=-1)
        a = _np.ascontiguousarray(a)
        arrays[f"in_{name}_dram"] = a
        args.append(nc.dram_tensor(f"in_{name}_dram", a.shape, _mybir.dt.from_np(a.dtype), kind="ExternalInput").ap())
    for i, shape in enumerate(_OUTS):
        args.append(nc.dram_tensor(f"out_{i}_dram", shape, F32, kind="ExternalOutput").ap())
    build(nc, *args)
    r = _run(nc, [arrays], core_ids=[0])
    return tuple(r.results[0][f"out_{i}_dram"] for i in range(len(_OUTS)))
```

```python
from contextlib import ExitStack

import concourse.bass as bass
from concourse import mybir

F32 = mybir.dt.float32
BF16 = mybir.dt.bfloat16
I32 = mybir.dt.int32
U32 = mybir.dt.uint32
ALU = mybir.AluOpType
ACT = mybir.ActivationFunctionType
AX = mybir.AxisListType

P = 128
D = 1024
KD = D // P
SEQ, DEC = 1024, 64
N = SEQ + DEC
NT = -(-N // P)
ROWS = [min(P, N - P * t) for t in range(NT)]
CHUNK = 64
PW = 512
WINDOWS = (2, 4, 8, 16)
NG = len(WINDOWS)
HIST = max(WINDOWS) - 1
HD = 64
NJ = 4
KV = 128
WIN = 128
INW = PW + 512 + 2 * KV
NE, TOPK, EG, TOPG = 64, 6, 8, 4
DE = 256
KF = DE // P
SCALE_R = 2.5
EPS = 1e-6
MAX_TILES = -(-(N * TOPK + NE * P) // P)
GROUPS, GROUP = 7, 8
assert NE + GROUPS * GROUP >= MAX_TILES
TAB = NE + GROUPS * GROUP + 2
RING = 4
PIECES = 4
WSLOT = KD * 2 * DE + KF * D

UL = HIST + SEQ + HIST + DEC
US = HIST + SEQ
KL = SEQ + WIN + DEC
BLOCKS = [(0, 512), (512, 512), (1024, DEC)]

CHUNKS = [(0, 0, 64, "v", -1), (64, 0, 128, "v", 0)]
for _c in range(2, SEQ // CHUNK):
    CHUNKS.append((64 * _c, 64 * (_c - 2), 192, "odd" if _c % 2 else "v", (_c - 2) // 2))
CHUNKS.append((SEQ, SEQ, 192, "v", SEQ // P))


def build(nc, x_prompt, x_sample, c_prompt, c_sample, state_pool, cache_k, cache_v, w_ada, b_ada,
          norm_gains, w_in, w_pool, pool_scale, attn_sinks, w_out, w_router, router_bias,
          w_gate, w_up, w_down, ws_gate, ws_up, ws_down,
          y_prompt, y_sample, pool_p, k_p, v_p, pool_s, k_s, v_s):
    with ExitStack() as ctx:
        def sb(name, shape, dt=F32):
            return ctx.enter_context(nc.sbuf_tensor(name, shape, dt))

        def sem(name):
            return ctx.enter_context(nc.semaphore(name))

        h2_rows = nc.dram_tensor("h2_rows", (N, D), F32, kind="Internal").ap()
        y_acc = nc.dram_tensor("y_acc", (N + P, D), F32, kind="Internal").ap()

        x = sb("x", [P, NT, D])
        rowsb = sb("rowsb", [P, 4, 2, D])
        tr = sb("tr", [P, KD * N])
        big = sb("big", [P, RING * WSLOT])
        colv = sb("colv", [P, 100])
        sil = sb("sil", [P, KD, 2])
        mods = sb("mods", [P, 2 * KD, 2])
        a1 = sb("a1", [P, KD, 2])
        ident = sb("ident", [P, P])
        ones = sb("ones", [P, P])
        onesb = sb("onesb", [P, P], BF16)
        triub = sb("triub", [P, P], BF16)
        iota1 = sb("iota1", [P, P])
        base = sb("base", [P, TAB])
        padcol = sb("padcol", [P, 1])
        prow = sb("prow", [P, 1])
        iotae = sb("iotae", [P, NE])
        lower8 = sb("lower8", [P, EG, EG])
        rec = sb("rec", [P, 16])
        ss = sb("ss", [P, NT])
        rstd = sb("rstd", [P, NT])
        ss1 = sb("ss1", [P, NT])
        r1 = sb("r1", [P, NT])
        ss2 = sb("ss2", [P, NT])
        r2 = sb("r2", [P, NT])
        ss3 = sb("ss3", [P, NT])
        r3 = sb("r3", [P, NT])
        sink = sb("sink", [P, NJ])
        wrt = sb("wrt", [P, KD, NE])
        rbias = sb("rbias", [P, NE])
        wtab = sb("wtab", [P, TAB])
        itab = sb("itab", [P, TAB])
        idxg = sb("idxg", [P, 1], I32)
        idxs = sb("idxs", [P, 1], I32)
        sl = sb("sl", [P, 4])
        etab = sb("etab", [1, TAB], I32)
        lasti = sb("lasti", [1, NE], I32)

        hT = tr[:, :].rearrange("p (k n) -> p k n", k=KD)
        def tr_at(at, n):
            return tr[:, at:at + n]
        xg = tr_at(0, D)
        xT = tr_at(D, D).rearrange("p (k n) -> p k n", k=KD)
        yw = tr_at(2 * D, D)
        oh = tr_at(3 * D, NT * P // 2).bitcast(BF16).rearrange("p (t s) -> p t s", t=NT)
        sg = tr_at(4 * D, DE)
        act_m = tr_at(4 * D + DE, DE)
        actT_m = tr_at(4 * D + 2 * DE, DE).rearrange("p (k n) -> p k n", k=KF)

        def at(a, n):
            return big[:, a:a + n]
        ada = [a_.rearrange("p (k n) -> p k n", k=KD) for a_ in
               (at(0, KD * 512), at(WSLOT + KD * INW, KD * 512), at(WSLOT + KD * INW + KD * 512, KD * 512),
                tr_at(0, KD * 512))]
        q = at(0, NJ * N).rearrange("p (j n) -> p j n", j=NJ)
        kT = at(NJ * N, KL)
        w1 = at(WSLOT, KD * INW).rearrange("p (k n) -> p k n", k=KD)
        wo = at(WSLOT, KD * D).rearrange("p (k n) -> p k n", k=KD)
        vat = WSLOT + KD * INW
        vt = at(vat, 10 * KV).rearrange("p (t n) -> p t n", n=KV)
        sF = WSLOT + KD * D
        tmpf = at(sF, D)
        junkf = at(sF + D, D)
        h2p = [at(sF + 2 * D, D), at(sF + 3 * D, D)]
        assert sF + 4 * D <= 3 * WSLOT and vat + 10 * KV <= 3 * WSLOT and NJ * N + KL <= WSLOT
        u = at(3 * WSLOT, NG * UL).rearrange("p (g n) -> p g n", g=NG)
        vodd = at(3 * WSLOT + NG * UL, 8 * KV).rearrange("p (t n) -> p t n", n=KV)
        assert NG * UL + 8 * KV <= WSLOT
        wpool = at(vat + 10 * KV, NG * P).rearrange("p (g n) -> p g n", g=NG)
        assert vat + 10 * KV + NG * P <= 3 * WSLOT
        at_g = [2 * WSLOT]
        def g_buf(n):
            at_g[0] += n
            assert at_g[0] <= sF + 2 * D
            return at(at_g[0] - n, n)
        shy = [g_buf(D), g_buf(D)]
        sgs, ups, acts = g_buf(DE), g_buf(DE), g_buf(DE)
        actTs = g_buf(KF * P).rearrange("p (k n) -> p k n", k=KF)
        def wslot(s):
            return at(WSLOT * s, WSLOT)
        wsh = wslot(3)

        def gate_up(w):
            return w[:, 0:KD * 2 * DE].rearrange("p (m k n) -> p m k n", m=2, k=KD)

        def down(w):
            return w[:, KD * 2 * DE:WSLOT].rearrange("p (k n) -> p k n", k=KF)

        def y_t(t):
            return at(D * t, D)

        xb = [rowsb[:, 1 + b // 2, b % 2, :] for b in range(6)]
        rowsb_flat = rowsb[:, :, :, :].rearrange("p a c n -> p (a c n)")
        mrow = rowsb_flat[0:2, 0:2 * D]

        scr = x[:, :, :].rearrange("p t n -> p (t n)")
        at_s = [0]
        def s_buf(n):
            at_s[0] += n
            assert at_s[0] <= NT * D
            return scr[:, at_s[0] - n:at_s[0]]
        piece = [s_buf(D) for _ in range(PIECES)]
        acc = [s_buf(D), s_buf(D)]
        brow, grow = s_buf(D), s_buf(D)
        stin, ckin, stg = s_buf(PW)[0:HIST, :], s_buf(KV), s_buf(P)[0:100, :]
        at_s[0] = 0
        qbd = [s_buf(4 * P).rearrange("p (j n) -> p j n", j=NJ) for _ in range(2)]
        probs = [s_buf(768).rearrange("p (j n) -> p j n", j=NJ) for _ in range(3)]
        pta = [s_buf(4 * P).rearrange("p (j n) -> p j n", j=NJ) for _ in range(2)]
        ptb = [s_buf(4 * P)[0:64, :].rearrange("p (j n) -> p j n", j=NJ) for _ in range(2)]
        small = s_buf(3 * 7 * NJ).rearrange("p (b v j) -> p b v j", b=3, v=7)
        sums = [s_buf(UL), s_buf(UL)]
        fix = s_buf(16)
        outst_p = s_buf(2 * PW)[0:HIST, :].rearrange("p (a n) -> p a n", a=2)
        outst_k = s_buf(2 * KV).rearrange("p (a n) -> p a n", a=2)

        hb = rowsb[:, 0:3, :, :].rearrange("p a b n -> p (a b n)")
        at_h = [0]
        def h_buf(n):
            at_h[0] += n
            assert at_h[0] <= 3 * 2 * D
            return hb[:, at_h[0] - n:at_h[0]]
        wp = h_buf(NT * NE * 5 // 2).bitcast(BF16).rearrange("p (t e c) -> p t e c", t=NT, e=NE)
        pos = h_buf(NT * NE).rearrange("p (e t) -> p e t", t=NT)
        score = h_buf(NT * NE).rearrange("p (t e) -> p t e", t=NT)
        rtmp = h_buf(NT * NE * TOPK // 2)
        sel = h_buf(NT * NE).rearrange("p (t e) -> p t e", t=NT)
        mask = h_buf(NT * NE).rearrange("p (t e) -> p t e", t=NT)
        g8 = h_buf(NT * EG * 8).rearrange("p (t g n) -> p t g n", t=NT, g=EG)
        def small_g(n, k=NT):
            return g_buf(n * k).rearrange("p (t n) -> p t n", t=k)
        maskb = g_buf(NT * NE // 2).bitcast(BF16).rearrange("p (t e) -> p t e", t=NT)
        gs, gm, top8, ixf = small_g(EG), small_g(EG), small_g(8), small_g(8)
        ix8 = g_buf(NT * 8).bitcast(U32).rearrange("p (t n) -> p t n", t=NT)
        cnt, ntl, tst = g_buf(NE), g_buf(NE), g_buf(NE)
        den = sb("den", [P, NT])
        tend = sb("tend", [P, NE])

        ps = ctx.enter_context(nc.psum_tensor("ps", [P, 8, 512], F32))

        def bank(b):
            return ps[:, b, :]

        def pair(b):
            return ps[:, b:b + 2, :].rearrange("p b n -> p (b n)")

        const_pool = sem("const_pool")
        small_in = sem("small_in")
        misc_in = sem("misc_in")
        ada_in = [sem(f"ada_in{s}") for s in range(4)]
        piece_in = [sem(f"piece_in{b}") for b in range(PIECES)]
        bg_in = sem("bg_in")
        acc_s = sem("acc_s")
        mrow_s = sem("mrow_s")
        mcol_mm = sem("mcol_mm")
        xr_in = [sem(f"xr_in{t}") for t in range(NT)]
        x_in = [sem(f"x_in{t}") for t in range(NT)]
        w_in_s = [sem(f"w_in_s{b}") for b in range(3)]
        w_out_s = sem("w_out_s")
        stg_t = sem("stg_t")
        colv_s = sem("colv_s")
        sil_s = sem("sil_s")
        ada_mm = sem("ada_mm")
        mods_s = sem("mods_s")
        row_mm = sem("row_mm")
        row_s = sem("row_s")
        dchain = sem("dchain")
        achain = sem("achain")
        pchain = sem("pchain")
        ss_s = sem("ss_s")
        ms_s = sem("ms_s")
        sq_s = sem("sq_s")
        rstd_s = sem("rstd_s")
        xn_s = sem("xn_s")
        ht_mm = sem("ht_mm")
        ht_s = sem("ht_s")
        misc_mm = sem("misc_mm")
        misc_ev = sem("misc_ev")
        uz_s = sem("uz_s")
        proj_mm = sem("proj_mm")
        ev_s = sem("ev_s")
        outs_mm = sem("outs_mm")
        outs_ev = sem("outs_ev")
        stored = sem("stored")
        outs_st = sem("outs_st")
        pool_st = sem("pool_st")
        wpool_s = sem("wpool_s")
        dstep = sem("dstep")
        pool_turn = sem("pool_turn")
        pooled = sem("pooled")
        vodd_s = sem("vodd_s")
        qbd_s = sem("qbd_s")
        sc_mm = sem("sc_mm")
        mx_s = sem("mx_s")
        ex_s = sem("ex_s")
        pr_s = sem("pr_s")
        pt_mm = sem("pt_mm")
        pta_s = sem("pta_s")
        ptb_s = sem("ptb_s")
        pv_mm = sem("pv_mm")
        o_s = sem("o_s")
        mix_mm = sem("mix_mm")
        ssm_s = sem("ssm_s")
        msm_s = sem("msm_s")
        sqm_s = sem("sqm_s")
        res_s = sem("res_s")
        x1_s = sem("x1_s")
        ssx_s = sem("ssx_s")
        msx_s = sem("msx_s")
        sqx_s = sem("sqx_s")
        h2a_s = sem("h2a_s")
        h2_s = sem("h2_s")
        h2_st = [sem(f"h2_st{b}") for b in range(2)]
        h2t_mm = sem("h2t_mm")
        h2t_s = sem("h2t_s")
        log_mm = sem("log_mm")
        score_s = sem("score_s")
        wsh_s = sem("wsh_s")
        shg_mm = sem("shg_mm")
        shs_s = sem("shs_s")
        sha_s = sem("sha_s")
        sht_mm = sem("sht_mm")
        sht_s = sem("sht_s")
        shd_mm = sem("shd_mm")
        shy_s = sem("shy_s")
        shy_st = [sem(f"shy_st{b}") for b in range(2)]
        maskb_s = sem("maskb_s")
        rank_mm = sem("rank_mm")
        tables = sem("tables")
        w_slot_s = [sem(f"w_slot{s}") for s in range(RING)]
        w_ready = sem("w_ready")
        oh_s = sem("oh_s")
        slot_mm = sem("slot_mm")
        idx_s = sem("idx_s")
        gathered = sem("gathered")
        xt_mm = sem("xt_mm")
        xt_s = sem("xt_s")
        gu_mm = sem("gu_mm")
        silu_s = sem("silu_s")
        act_s = sem("act_s")
        at_mm = sem("at_mm")
        at_s = sem("at_s")
        dn_mm = sem("dn_mm")
        yw_s = sem("yw_s")
        added = sem("added")
        y_in = [sem(f"y_in{t}") for t in range(NT)]
        fin_ss = sem("fin_ss")
        fin_ms = sem("fin_ms")
        fin_sq = sem("fin_sq")
        fin_g = sem("fin_g")
        fin_s = [sem("fin_even"), sem("fin_odd")]

        def chained(eng, s):
            n = [0]

            def link(ins):
                n[0] += 1
                ins.then_inc(s, 1)
                eng.wait_ge(s, n[0])
            return link

        def rows_of(prompt, sample, t):
            return prompt[0, P * t:P * (t + 1), :] if t < SEQ // P else sample[0, :, :]

        ada_view = w_ada[0].rearrange("(k p) n -> p k n", p=P)
        gate_v = w_gate[0].rearrange("e (p k) n -> e p (k n)", k=KD)
        up_v = w_up[0].rearrange("e (p k) n -> e p (k n)", k=KD)
        down_v = w_down[0].rearrange("e (k p) n -> e p k n", p=P)

        groups = []
        for ct in range(NG):
            for a, n_ in BLOCKS:
                groups.append(("ct", ct, a, n_))
        N_U = len(groups)
        for g in range(3):
            groups.append(("v", g, 0, 0))
        N_V = len(groups)
        for ct in range(NG, 9):
            for a, n_ in BLOCKS:
                groups.append(("ct", ct, a, n_))
        N_PROJ = len(groups)
        for g in range(NG):
            for a, n_ in BLOCKS:
                groups.append(("pool", g, a, n_))
        VECS = [(2, 0, 1), (3, 2, None), (4, 1, 2), (5, 3, 3)]
        LAST_U = N_V + 10
        ROWS_AT = [6, N_U, N_V + 3, N_V + 9]

        def evac_group(eng, n, kind, c, a, n_):
            src = bank(n % 4)
            def copy(out, in_):
                return eng.activation(out, in_, ACT.Copy)
            if kind == "v":
                if c < 2:
                    return copy(vt[:, 4 * c:4 * c + 4, :], src.rearrange("p (t n) -> p t n", t=4))
                return copy(vt[0:DEC, 9, :], src[0:DEC, 0:KV])
            if kind == "pool":
                out, sc = hT[:, c, a:a + n_], colv[:, 96 + c:97 + c]
                return eng.activation(out, src[:, 0:n_], ACT.Copy, scale=sc)
            if c < NG:
                to = HIST + a if a < SEQ else US + HIST
                return copy(u[:, c, to:to + n_], src[:, 0:n_])
            if c < 8:
                return copy(q[:, c - 4, a:a + n_], src[:, 0:n_])
            to = a if a < SEQ else SEQ + WIN
            return copy(kT[:, to:to + n_], src[:, 0:n_])

        NCH = len(CHUNKS)

        def tiles(eng, tile, last):
            with eng.Fori(1, NE) as i:
                tile(i)
            with eng.Fori(0, GROUPS) as g:
                with eng.If(g * GROUP + NE <= last):
                    with eng.Fori(0, GROUP) as j:
                        with eng.If(g * GROUP + NE + j <= last):
                            tile(g * GROUP + NE + j)

        block = ctx.enter_context(nc.Block())

        @block.sync
        def _(sp):
            sp.dma_start(stg[0:48, :], b_ada[0].rearrange("(r n) -> r n", n=P)).then_inc(small_in, 16)
            sp.dma_start(stg[48:80, :], norm_gains[0].rearrange("g (r n) -> (g r) n", n=P)).then_inc(small_in, 16)
            sp.dma_start(stg[80:88, :], c_prompt[0].rearrange("(r n) -> r n", n=P)).then_inc(small_in, 16)
            sp.dma_start(stg[88:96, :], c_sample[0].rearrange("(r n) -> r n", n=P)).then_inc(small_in, 16)
            sp.dma_start(stg[96:100, :], pool_scale[0].rearrange("(r n) -> r n", n=P)).then_inc(small_in, 16)
            for b in range(4):
                sp.dma_start(ada[b], ada_view[:, :, 512 * b:512 * (b + 1)]).then_inc(ada_in[b], 16)
            for t in range(6):
                sp.dma_start(xb[t][0:ROWS[t], :], rows_of(x_prompt, x_sample, t)).then_inc(x_in[t], 16)
            w_in_v = w_in[0].rearrange("(k p) n -> p k n", p=P)
            sp.dma_start(w1[:, :, 0:PW], w_in_v[:, :, 0:PW]).then_inc(w_in_s[0], 16)
            sp.dma_start(w1[:, :, INW - KV:INW], w_in_v[:, :, INW - KV:INW]).then_inc(w_in_s[1], 16)
            sp.dma_start(w1[:, :, PW:INW - KV], w_in_v[:, :, PW:INW - KV]).then_inc(w_in_s[2], 16)
            for t in range(6, NT):
                sp.wait_ge(ht_mm, t - 5)
                sp.dma_start(xb[t - 6][0:ROWS[t], :], rows_of(x_prompt, x_sample, t)).then_inc(x_in[t], 16)
            sp.dma_start(wpool, w_pool[0].rearrange("g c d -> c g d")).then_inc(wpool_s, 16)
            sp.dma_start(vt[:, 8, :], cache_v[0, 0].rearrange("s h d -> s (h d)")).then_inc(vodd_s, 16)
            for i, (v, kind, gain_row) in enumerate(VECS):
                if i >= 1:
                    sp.wait_ge(row_s, 2 * i)
                sp.dma_start(brow, b_ada[0:1, D * v:D * (v + 1)].to_broadcast([P, D])).then_inc(bg_in, 16)
                if gain_row is not None:
                    sp.dma_start(grow, norm_gains[0, gain_row:gain_row + 1, :].to_broadcast([P, D])).then_inc(bg_in, 16)
                for k in range(KD):
                    m = KD * i + k
                    if m >= PIECES:
                        sp.wait_ge(acc_s, 2 * (m - PIECES + 1))
                    sp.dma_start(piece[m % PIECES], ada_view[:, k, D * v:D * (v + 1)]).then_inc(piece_in[m % PIECES], 16)
            sp.wait_ge(ev_s, N_V)
            sp.dma_start(vodd[0:64, 0:8, :], vt[64:128, 0:8, :]).then_inc(vodd_s, 16)
            sp.dma_start(vodd[64:128, 0:7, :], vt[0:64, 1:8, :]).then_inc(vodd_s, 16)
            sp.dma_start(v_p[0, 0].rearrange("s h d -> s (h d)"), vt[:, 7, :]).then_inc(stored, 16)
            sp.dma_start(v_s[0, 0, DEC:WIN].rearrange("s h d -> s (h d)"), vt[0:DEC, 9, :]).then_inc(stored, 16)
            sp.wait_ge(proj_mm, N_PROJ)
            sp.dma_start(wo[:, 0:NG, :], w_out[0, 0:PW].rearrange("(k p) n -> p k n", p=P)).then_inc(w_out_s, 16)
            for h in range(2):
                src = w_out[0, PW + 256 * h:PW + 256 * (h + 1)].rearrange("(j d) n -> d j n", d=HD)
                sp.dma_start(wo[64 * h:64 * h + 64, NG:NG + NJ, :], src).then_inc(w_out_s, 16)
            def load_expert(g, s):
                w = gate_up(wslot(s))
                def of(v):
                    return v.rearrange("(g s) p n -> s g p n", s=RING)[s, bass.ds(g, 1)].rearrange("a p n -> (a p) n")
                sp.dma_start(w[:, 0].rearrange("p k n -> p (k n)"), of(gate_v)).then_inc(w_slot_s[s], 16)
                sp.dma_start(w[:, 1].rearrange("p k n -> p (k n)"), of(up_v)).then_inc(w_slot_s[s], 16)
                d = down_v.rearrange("(g s) p k n -> s g p k n", s=RING)[s, bass.ds(g, 1)]
                sp.dma_start(down(wslot(s)), d.rearrange("a p k n -> (a p) k n"))\
                  .then_inc(w_slot_s[s], 16)

            sp.wait_ge(pv_mm, NCH)
            sp.wait_ge(outs_st, 64)
            for t in range(NT):
                sp.dma_start(x[0:ROWS[t], t, :], rows_of(x_prompt, x_sample, t)).then_inc(xr_in[t], 16)
            gu = gate_up(wsh)
            sp.dma_start(gu[:, 0].rearrange("p k n -> p (k n)"), ws_gate[0].rearrange("(p k) n -> p (k n)", k=KD)).then_inc(wsh_s, 16)
            sp.dma_start(gu[:, 1].rearrange("p k n -> p (k n)"), ws_up[0].rearrange("(p k) n -> p (k n)", k=KD)).then_inc(wsh_s, 16)
            sp.dma_start(down(wsh), ws_down[0].rearrange("(k p) n -> p k n", p=P)).then_inc(wsh_s, 16)
            load_expert(0, 0)
            for t in range(NT):
                sp.wait_ge(h2_s, t + 1)
                sp.dma_start(h2_rows[P * t:P * t + ROWS[t], :], h2p[t % 2][0:ROWS[t], :]).then_inc(h2_st[t % 2], 16)
            sp.wait_ge(mix_mm, NT)
            sp.wait_ge(h2t_mm, NT)
            sp.wait_ge(h2_st[0], 16 * ((NT + 1) // 2))
            sp.wait_ge(h2_st[1], 16 * (NT // 2))
            sp.wait_ge(h2_s, NT)
            load_expert(0, 1)
            for t in range(NT):
                sp.wait_ge(shy_s, t + 1)
                sp.dma_start(y_acc[P * t:P * t + ROWS[t], :], shy[t % 2][0:ROWS[t], :]).then_inc(shy_st[t % 2], 16)
            load_expert(0, 3)
            for b in range(2):
                sp.wait_ge(shy_st[b], 16 * ((NT + 1 - b) // 2))
            sp.wait_ge(tables, 1)
            load_expert(0, 2)
            sp.wait_ge(w_slot_s[0], 48)
            sp.sem_inc(w_ready, 1)
            sp.wait_ge(w_slot_s[1], 48)
            sp.sem_inc(w_ready, 1)
            sp.wait_ge(w_slot_s[2], 48)
            sp.sem_inc(w_ready, 1)
            with sp.Fori(1, NE // RING) as g:
                for s in range(RING):
                    last_of = sp.value_load(lasti[0:1, :].rearrange("a (g s) -> a s g", s=RING)[:, s, bass.ds(g - 1, 1)], min_val=0, max_val=MAX_TILES - 1)
                    sp.wait_ge(dn_mm, last_of + 1)
                    load_expert(g, s)
                    if s == 0:
                        sp.wait_ge(w_slot_s[RING - 1], g * 48)
                    else:
                        sp.wait_ge(w_slot_s[s - 1], g * 48 + 48)
                    sp.sem_inc(w_ready, 1)
            sp.wait_ge(w_slot_s[RING - 1], 48 * NE // RING)
            sp.sem_inc(w_ready, 1)

            last = sp.value_load(lasti[0:1, NE - 1:NE], min_val=NE - 1, max_val=MAX_TILES - 1)
            sp.wait_ge(added, 16 * (last + 2))
            for t in range(NT):
                sp.dma_start(y_t(t)[0:ROWS[t], :], y_acc[P * t:P * t + ROWS[t], :]).then_inc(y_in[t], 16)
            for t in range(NT):
                sp.wait_ge(fin_s[t % 2], t // 2 + 1)
                sp.dma_start(rows_of(y_prompt, y_sample, t), x[0:ROWS[t], t, :]).then_inc(stored, 16)
            sp.wait_ge(stored, 16 * (2 + NT))
            sp.wait_ge(pool_st, 32)

        @block.gpsimd
        def _(pool):
            link = chained(pool, pchain)
            pool.dma_start(sink[0:64, :], attn_sinks[0:1, 0:NJ].to_broadcast([64, NJ])).then_inc(misc_in, 16)
            pool.dma_start(sink[64:128, :], attn_sinks[0:1, NJ:2 * NJ].to_broadcast([64, NJ])).then_inc(misc_in, 16)
            pool.dma_start(rbias[:, :], router_bias[0:1, :].to_broadcast([P, NE])).then_inc(misc_in, 16)
            pool.dma_start(wrt[:, :, :].rearrange("p k n -> p (k n)"), w_router[0].rearrange("(p k) n -> p (k n)", k=KD)).then_inc(misc_in, 16)
            pool.dma_start(stin[:, :], state_pool[0, 0]).then_inc(misc_in, 16)
            pool.dma_start(ckin[:, :], cache_k[0, 0].rearrange("s h d -> s (h d)")).then_inc(misc_in, 16)
            pool.dma_start(k_s[0, 0, 0:DEC], cache_k[0, 0, DEC:WIN]).then_inc(pool_st, 16)
            pool.dma_start(v_s[0, 0, 0:DEC], cache_v[0, 0, DEC:WIN]).then_inc(pool_st, 16)
            pool.dma_start(y_acc[N:N + P, :], x_prompt[0, 0:P, :]).then_inc(added, 16)
            link(pool.memset(ident[:, :], 0.0))
            pool.affine_select(out=ident[:, :], in_=ident[:, :], compare_op=ALU.not_equal, fill=1.0, base=0,
                               pattern=[[-1, P]], channel_multiplier=1).then_inc(const_pool, 1)
            pool.memset(ones[:, :], 1.0)
            pool.memset(onesb[:, :], 1.0)
            link(pool.memset(triub[:, :], 1.0))
            pool.affine_select(out=triub[:, :], in_=triub[:, :], compare_op=ALU.is_gt, fill=0.0, base=0,
                               pattern=[[1, P]], channel_multiplier=-1)
            low = dict(allow_small_or_imprecise_dtypes=True)
            pool.iota(iota1[:, :], [[1, P]], base=1, channel_multiplier=0, **low)
            pool.iota(base[:, :], [[P, TAB]], base=0, channel_multiplier=0, **low)
            pool.iota(padcol[:, :], [[0, 1]], base=N + 1, channel_multiplier=1, **low)
            pool.iota(prow[:, :], [[0, 1]], base=1, channel_multiplier=1, **low)
            pool.iota(iotae[:, :], [[1, NE]], base=0, channel_multiplier=0, **low)
            pool.iota(rec[:, :], [[1, 16]], base=1, channel_multiplier=0, **low)
            link(pool.memset(lower8[:, :, :], 1.0))
            pool.affine_select(out=lower8[:, :, :], in_=lower8[:, :, :], compare_op=ALU.is_gt, fill=0.0, base=0,
                               pattern=[[1, EG], [-1, EG]], channel_multiplier=0)
            pool.memset(wtab[:, :], 0.0).then_inc(const_pool, 1)
            pool.wait_ge(const_pool, 2)
            pool.wait_ge(ada_mm, 4)
            pool.memset(u[:, :, 0:HIST], 0.0).then_inc(uz_s, 1)

            pool.wait_ge(row_mm, 4)
            for b in range(2):
                ins = pool.memset(qbd[b], 0.0)
            ins.then_inc(uz_s, 1)
            pool.wait_ge(uz_s, 2)
            pool.wait_ge(ev_s, N_PROJ - 3)
            for n, (qc, _, _, _, _) in enumerate(CHUNKS):
                if n >= 2:
                    pool.wait_ge(sc_mm, n - 1)
                for h in range(2):
                    r = slice(64 * h, 64 * h + 64)
                    pool.tensor_copy(qbd[n % 2][r, :, r], q[r, :, qc:qc + CHUNK]).then_inc(qbd_s, 1)
                    pool.wait_ge(qbd_s, 2 * n + h + 1)

            for t in range(NT):
                r, c = slice(0, ROWS[t]), t // (SEQ // P)
                pool.wait_ge(xr_in[t], 16)
                pool.wait_ge(res_s, t + 1)
                pool.tensor_tensor(x[r, t, :], x[r, t, :], tmpf[r, :], ALU.add).then_inc(x1_s, 1)
                pool.wait_ge(h2a_s, t + 1)
                if t >= 2:
                    pool.wait_ge(h2_st[t % 2], 16 * (t // 2))
                    pool.wait_ge(h2t_mm, t - 1)
                pool.tensor_tensor(h2p[t % 2][r, :].rearrange("p (k q) -> p q k", k=KD),
                                   junkf[r, :].rearrange("p (q k) -> p q k", k=KD),
                                   rowsb[r, 2, c, :].rearrange("p (q k) -> p q k", k=KD), ALU.add).then_inc(h2_s, 1)

            for t in range(NT):
                pool.wait_ge(shs_s, 2 * (t + 1))
                if t >= 1:
                    pool.wait_ge(sht_mm, t)
                pool.tensor_tensor(acts[0:ROWS[t], :], sgs[0:ROWS[t], :], ups[0:ROWS[t], :], ALU.mult)\
                    .then_inc(sha_s, 1)

            for b in range(2):
                pool.wait_ge(shy_st[b], 16 * ((NT + 1 - b) // 2))
            pool.wait_ge(added, 16)

            gather_bound, add_bound = pool.to_reg(N - 1), pool.to_reg(N + P - 1)

            def gather(i):
                pool.wait_ge(idx_s, i + 1)
                pool.sem_inc(pool_turn, 1)
                pool.indirect_dma_start(out=xg, out_offset=None, in_=h2_rows,
                                        in_offset=bass.IndirectOffsetOnAxis(ap=idxg[:, 0:1], axis=0),
                                        bounds_check=gather_bound, oob_is_err=False).then_inc(gathered, 16)

            def scatter_add(i):
                pool.wait_ge(yw_s, i + 2)
                pool.sem_inc(pool_turn, 1)
                pool.indirect_dma_start(out=y_acc, out_offset=bass.IndirectOffsetOnAxis(ap=idxs[:, 0:1], axis=0),
                                        in_=yw, in_offset=None, bounds_check=add_bound,
                                        compute_op=ALU.add).then_inc(added, 16)

            pool.wait_ge(shd_mm, NT)
            pool.memset(xg, 0.0).then_inc(uz_s, 1)
            pool.wait_ge(uz_s, 3)
            gather(0)
            pool.wait_ge(xt_mm, 1)
            gather(1)
            pool.wait_ge(tables, 1)
            last = pool.value_load(lasti[0:1, NE - 1:NE], min_val=NE - 1, max_val=MAX_TILES - 1)
            pool.wait_ge(xt_mm, 2)
            gather(2)

            def tile(i):
                pool.wait_ge(xt_mm, i + 2)
                gather(i + 2)
                scatter_add(i - 1)
            tiles(pool, tile, last)
            scatter_add(last)

            for t in range(0, NT, 2):
                r = slice(0, ROWS[t])
                pool.wait_ge(fin_g, t + 1)
                pool.tensor_tensor(x[r, t, :], x[r, t, :], y_t(t)[r, :], ALU.add).then_inc(fin_s[0], 1)

        @block.scalar
        def _(act):
            link = chained(act, achain)
            act.wait_ge(colv_s, 1)
            act.activation(sil[:, :, :].rearrange("p k c -> p c k"), colv[:, 80:96].rearrange("p (c k) -> p c k", c=2),
                           ACT.Silu).then_inc(sil_s, 1)
            act.wait_ge(ms_s, 1)
            for g in range(3):
                three = range(3 * g, 3 * g + 3)
                for t in three:
                    r = slice(0, ROWS[t])
                    act.wait_ge(x_in[t], 16)
                    ins = act.activation(pair(4)[r, :], xb[t % 6][r, :], ACT.Square, accum_out=ss[r, t:t + 1])
                    if t < 3 * g + 2:
                        link(ins)
                    else:
                        ins.then_inc(ss_s, 1)
                act.wait_ge(ms_s, g + 2)
                act.activation(rstd[:, 3 * g:3 * g + 3], ss[:, 3 * g:3 * g + 3], ACT.Sqrt).then_inc(sq_s, 1)
                act.wait_ge(rstd_s, g + 1)
                for t in three:
                    r = slice(0, ROWS[t])
                    act.activation(xb[t % 6][r, :], xb[t % 6][r, :], ACT.Copy, scale=rstd[r, t:t + 1]).then_inc(xn_s, 1)
                if g == 0:
                    for b in range(4):
                        act.wait_ge(ada_mm, b + 1)
                        act.activation(mrow[:, 512 * b:512 * (b + 1)], bank(b)[0:2, :], ACT.Copy).then_inc(mrow_s, 1)

            for n, (kind, c, a, n_) in enumerate(groups):
                act.wait_ge(proj_mm, n + 1)
                evac_group(act, n, kind, c, a, n_).then_inc(ev_s, 1)
                if n == N_PROJ - 1:
                    act.wait_ge(outs_mm, 2)
                    act.wait_ge(row_s, 8)
                    act.activation(outst_p[:, 0, :], bank(4)[0:HIST, :], ACT.Copy)
                    act.activation(outst_p[:, 1, :], bank(5)[0:HIST, :], ACT.Copy)
                    act.activation(outst_k[:, 0, :], bank(6)[:, 0:KV], ACT.Copy)
                    act.activation(outst_k[0:DEC, 1, :], bank(6)[0:DEC, KV:2 * KV], ACT.Copy).then_inc(outs_ev, 1)
                    act.wait_ge(outs_ev, 1)
                    act.dma_start(pool_p[0, 0], outst_p[:, 0, :]).then_inc(outs_st, 16)
                    act.dma_start(pool_s[0, 0], outst_p[:, 1, :]).then_inc(outs_st, 16)
                    act.dma_start(k_p[0, 0].rearrange("s h d -> s (h d)"), outst_k[:, 0, :]).then_inc(outs_st, 16)
                    act.dma_start(k_s[0, 0, DEC:WIN].rearrange("s h d -> s (h d)"), outst_k[0:DEC, 1, :]).then_inc(outs_st, 16)

            def exps(n):
                b, nk = n % 3, CHUNKS[n][2]
                act.wait_ge(mx_s, n + 1)
                if n >= 3:
                    act.wait_ge(pt_mm, n - 2)
                act.activation(small[:, b, 3, :], small[:, b, 2, :], ACT.Exp)
                for j in range(NJ):
                    src = ps[:, 2 * (n % 2) + j // 2, 192 * (j % 2):192 * (j % 2) + nk]
                    ins = act.activation(probs[b][:, j, 0:nk], src, ACT.Exp, bias=small[:, b, 1, j:j + 1],
                                         scale=HD ** -0.5, accum_out=small[:, b, 4, j:j + 1])
                ins.then_inc(ex_s, 1)

            def copy_pta(n):
                act.wait_ge(pt_mm, n + 1)
                if n >= 2:
                    act.wait_ge(pv_mm, n - 1)
                nk = CHUNKS[n][2]
                if nk >= 128:
                    act.activation(pta[n % 2], bank(4).rearrange("p (j n) -> p j n", j=NJ), ACT.Copy).then_inc(pta_s, 1)
                else:
                    act.sem_inc(pta_s, 1)

            for m in range(NCH + 2):
                if m < NCH:
                    exps(m)
                if m >= 2:
                    copy_pta(m - 2)

            def h2t_copy(t):
                act.wait_ge(h2t_mm, t + 1)
                act.activation(hT[:, :, P * t:P * t + ROWS[t]],
                               pair(4).rearrange("p (k n) -> p k n", k=KD)[:, :, 0:ROWS[t]], ACT.Copy).then_inc(h2t_s, 1)

            for t in range(NT):
                r = slice(0, ROWS[t])
                act.wait_ge(mix_mm, t + 1)
                if t >= 1:
                    act.wait_ge(h2_s, t)
                act.activation(junkf[r, :], pair(2 * (t % 2))[r, :], ACT.Square, accum_out=ss1[r, t:t + 1]).then_inc(ssm_s, 1)
                if t >= 1:
                    h2t_copy(t - 1)
                act.wait_ge(msm_s, t + 1)
                act.activation(r1[r, t:t + 1], ss1[r, t:t + 1], ACT.Sqrt).then_inc(sqm_s, 1)
                act.wait_ge(x1_s, t + 1)
                act.activation(junkf[r, :], x[r, t, :], ACT.Square, accum_out=ss2[r, t:t + 1]).then_inc(ssx_s, 1)
                act.wait_ge(msx_s, t + 1)
                act.activation(r2[r, t:t + 1], ss2[r, t:t + 1], ACT.Sqrt).then_inc(sqx_s, 1)
            h2t_copy(NT - 1)
            act.wait_ge(log_mm, NT)
            act.wait_ge(misc_ev, 3)
            act.activation(score[:, 0:8, :], bank(6).rearrange("p (t e) -> p t e", e=NE), ACT.Sigmoid)
            act.activation(score[0:DEC, 8, :], bank(7)[0:DEC, 0:NE], ACT.Sigmoid).then_inc(score_s, 1)

            def sh_silu(t):
                r = slice(0, ROWS[t])
                act.wait_ge(shg_mm, t + 1)
                if t >= 1:
                    act.wait_ge(sha_s, t)
                act.activation(sgs[r, :], bank(4)[r, 0:DE], ACT.Silu).then_inc(shs_s, 1)
                act.activation(ups[r, :], bank(4)[r, DE:2 * DE], ACT.Copy).then_inc(shs_s, 1)

            def sh_tail(t):
                r = slice(0, ROWS[t])
                act.wait_ge(sht_mm, t + 1)
                act.activation(actTs[:, :, r], bank(5)[:, 0:DE].rearrange("p (k n) -> p k n", k=KF)[:, :, r], ACT.Copy)\
                    .then_inc(sht_s, 1)
                act.wait_ge(shd_mm, t + 1)
                if t >= 2:
                    act.wait_ge(shy_st[t % 2], 16 * (t // 2))
                act.activation(shy[t % 2][r, :], pair(0)[r, :], ACT.Copy).then_inc(shy_s, 1)

            for t in range(NT):
                sh_silu(t)
                if t >= 1:
                    sh_tail(t - 1)
            sh_tail(NT - 1)

            def xt_copy(i):
                act.wait_ge(xt_mm, i + 1)
                act.activation(xT, pair(0).rearrange("p (k n) -> p k n", k=KD), ACT.Copy).then_inc(xt_s, 1)

            def silu_of(i):
                act.wait_ge(gu_mm, i + 1)
                act.activation(sg, bank(4)[:, 0:DE], ACT.Silu).then_inc(silu_s, 1)

            xt_copy(0)
            silu_of(0)
            xt_copy(1)
            act.wait_ge(tables, 1)
            last = act.value_load(lasti[0:1, NE - 1:NE], min_val=NE - 1, max_val=MAX_TILES - 1)

            def tile(i):
                act.wait_ge(gu_mm, i + 1)
                act.wait_ge(act_s, i)
                act.activation(sg, bank(4)[:, 0:DE], ACT.Silu).then_inc(silu_s, 1)
                xt_copy(i + 1)
            tiles(act, tile, last)

            for g in range(3):
                for t in range(3 * g, 3 * g + 3):
                    r = slice(0, ROWS[t])
                    act.wait_ge(y_in[t], 16)
                    ins = act.activation(pair(4)[r, :], y_t(t)[r, :], ACT.Square, accum_out=ss3[r, t:t + 1])
                    if t < 3 * g + 2:
                        link(ins)
                    else:
                        ins.then_inc(fin_ss, 1)
                act.wait_ge(fin_ms, g + 1)
                act.activation(r3[:, 3 * g:3 * g + 3], ss3[:, 3 * g:3 * g + 3], ACT.Sqrt).then_inc(fin_sq, 1)

        @block.vector
        def _(dve):
            link = chained(dve, dchain)
            dve.memset(ss1[:, :], 1.0)
            dve.memset(ss3[:, :], 1.0)
            dve.memset(ss2[:, :], 1.0)
            dve.memset(ss[:, :], 1.0).then_inc(ms_s, 1)
            dve.wait_ge(stg_t, 1)
            dve.tensor_copy(colv[:, :], bank(7)[:, 0:100]).then_inc(colv_s, 1)
            dve.wait_ge(const_pool, 2)
            link(dve.reciprocal(rec[:, :], rec[:, :]))
            def mean_eps(s):
                return dve.tensor_scalar(s, s, 1.0 / D, EPS, ALU.mult, ALU.add)

            def rms_of_three(g):
                dve.wait_ge(ss_s, g + 1)
                mean_eps(ss[:, 3 * g:3 * g + 3]).then_inc(ms_s, 1)
                dve.wait_ge(sq_s, g + 1)
                dve.reciprocal(rstd[:, 3 * g:3 * g + 3], rstd[:, 3 * g:3 * g + 3]).then_inc(rstd_s, 1)
            rms_of_three(0)
            dve.wait_ge(mcol_mm, 1)
            dve.wait_ge(colv_s, 1)
            link(dve.tensor_tensor(mods[:, :, :], bank(6)[:, 0:4 * KD].rearrange("p (r c) -> p r c", c=2),
                                   colv[:, 0:2 * KD].unsqueeze(2).to_broadcast([P, 2 * KD, 2]), ALU.add))
            dve.scalar_tensor_tensor(a1[:, :, :], mods[:, KD:2 * KD, :], 1.0,
                                     colv[:, 48:48 + KD].unsqueeze(2).to_broadcast([P, KD, 2]), ALU.add, ALU.mult)\
                .then_inc(mods_s, 1)
            dve.wait_ge(mods_s, 1)
            rms_of_three(1)
            for t in range(NT):
                c = t // (SEQ // P)
                if t == 3:
                    rms_of_three(2)
                dve.wait_ge(ht_mm, t + 1)
                src = pair(2 * (t % 2))
                for k in range(KD):
                    ins = dve.tensor_scalar(hT[:, k, P * t:P * t + ROWS[t]], src[:, P * k:P * k + ROWS[t]],
                                            a1[:, k, c:c + 1], mods[:, k, c:c + 1], ALU.mult, ALU.add)
                ins.then_inc(ht_s, 1)
            dve.wait_ge(misc_mm, 1)
            dve.tensor_copy(u[:, :, US:US + HIST], bank(4)[:, 0:NG * HIST].rearrange("p (g n) -> p g n", g=NG))
            dve.tensor_copy(kT[:, SEQ:SEQ + WIN], bank(5)[:, 0:WIN]).then_inc(misc_ev, 1)

            def pooling():
                dve.wait_ge(ev_s, N_U)
                dve.wait_ge(outs_mm, 1)
                dve.wait_ge(uz_s, 1)
                for g, w in enumerate(WINDOWS):
                    cur, s = u[:, g, :], 1
                    for b in range(g + 1):
                        nxt, lo = sums[b % 2], 2 * s - 1
                        link(dve.tensor_tensor(nxt[:, lo:UL], cur[:, lo:UL], cur[:, lo - s:UL - s], ALU.add))
                        cur, s = nxt, 2 * s
                    first = slice(HIST, HIST + w - 1)
                    link(dve.tensor_tensor(fix[:, 0:w - 1], cur[:, first], rec[:, 0:w - 1], ALU.mult))
                    link(dve.tensor_tensor(fix[:, 0:w - 1], fix[:, 0:w - 1], u[:, g, first], ALU.subtract))
                    link(dve.scalar_tensor_tensor(u[:, g, HIST:UL], cur[:, HIST:UL], 1.0 / w, u[:, g, HIST:UL],
                                                  ALU.mult, ALU.subtract))
                    dve.tensor_copy(u[:, g, first], fix[:, 0:w - 1]).then_inc(pooled, 1)
                    dve.wait_ge(pooled, g + 1)

            for i, (_, kind, gain_row) in enumerate(VECS):
                for k in range(KD):
                    m = KD * i + k
                    dve.wait_ge(piece_in[m % PIECES], 16 * (m // PIECES + 1))
                    for c in range(2):
                        if k == 0:
                            dve.tensor_scalar(acc[c], piece[m % PIECES], sil[:, k, c:c + 1], None, ALU.mult).then_inc(acc_s, 1)
                        else:
                            dve.wait_ge(acc_s, 2 * m + c - 1)
                            dve.scalar_tensor_tensor(acc[c], piece[m % PIECES], sil[:, k, c:c + 1], acc[c],
                                                     ALU.mult, ALU.add).then_inc(acc_s, 1)
                dve.wait_ge(bg_in, 16 * sum(1 + (g is not None) for _, _, g in VECS[:i + 1]))
                dve.wait_ge(row_mm, i + 1)
                for c in range(2):
                    row = rowsb[:, kind, c, :]
                    link(dve.tensor_tensor(row, pair(6 if c == 0 else 4), brow, ALU.add))
                    if kind == 1:
                        dve.scalar_tensor_tensor(row, row, 1.0, grow, ALU.add, ALU.mult).then_inc(row_s, 1)
                    elif gain_row is not None:
                        dve.tensor_tensor(row, row, grow, ALU.mult).then_inc(row_s, 1)
                    else:
                        dve.sem_inc(row_s, 1)
            pooling()

            def maxima(n):
                b, nk = n % 3, CHUNKS[n][2]
                dve.wait_ge(sc_mm, n + 1)
                if n >= 3:
                    dve.wait_ge(pr_s, n - 2)
                s = ps[:, 2 * (n % 2):2 * (n % 2) + 2, 0:384].rearrange("p a (c n) -> p a c n", c=2)[:, :, :, 0:nk]
                v = small[:, b, :, :]
                link(dve.tensor_reduce(v[:, 0, :], s, AX.X, ALU.max))
                link(dve.scalar_tensor_tensor(v[:, 0, :], v[:, 0, :], HD ** -0.5, sink[:, :], ALU.mult, ALU.max))
                link(dve.tensor_scalar(v[:, 1, :], v[:, 0, :], -1.0, None, ALU.mult))
                dve.tensor_tensor(v[:, 2, :], sink[:, :], v[:, 1, :], ALU.add).then_inc(mx_s, 1)

            def normalise(n):
                b, nk = n % 3, CHUNKS[n][2]
                v = small[:, b, :, :]
                dve.wait_ge(ex_s, n + 1)
                link(dve.tensor_tensor(v[:, 5, :], v[:, 3, :], v[:, 4, :], ALU.add))
                link(dve.reciprocal(v[:, 6, :], v[:, 5, :]))
                dve.tensor_tensor(probs[b][:, :, 0:nk], probs[b][:, :, 0:nk],
                                  v[:, 6, :].unsqueeze(2).to_broadcast([P, NJ, nk]), ALU.mult).then_inc(pr_s, 1)

            def copy_ptb(n):
                dve.wait_ge(pt_mm, n + 1)
                if n >= 2:
                    dve.wait_ge(pv_mm, n - 1)
                if CHUNKS[n][2] % 128:
                    dve.tensor_copy(ptb[n % 2], bank(5)[0:64, :].rearrange("p (j n) -> p j n", j=NJ)).then_inc(ptb_s, 1)
                else:
                    dve.sem_inc(ptb_s, 1)

            def copy_o(n):
                dve.wait_ge(pv_mm, n + 1)
                qc = CHUNKS[n][0]
                dve.tensor_copy(hT[:, NG:NG + NJ, qc:qc + CHUNK],
                                bank(6 + n % 2)[:, 0:NJ * CHUNK].rearrange("p (j n) -> p j n", j=NJ)).then_inc(o_s, 1)

            dve.wait_ge(misc_in, 16 * 6)
            for m in range(NCH + 3):
                if m < NCH:
                    maxima(m)
                if 1 <= m <= NCH:
                    normalise(m - 1)
                if 2 <= m <= NCH + 1:
                    copy_ptb(m - 2)
                if m >= 3:
                    copy_o(m - 3)

            dve.wait_ge(row_s, 8)
            for t in range(NT):
                r, c = slice(0, ROWS[t]), t // (SEQ // P)
                dve.wait_ge(ssm_s, t + 1)
                mean_eps(ss1[r, t:t + 1]).then_inc(msm_s, 1)
                dve.wait_ge(sqm_s, t + 1)
                link(dve.reciprocal(r1[r, t:t + 1], r1[r, t:t + 1]))
                dve.scalar_tensor_tensor(tmpf[r, :], pair(2 * (t % 2))[r, :], r1[r, t:t + 1], rowsb[r, 0, c, :],
                                         ALU.mult, ALU.mult).then_inc(res_s, 1)
                dve.wait_ge(ssx_s, t + 1)
                mean_eps(ss2[r, t:t + 1]).then_inc(msx_s, 1)
                dve.wait_ge(sqx_s, t + 1)
                link(dve.reciprocal(r2[r, t:t + 1], r2[r, t:t + 1]))
                dve.scalar_tensor_tensor(junkf[r, :], x[r, t, :], r2[r, t:t + 1], rowsb[r, 1, c, :],
                                         ALU.mult, ALU.mult).then_inc(h2a_s, 1)

            dve.wait_ge(h2_s, NT)
            dve.wait_ge(log_mm, NT)
            dve.memset(score[:, 8, :], 0.0).then_inc(misc_ev, 2)
            dve.wait_ge(score_s, 1)
            bias9 = rbias[:, :].unsqueeze(1).to_broadcast([P, NT, NE])
            link(dve.tensor_tensor(sel, score, bias9, ALU.add))
            for t in range(NT):
                for g in range(EG):
                    ins = dve.max(g8[:, t, g, :], sel[:, t, EG * g:EG * g + 8])
            link(ins)
            link(dve.tensor_tensor(gs[:, :, :], g8[:, :, :, 0], g8[:, :, :, 1], ALU.add))
            half = NT * EG * EG
            above = rtmp.bitcast(BF16)[:, 0:half].rearrange("p (t i j) -> p t i j", t=NT, i=EG)
            equal = rtmp.bitcast(BF16)[:, half:2 * half].rearrange("p (t i j) -> p t i j", t=NT, i=EG)
            of_j = gs[:, :, :].unsqueeze(2).to_broadcast([P, NT, EG, EG])
            of_i = gs[:, :, :].unsqueeze(3).to_broadcast([P, NT, EG, EG])
            dve.tensor_tensor(above, of_j, of_i, ALU.is_gt)
            link(dve.tensor_tensor(equal, of_j, of_i, ALU.is_equal))
            link(dve.tensor_tensor(equal, equal, lower8[:, :, :].unsqueeze(1).to_broadcast([P, NT, EG, EG]), ALU.mult))
            link(dve.tensor_tensor(above, above, equal, ALU.add))
            link(dve.tensor_reduce(gm[:, :, :], above, AX.X, ALU.add))
            link(dve.tensor_scalar(gm[:, :, :], gm[:, :, :], TOPG - 0.5, -1.0, ALU.is_lt, ALU.add))
            link(dve.tensor_scalar(gm[:, :, :], gm[:, :, :], 3.0e38, None, ALU.mult))
            link(dve.tensor_tensor(sel.rearrange("p t (g e) -> p t g e", g=EG), sel.rearrange("p t (g e) -> p t g e", g=EG),
                                   gm[:, :, :].unsqueeze(3).to_broadcast([P, NT, EG, 8]), ALU.add))
            for t in range(NT):
                ins = dve.max(top8[:, t, :], sel[:, t, :])
            link(ins)
            for t in range(NT):
                ins = dve.max_index(ix8[:, t, :], top8[:, t, :], sel[:, t, :])
            link(ins)
            link(dve.tensor_copy(ixf[:, :, :], ix8[:, :, :]))
            hit = rtmp.bitcast(BF16).rearrange("p (t e k) -> p t e k", t=NT, e=NE)
            link(dve.tensor_tensor(hit, iotae[:, :].unsqueeze(1).unsqueeze(3).to_broadcast([P, NT, NE, TOPK]),
                                   ixf[:, :, 0:TOPK].unsqueeze(2).to_broadcast([P, NT, NE, TOPK]), ALU.is_equal))
            link(dve.tensor_reduce(mask, hit, AX.X, ALU.add))
            link(dve.memset(mask[DEC:P, NT - 1, :], 0.0))
            dve.tensor_copy(maskb, mask).then_inc(maskb_s, 1)
            wn = sel
            link(dve.tensor_tensor(wn, mask, score, ALU.mult))
            link(dve.tensor_reduce(den[:, :], wn, AX.X, ALU.add))
            link(dve.memset(den[DEC:P, NT - 1:NT], 1.0))
            link(dve.reciprocal(den[:, :], den[:, :]))
            link(dve.scalar_tensor_tensor(wn, wn, SCALE_R, den[:, :].unsqueeze(2).to_broadcast([P, NT, NE]),
                                          ALU.mult, ALU.mult))
            link(dve.tensor_copy(wp[:, :, :, 2], wn))
            link(dve.tensor_tensor(wn, wn, wp[:, :, :, 2], ALU.subtract))
            link(dve.tensor_copy(wp[:, :, :, 3], wn))
            link(dve.tensor_tensor(wp[:, :, :, 4], wn, wp[:, :, :, 3], ALU.subtract))
            dve.tensor_copy(wp[:, :, :, 0], base[:, 0:NT].unsqueeze(2).to_broadcast([P, NT, NE]))
            link(dve.tensor_scalar(wp[:, :, :, 1], mask, 0.0, prow[:, 0:1], ALU.mult, ALU.add))
            dve.wait_ge(rank_mm, 1)
            dve.memset(ntl[:, :], 1.0)
            link(dve.tensor_copy(cnt[:, :], bank(7)[:, NE:2 * NE]))
            for j in range(1, NT):
                link(dve.scalar_tensor_tensor(ntl[:, :], cnt[:, :], float(P * j), ntl[:, :], ALU.is_gt, ALU.add))
            link(dve.tensor_tensor_scan(tend[:, :], ones[:, 0:NE], ntl[:, :], 0.0, ALU.mult, ALU.add))
            link(dve.tensor_tensor(tst[:, :], tend[:, :], ntl[:, :], ALU.subtract))
            link(dve.tensor_scalar(tst[:, :], tst[:, :], float(P), 1.0, ALU.mult, ALU.add))
            start9 = tst[:, :].unsqueeze(1).to_broadcast([P, NT, NE])
            dve.tensor_tensor(sel[:, 0:8, :], bank(6).rearrange("p (t e) -> p t e", e=NE), start9[:, 0:8, :], ALU.add)
            link(dve.tensor_tensor(sel[:, 8:9, :], bank(7)[:, 0:NE].unsqueeze(1), start9[:, 8:9, :], ALU.add))
            link(dve.tensor_tensor(pos.rearrange("p e t -> p t e"), sel, mask, ALU.mult))
            dve.tensor_scalar(lasti[:, :], tend[0:1, :], -1.0, None, ALU.add)
            link(dve.tensor_scalar(cnt, tend[:, :], float(P), None, ALU.mult))
            ef = score[0:1, 0:4, :].rearrange("p t e -> p (t e)")[:, 0:TAB]
            step = NT * NE * TOPK // NE
            for a in range(0, TAB, step):
                m = min(step, TAB - a)
                past = rtmp[0:1, :].bitcast(BF16)[:, 0:m * NE].rearrange("p (i e) -> p i e", e=NE)
                link(dve.tensor_tensor(past, cnt[0:1, :].unsqueeze(1).to_broadcast([1, m, NE]),
                                       base[0:1, a:a + m].unsqueeze(2).to_broadcast([1, m, NE]), ALU.is_le))
                link(dve.tensor_reduce(ef[:, a:a + m], past, AX.X, ALU.add))
            dve.tensor_scalar(etab[:, :], ef, float(NE - 1), None, ALU.min).then_inc(tables, 1)
            dve.wait_ge(tables, 1)
            dve.wait_ge(shd_mm, NT)

            def one_hot(i):
                e = dve.value_load(etab[0:1, bass.ds(i, 1)], min_val=0, max_val=NE - 1)
                dve.scalar_tensor_tensor(oh, pos[:, bass.ds(e, 1), :].rearrange("p a t -> p t a").to_broadcast([P, NT, P]),
                                         base[:, bass.ds(i, 1)], iota1[:, :].unsqueeze(1).to_broadcast([P, NT, P]),
                                         ALU.subtract, ALU.is_equal).then_inc(oh_s, 1)

            def slots(i):
                s = bank(6)
                dve.wait_ge(slot_mm, i + 1)
                dve.tensor_reduce(sl[:, 0:1], s[:, 0:2], AX.X, ALU.add)
                dve.tensor_reduce(wtab[:, bass.ds(i, 1)], s[:, 2:5], AX.X, ALU.add).then_inc(dstep, 1)
                dve.wait_ge(dstep, 2 * i + 1)
                dve.tensor_scalar(sl[:, 1:2], sl[:, 0:1], 0.0, padcol[:, 0:1], ALU.is_equal, ALU.mult).then_inc(dstep, 1)
                dve.wait_ge(dstep, 2 * i + 2)
                dve.scalar_tensor_tensor(itab[:, bass.ds(i, 1)], sl[:, 0:1], -1.0, sl[:, 1:2], ALU.add, ALU.add)
                dve.scalar_tensor_tensor(idxg[:, 0:1], sl[:, 0:1], -1.0, sl[:, 1:2], ALU.add, ALU.add).then_inc(idx_s, 1)

            def act_of(i):
                dve.wait_ge(silu_s, i + 1)
                dve.tensor_tensor(act_m, sg, bank(4)[:, DE:2 * DE], ALU.mult).then_inc(act_s, 1)

            def at_copy(i):
                dve.wait_ge(at_mm, i + 1)
                dve.tensor_copy(actT_m, bank(5)[:, 0:DE].rearrange("p (k n) -> p k n", k=KF)).then_inc(at_s, 1)

            def y_of(i):
                dve.wait_ge(dn_mm, i + 1)
                dve.tensor_copy(idxs[:, 0:1], itab[:, bass.ds(i, 1)])
                dve.tensor_scalar(yw, pair(2), wtab[:, bass.ds(i, 1)], None, ALU.mult).then_inc(yw_s, 1)

            dve.sem_inc(yw_s, 1)
            one_hot(0)
            slots(0)
            one_hot(1)
            dve.wait_ge(gathered, 16)
            slots(1)
            one_hot(2)
            act_of(0)
            dve.wait_ge(gathered, 32)
            slots(2)
            last = dve.value_load(lasti[0:1, NE - 1:NE], min_val=NE - 1, max_val=MAX_TILES - 1)

            def tile(i):
                at_copy(i - 1)
                one_hot(i + 2)
                act_of(i)
                dve.wait_ge(gathered, 16 * (i + 2))
                slots(i + 2)
                dve.wait_ge(added, 16 * i)
                y_of(i - 1)
            tiles(dve, tile, last)
            at_copy(last)
            dve.wait_ge(added, 16 * (last + 1))
            y_of(last)

            for g in range(3):
                three = slice(3 * g, 3 * g + 3)
                dve.wait_ge(fin_ss, g + 1)
                mean_eps(ss3[:, three]).then_inc(fin_ms, 1)
                dve.wait_ge(fin_sq, g + 1)
                link(dve.reciprocal(r3[:, three], r3[:, three]))
                for t in range(3 * g, 3 * g + 3):
                    r, c = slice(0, ROWS[t]), t // (SEQ // P)
                    dve.scalar_tensor_tensor(y_t(t)[r, :], y_t(t)[r, :], r3[r, t:t + 1], rowsb[r, 3, c, :],
                                             ALU.mult, ALU.mult).then_inc(fin_g, 1)
                    if t % 2:
                        dve.wait_ge(fin_g, t + 1)
                        dve.tensor_tensor(x[r, t, :], x[r, t, :], y_t(t)[r, :], ALU.add).then_inc(fin_s[t % 2], 1)

        @block.tensor
        def _(pe):
            pe.wait_ge(const_pool, 1)
            pe.wait_ge(small_in, 16 * 5)
            pe.transpose(bank(7)[:, 0:100], stg[:, :], ident[0:100, 0:100]).then_inc(stg_t, 1)

            def transposes(t):
                r = slice(0, ROWS[t])
                pe.wait_ge(xn_s, t + 1)
                if t >= 2:
                    pe.wait_ge(ht_s, t - 1)
                for k in range(KD):
                    ins = pe.transpose(pair(2 * (t % 2))[:, P * k:P * k + ROWS[t]], xb[t % 6][r, P * k:P * (k + 1)],
                                       ident[r, r])
                ins.then_inc(ht_mm, 1)

            pe.wait_ge(sil_s, 1)
            for b in range(4):
                pe.wait_ge(ada_in[b], 16)
                for k in range(KD):
                    ins = pe.matmul(bank(b)[0:2, :], sil[:, k, :], ada[b][:, k, :], start=(k == 0), stop=(k == KD - 1))
                ins.then_inc(ada_mm, 1)
            pe.wait_ge(mrow_s, 4)
            for r_ in range(2 * KD):
                ins = pe.transpose(bank(6)[:, 2 * r_:2 * r_ + 2], mrow[:, P * r_:P * (r_ + 1)], ident[0:2, 0:2])
            ins.then_inc(mcol_mm, 1)
            for t in range(NT):
                transposes(t)

            pe.wait_ge(misc_in, 16 * 6)
            pe.wait_ge(rstd_s, 3)
            for g in range(NG):
                pe.transpose(bank(4)[:, HIST * g:HIST * (g + 1)], stin[:, P * g:P * (g + 1)], ident[0:HIST, 0:HIST])
            pe.transpose(bank(5)[:, 0:WIN], ckin[:, :], ident[:, :]).then_inc(misc_mm, 1)

            def ada_rows(i):
                pe.wait_ge(acc_s, 2 * KD * (i + 1))
                if i >= 1:
                    pe.wait_ge(row_s, 2 * i)
                for c in range(2):
                    for half in range(2):
                        ins = pe.matmul(bank((6 if c == 0 else 4) + half), ones[:, :], acc[c][:, 512 * half:512 * (half + 1)],
                                        start=True, stop=True)
                ins.then_inc(row_mm, 1)

            pe.wait_ge(w_in_s[0], 16)
            pe.wait_ge(misc_ev, 1)
            for n, (kind, c, a, n_) in enumerate(groups):
                if n == 0:
                    pe.wait_ge(ht_s, NT)
                if n == N_U:
                    pe.wait_ge(w_in_s[1], 16)
                if n == N_V:
                    pe.wait_ge(w_in_s[2], 16)
                if n in ROWS_AT:
                    ada_rows(ROWS_AT.index(n))
                if n >= 4:
                    pe.wait_ge(ev_s, n - 3)
                out = bank(n % 4)
                if kind == "ct":
                    for k in range(KD):
                        ins = pe.matmul(out[:, 0:n_], w1[:, k, P * c:P * (c + 1)], hT[:, k, a:a + n_], start=(k == 0), stop=(k == KD - 1))
                elif kind == "v":
                    for t in range(4 * c, min(4 * c + 4, NT)):
                        o = out[0:ROWS[t], P * (t % 4):P * (t % 4) + KV]
                        for k in range(KD):
                            ins = pe.matmul(o, hT[:, k, P * t:P * t + ROWS[t]], w1[:, k, INW - KV:INW],
                                            start=(k == 0), stop=(k == KD - 1))
                else:
                    pe.wait_ge(pooled, c + 1)
                    pe.wait_ge(wpool_s, 16)
                    o = HIST + a if a < SEQ else US + HIST
                    ins = pe.matmul(out[:, 0:n_], wpool[:, c, :], u[:, c, o:o + n_], start=True, stop=True)
                ins.then_inc(proj_mm, 1)
                if n == LAST_U:
                    pe.wait_ge(ev_s, N_U)
                    pe.wait_ge(row_s, 8)
                    for g in range(NG):
                        pe.transpose(bank(4)[0:HIST, P * g:P * (g + 1)], u[:, g, US - HIST:US], ident[:, :])
                        ins = pe.transpose(bank(5)[0:HIST, P * g:P * (g + 1)], u[:, g, UL - HIST:UL], ident[:, :])
                    ins.then_inc(outs_mm, 1)
                if n == N_PROJ - 1:
                    pe.wait_ge(ev_s, N_PROJ)
                    pe.transpose(bank(6)[:, 0:KV], kT[:, SEQ - WIN:SEQ], ident[:, :])
                    pe.transpose(bank(6)[0:DEC, KV:2 * KV], kT[:, SEQ + WIN:KL], ident[:, :]).then_inc(outs_mm, 1)

            def scores(n):
                b, (qc, kc, nk, _, _) = n % 2, CHUNKS[n]
                pe.wait_ge(qbd_s, 2 * (n + 1))
                if n >= 2:
                    pe.wait_ge(ex_s, n - 1)
                for j in range(NJ):
                    ins = pe.matmul(ps[:, 2 * b + j // 2, 192 * (j % 2):192 * (j % 2) + nk], qbd[b][:, j, :],
                                    kT[:, kc:kc + nk], start=True, stop=True)
                ins.then_inc(sc_mm, 1)

            def prob_t(n):
                b, nk = n % 3, CHUNKS[n][2]
                pe.wait_ge(pr_s, n + 1)
                if n >= 1:
                    pe.wait_ge(pta_s, n)
                    pe.wait_ge(ptb_s, n)
                for j in range(NJ):
                    if nk >= 128:
                        ins = pe.transpose(bank(4)[:, P * j:P * (j + 1)], probs[b][:, j, 0:128], ident[:, :])
                    if nk % 128:
                        ins = pe.transpose(bank(5)[0:64, P * j:P * (j + 1)], probs[b][:, j, nk - 64:nk], ident[:, :])
                ins.then_inc(pt_mm, 1)

            def pv(n):
                b, (_, _, nk, where, tile) = n % 2, CHUNKS[n]
                v = vodd if where == "odd" else vt
                pe.wait_ge(pta_s, n + 1)
                pe.wait_ge(ptb_s, n + 1)
                if n >= 2:
                    pe.wait_ge(o_s, n - 1)
                for h in range(2):
                    r = slice(64 * h, 64 * h + 64)
                    out = bank(6 + b)[r, 0:NJ * CHUNK]
                    if nk >= 128:
                        ins = pe.matmul(out, v[:, tile, r], pta[b][:, :, r], start=True, stop=(nk == 128))
                    if nk % 128:
                        ins = pe.matmul(out, v[0:64, tile + 1, r], ptb[b][:, :, r], start=(nk == 64), stop=True)
                ins.then_inc(pv_mm, 1)

            pe.wait_ge(ev_s, len(groups))
            pe.wait_ge(outs_ev, 1)
            pe.wait_ge(vodd_s, 48)
            for m in range(NCH + 3):
                if m < NCH:
                    scores(m)
                if 2 <= m <= NCH + 1:
                    prob_t(m - 2)
                if m >= 3:
                    pv(m - 3)

            pe.wait_ge(o_s, NCH)
            pe.wait_ge(w_out_s, 48)

            def mix(t):
                if t >= 2:
                    pe.wait_ge(res_s, t - 1)
                for half in range(2):
                    for k in range(KD):
                        ins = pe.matmul(bank(2 * (t % 2) + half)[0:ROWS[t], :], hT[:, k, P * t:P * t + ROWS[t]],
                                        wo[:, k, 512 * half:512 * half + 512], start=(k == 0), stop=(k == KD - 1))
                ins.then_inc(mix_mm, 1)

            def h2_t(t):
                r = slice(0, ROWS[t])
                pe.wait_ge(h2_s, t + 1)
                if t >= 1:
                    pe.wait_ge(h2t_s, t)
                for k in range(KD):
                    ins = pe.transpose(pair(4)[:, P * k:P * k + ROWS[t]], h2p[t % 2][r, P * k:P * (k + 1)], ident[r, r])
                ins.then_inc(h2t_mm, 1)

            def logits(t):
                pe.wait_ge(h2t_s, t + 1)
                out = bank(6 + t // 8)[0:ROWS[t], NE * (t % 8):NE * (t % 8 + 1)]
                for k in range(KD):
                    ins = pe.matmul(out, hT[:, k, P * t:P * t + ROWS[t]], wrt[:, k, :], start=(k == 0), stop=(k == KD - 1))
                ins.then_inc(log_mm, 1)

            for t in range(NT + 1):
                if t < NT:
                    mix(t)
                if t >= 1:
                    h2_t(t - 1)
                if t >= 2:
                    logits(t - 2)
            logits(NT - 1)

            def swiglu_in(xt, w, cols):
                gu = gate_up(w)
                for k in range(KD):
                    ins = pe.matmul(bank(4)[0:cols, :], xt[:, k, :], gu[:, :, k, :], start=(k == 0), stop=(k == KD - 1))
                return ins

            def swiglu_out(b, at_, w, cols):
                d = down(w)
                for half in range(2):
                    for k in range(KF):
                        ins = pe.matmul(bank(b + half)[0:cols, :], at_[:, k, 0:cols], d[:, k, 512 * half:512 * half + 512],
                                        start=(k == 0), stop=(k == KF - 1))
                return ins

            pe.wait_ge(wsh_s, 48)

            def sh_out(t):
                r = slice(0, ROWS[t])
                pe.wait_ge(sht_s, t + 1)
                if t >= 1:
                    pe.wait_ge(shy_s, t)
                swiglu_out(0, actTs, wsh, ROWS[t]).then_inc(shd_mm, 1)

            def sh_t(t):
                r = slice(0, ROWS[t])
                pe.wait_ge(sha_s, t + 1)
                if t >= 1:
                    pe.wait_ge(shd_mm, t)
                for k in range(KF):
                    ins = pe.transpose(bank(5)[:, P * k:P * k + ROWS[t]], acts[r, P * k:P * (k + 1)], ident[r, r])
                ins.then_inc(sht_mm, 1)

            for t in range(NT):
                if t >= 1:
                    sh_t(t - 1)
                swiglu_in(hT[:, :, P * t:P * t + ROWS[t]], wsh, ROWS[t]).then_inc(shg_mm, 1)
                if t >= 1:
                    sh_out(t - 1)
                if t == 6:
                    pe.wait_ge(maskb_s, 1)
                    for tt in range(NT + 1):
                        out = bank(6)[:, NE * tt:NE * (tt + 1)] if tt < 8 else bank(7)[:, NE * (tt - 8):NE * (tt - 7)]
                        for s in range(min(tt + 1, NT)):
                            ins = pe.matmul(out, (triub if s == tt else onesb)[:, :], maskb[:, s, :],
                                            start=(s == 0), stop=(s == min(tt, NT - 1)))
                    ins.then_inc(rank_mm, 1)
            sh_t(NT - 1)
            sh_out(NT - 1)

            def slots(i):
                e = pe.value_load(etab[0:1, bass.ds(i, 1)], min_val=0, max_val=NE - 1)
                pe.wait_ge(oh_s, i + 1)
                for t in range(NT):
                    ins = pe.matmul(bank(6)[:, 0:5], oh[:, t, :], wp[:, t, bass.ds(e, 1), :].rearrange("p a c -> p (a c)"),
                                    start=(t == 0), stop=(t == NT - 1))
                ins.then_inc(slot_mm, 1)

            def x_t(i):
                pe.wait_ge(gathered, 16 * (i + 1))
                for k in range(KD):
                    ins = pe.transpose(pair(0)[:, P * k:P * (k + 1)], xg[:, P * k:P * (k + 1)], ident[:, :])
                ins.then_inc(xt_mm, 1)

            def ring_slot(i):
                e = pe.value_load(etab[0:1, bass.ds(i, 1)], min_val=0, max_val=NE - 1)
                return e, (e & (RING - 1)) * WSLOT

            def expert_in(i):
                e, o = ring_slot(i)
                pe.wait_ge(w_ready, e + 1)
                pe.wait_ge(xt_s, i + 1)
                swiglu_in(xT, big[:, bass.ds(o, WSLOT)], P).then_inc(gu_mm, 1)

            def act_t(i):
                pe.wait_ge(act_s, i + 1)
                for k in range(KF):
                    ins = pe.transpose(bank(5)[:, P * k:P * (k + 1)], act_m[:, P * k:P * (k + 1)], ident[:, :])
                ins.then_inc(at_mm, 1)

            def expert_out(i):
                e, o = ring_slot(i)
                pe.wait_ge(at_s, i + 1)
                swiglu_out(2, actT_m, big[:, bass.ds(o, WSLOT)], P).then_inc(dn_mm, 1)

            pe.wait_ge(tables, 1)
            pe.wait_ge(shy_s, NT)
            slots(0)
            pe.wait_ge(idx_s, 1)
            slots(1)
            x_t(0)
            expert_in(0)
            pe.wait_ge(xt_s, 1)
            x_t(1)
            pe.wait_ge(idx_s, 2)
            slots(2)
            last = pe.value_load(lasti[0:1, NE - 1:NE], min_val=NE - 1, max_val=MAX_TILES - 1)

            def tile(i):
                act_t(i - 1)
                expert_in(i)
                x_t(i + 1)
                pe.wait_ge(idx_s, i + 2)
                slots(i + 2)
                pe.wait_ge(yw_s, i)
                expert_out(i - 1)
            tiles(pe, tile, last)
            act_t(last)
            pe.wait_ge(yw_s, last + 1)
            expert_out(last)


_INS = ["x_prompt", "x_sample", "c_prompt", "c_sample", "state_pool", "cache_k", "cache_v", "w_ada", "b_ada",
        "norm_gains", "w_in", "w_pool", "pool_scale", "attn_sinks", "w_out", "w_router", "router_bias",
        "w_gate", "w_up", "w_down", "ws_gate", "ws_up", "ws_down"]
_OUTS = [(1, SEQ, D), (1, DEC, D), (1, 1, HIST, PW), (1, 1, WIN, 2, HD), (1, 1, WIN, 2, HD),
         (1, 1, HIST, PW), (1, 1, WIN, 2, HD), (1, 1, WIN, 2, HD)]


def kernel(**inputs):
    import numpy as _np
    import concourse.bacc as _bacc
    from concourse import mybir as _mybir
    from concourse.bass_utils import run_bass_kernel_spmd as _run

    nc = _bacc.Bacc("TRN2", target_bir_lowering=False, num_devices=1)
    arrays, args = {}, []
    for name in _INS:
        a = _np.asarray(inputs[name])
        if name == "w_in":
            qcols = a[..., PW:PW + 512].reshape(1, D, 2, NJ, HD).transpose(0, 1, 3, 2, 4).reshape(1, D, 512)
            a = _np.concatenate([a[..., :PW], qcols, a[..., PW + 512:]], axis=-1)
        a = _np.ascontiguousarray(a)
        arrays[f"in_{name}_dram"] = a
        args.append(nc.dram_tensor(f"in_{name}_dram", a.shape, _mybir.dt.from_np(a.dtype), kind="ExternalInput").ap())
    for i, shape in enumerate(_OUTS):
        args.append(nc.dram_tensor(f"out_{i}_dram", shape, F32, kind="ExternalOutput").ap())
    build(nc, *args)
    r = _run(nc, [arrays], core_ids=[0])
    return tuple(r.results[0][f"out_{i}_dram"] for i in range(len(_OUTS)))
```

```python
from contextlib import ExitStack

import concourse.bass as bass
from concourse import mybir

F32 = mybir.dt.float32
F32R = mybir.dt.float32r
BF16 = mybir.dt.bfloat16
I32 = mybir.dt.int32
U32 = mybir.dt.uint32
ALU = mybir.AluOpType
ACT = mybir.ActivationFunctionType
AX = mybir.AxisListType

P = 128
D = 1024
KD = D // P
SEQ, DEC = 1024, 64
N = SEQ + DEC
NT = -(-N // P)
ROWS = [min(P, N - P * t) for t in range(NT)]
CHUNK = 64
PW = 512
WINDOWS = (2, 4, 8, 16)
NG = len(WINDOWS)
HIST = max(WINDOWS) - 1
HD = 64
NJ = 4
KV = 128
WIN = 128
INW = PW + 512 + 2 * KV
NE, TOPK, EG, TOPG = 64, 6, 8, 4
DE = 256
KF = DE // P
SCALE_R = 2.5
EPS = 1e-6
MAX_TILES = -(-(N * TOPK + NE * P) // P)
GROUPS, GROUP = 7, 8
AHEAD = 3
assert NE - 1 + GROUPS * GROUP >= MAX_TILES and GROUP % 2 == 0 and NE % 2 == 0
TAB = NE + GROUPS * GROUP + AHEAD
RING = 4
HIS = 2
SBUF_AT = 16512
PIECES = 4
WSLOT = KD * 2 * DE + KF * D

UL = HIST + SEQ + HIST + DEC
US = HIST + SEQ
KL = SEQ + WIN + DEC
BLOCKS = [(0, 512), (512, 512), (1024, DEC)]

CHUNKS = [(0, 0, 64, "v", -1), (64, 0, 128, "v", 0)]
for _c in range(2, SEQ // CHUNK):
    CHUNKS.append((64 * _c, 64 * (_c - 2), 192, "odd" if _c % 2 else "v", (_c - 2) // 2))
CHUNKS.append((SEQ, SEQ, 192, "v", SEQ // P))


def build(nc, x_prompt, x_sample, c_prompt, c_sample, state_pool, cache_k, cache_v, w_ada, b_ada,
          norm_gains, w_in, w_pool, pool_scale, attn_sinks, w_out, w_router, router_bias,
          w_gate, w_up, w_down, ws_gate, ws_up, ws_down,
          y_prompt, y_sample, pool_p, k_p, v_p, pool_s, k_s, v_s):
    with ExitStack() as ctx:
        def sb(name, shape, dt=F32):
            return ctx.enter_context(nc.sbuf_tensor(name, shape, dt))

        def sem(name):
            return ctx.enter_context(nc.semaphore(name))

        h2_rows = nc.dram_tensor("h2_rows", (N, D), F32, kind="Internal").ap()
        x1_rows = nc.dram_tensor("x1_rows", (N, D), F32, kind="Internal").ap()
        y_acc = nc.dram_tensor("y_acc", (N + P, D), F32, kind="Internal").ap()

        BIG, TR, XS, RW = RING * WSLOT, KD * N, NT * D, 4 * 2 * D
        arena = sb("arena", [P, BIG + TR + XS + RW])
        big = arena[:, 0:BIG]
        tr = arena[:, BIG:BIG + TR]
        xs = arena[:, BIG + TR:BIG + TR + XS]
        rowsb = arena[:, BIG + TR + XS:BIG + TR + XS + RW].rearrange("p (a c n) -> p a c n", a=4, c=2)

        def f32r_at(name, where, n):
            return nc.alloc_sbuf_tensor_at(name, [P, n], F32R, offset=SBUF_AT + 4 * where)
        lor = f32r_at("lo_ring", 0, BIG)
        hi_gu = f32r_at("hi_gate_up", BIG + TR, (HIS - 1) * WSLOT + 2 * KD * DE)
        hi_dn = f32r_at("hi_down", BIG + TR + 2 * KD * DE, (HIS - 1) * WSLOT + KF * D)
        MAT = KD * DE
        raw = [nc.alloc_sbuf_tensor_at(f"raw{m}", [P, (RING - 1) * WSLOT + MAT], F32, offset=SBUF_AT + 4 * MAT * m)
               for m in range(3)]
        assert WSLOT == 3 * MAT
        colv = sb("colv", [P, 100])
        sil = sb("sil", [P, KD, 2])
        mods = sb("mods", [P, 2 * KD, 2])
        a1 = sb("a1", [P, KD, 2])
        ident = sb("ident", [P, P])
        ones = sb("ones", [P, P])
        onesb = sb("onesb", [P, P], BF16)
        triub = sb("triub", [P, P], BF16)
        iota1 = sb("iota1", [P, P])
        base = sb("base", [P, TAB])
        padcol = sb("padcol", [P, 1])
        prow = sb("prow", [P, 1])
        iotae = sb("iotae", [P, NE])
        lower8 = sb("lower8", [P, EG, EG])
        rec = sb("rec", [P, 16])
        ss = sb("ss", [P, NT])
        rstd = sb("rstd", [P, NT])
        ss1 = sb("ss1", [P, NT])
        r1 = sb("r1", [P, NT])
        ss2 = sb("ss2", [P, NT])
        r2 = sb("r2", [P, NT])
        ss3 = sb("ss3", [P, NT])
        r3 = sb("r3", [P, NT])
        sink = sb("sink", [P, NJ])
        wrt = sb("wrt", [P, KD, NE])
        rbias = sb("rbias", [P, NE])
        wtab = sb("wtab", [P, TAB])
        itab = sb("itab", [P, TAB])
        idxg = [sb(f"idxg{b}", [P, 1], I32) for b in range(2)]
        idxs = [sb(f"idxs{b}", [P, 1], I32) for b in range(2)]
        wcol = [sb(f"wcol{b}", [P, 1]) for b in range(2)]
        sl = sb("sl", [P, 4])
        etab = sb("etab", [1, TAB], I32)
        ftab = sb("ftab", [1, TAB], I32)
        lasti = sb("lasti", [1, NE], I32)

        hT = tr[:, :].rearrange("p (k n) -> p k n", k=KD)
        def tr_at(at, n):
            return tr[:, at:at + n]
        xg = [tr_at(0, D), tr_at(D, D)]
        yw = [tr_at(2 * D, D), tr_at(3 * D, D)]
        oh = tr_at(4 * D, NT * P // 2).bitcast(BF16).rearrange("p (t s) -> p t s", t=NT)
        sg = tr_at(5 * D, DE)
        act_m = tr_at(5 * D + DE, DE)
        def f32r_tiles(name, where, k):
            return f32r_at(name, where, k * P)[:, :].rearrange("p (k n) -> p k n", k=k)
        xTh, xTl = f32r_tiles("xTh", BIG + 6 * D, KD), f32r_tiles("xTl", BIG + 7 * D, KD)
        aTh, aTl = f32r_tiles("aTh", BIG + 8 * D, KF), f32r_tiles("aTl", BIG + 5 * D + 2 * DE, KF)

        def at(a, n):
            return big[:, a:a + n]
        ada = [a_.rearrange("p (k n) -> p k n", k=KD) for a_ in
               (at(0, KD * 512), at(WSLOT + KD * INW, KD * 512), at(WSLOT + KD * INW + KD * 512, KD * 512),
                tr_at(0, KD * 512))]
        q = at(0, NJ * N).rearrange("p (j n) -> p j n", j=NJ)
        kT = at(NJ * N, KL)
        w1 = at(WSLOT, KD * INW).rearrange("p (k n) -> p k n", k=KD)
        wo = at(WSLOT, KD * D).rearrange("p (k n) -> p k n", k=KD)
        vat = WSLOT + KD * INW
        vt = at(vat, 10 * KV).rearrange("p (t n) -> p t n", n=KV)
        sF = WSLOT + KD * D
        tmpf = at(sF, D)
        junkf = at(sF + D, D)
        h2p = [at(sF + 2 * D, D), at(sF + 3 * D, D)]
        assert sF + 4 * D <= 3 * WSLOT and vat + 10 * KV <= 3 * WSLOT and NJ * N + KL <= WSLOT
        u = at(3 * WSLOT, NG * UL).rearrange("p (g n) -> p g n", g=NG)
        vodd = at(3 * WSLOT + NG * UL, 8 * KV).rearrange("p (t n) -> p t n", n=KV)
        assert NG * UL + 8 * KV <= WSLOT
        wpool = at(vat + 10 * KV, NG * P).rearrange("p (g n) -> p g n", g=NG)
        assert vat + 10 * KV + NG * P <= 3 * WSLOT
        at_g = [0]
        Xh = [f32r_tiles("Xh0", WSLOT - 2 * D, KD), f32r_tiles("Xh1", BIG + TR + WSLOT + 2 * DE, KD)]
        Xl = [f32r_tiles("Xl0", WSLOT - D, KD), f32r_tiles("Xl1", BIG + TR + WSLOT + 2 * DE + D, KD)]
        aTsh, aTsl = f32r_tiles("aTsh", BIG + TR + WSLOT, KF), f32r_tiles("aTsl", BIG + TR + WSLOT + DE, KF)
        def g_buf(n):
            at_g[0] += n
            assert at_g[0] <= WSLOT - 2 * D
            return at(at_g[0] - n, n)
        shy = [g_buf(D), g_buf(D)]
        sgs, ups, acts = g_buf(DE), g_buf(DE), g_buf(DE)
        actTs = g_buf(KF * P).rearrange("p (k n) -> p k n", k=KF)

        def x1_t(t):
            return at(WSLOT + D * t, D)

        def y_t(t):
            return at((3 * WSLOT + D * t) % BIG, D)

        def xf(t):
            return xs[:, WSLOT + D * (t % 3):WSLOT + D * (t % 3 + 1)]
        assert WSLOT + 3 * D <= XS

        xb = [rowsb[:, 1 + b // 2, b % 2, :] for b in range(6)]
        rowsb_flat = rowsb[:, :, :, :].rearrange("p a c n -> p (a c n)")
        mrow = rowsb_flat[0:2, 0:2 * D]

        at_s = [0]
        def s_buf(n):
            at_s[0] += n
            assert at_s[0] <= NT * D
            return xs[:, at_s[0] - n:at_s[0]]
        piece = [s_buf(D) for _ in range(PIECES)]
        acc = [s_buf(D), s_buf(D)]
        brow, grow = s_buf(D), s_buf(D)
        stin, ckin, stg = s_buf(PW)[0:HIST, :], s_buf(KV), s_buf(P)[0:100, :]
        at_s[0] = 0
        qbd = [s_buf(4 * P).rearrange("p (j n) -> p j n", j=NJ) for _ in range(2)]
        probs = [s_buf(768).rearrange("p (j n) -> p j n", j=NJ) for _ in range(3)]
        pta = [s_buf(4 * P).rearrange("p (j n) -> p j n", j=NJ) for _ in range(2)]
        ptb = [s_buf(4 * P)[0:64, :].rearrange("p (j n) -> p j n", j=NJ) for _ in range(2)]
        small = s_buf(3 * 7 * NJ).rearrange("p (b v j) -> p b v j", b=3, v=7)
        sums = [s_buf(UL), s_buf(UL)]
        fix = s_buf(16)
        outst_p = s_buf(2 * PW)[0:HIST, :].rearrange("p (a n) -> p a n", a=2)
        outst_k = s_buf(2 * KV).rearrange("p (a n) -> p a n", a=2)

        hb = rowsb[:, 0:3, :, :].rearrange("p a b n -> p (a b n)")
        at_h = [0]
        def h_buf(n):
            at_h[0] += n
            assert at_h[0] <= 3 * 2 * D
            return hb[:, at_h[0] - n:at_h[0]]
        score = h_buf(NT * NE).rearrange("p (t e) -> p t e", t=NT)
        rtmp = h_buf(NT * NE * TOPK // 2)
        g8 = rtmp[:, 2 * NT * NE:3 * NT * NE].rearrange("p (t g n) -> p t g n", t=NT, g=EG)
        sel = h_buf(NT * NE).rearrange("p (t e) -> p t e", t=NT)
        at_h[0] = HIS * WSLOT - XS
        wp = h_buf(NT * NE * 5 // 2).bitcast(BF16).rearrange("p (t e c) -> p t e c", t=NT, e=NE)
        pos = h_buf(NT * NE).rearrange("p (e t) -> p e t", t=NT)
        mask = h_buf(NT * NE).rearrange("p (t e) -> p t e", t=NT)
        def small_g(n, k=NT):
            return g_buf(n * k).rearrange("p (t n) -> p t n", t=k)
        maskb = g_buf(NT * NE // 2).bitcast(BF16).rearrange("p (t e) -> p t e", t=NT)
        gs, gm, top8, ixf = small_g(EG), small_g(EG), small_g(8), small_g(8)
        ix8 = g_buf(NT * 8).bitcast(U32).rearrange("p (t n) -> p t n", t=NT)
        cnt, ntl, tst = g_buf(NE), g_buf(NE), g_buf(NE)
        den = sb("den", [P, NT])
        tend = sb("tend", [P, NE])

        ps = ctx.enter_context(nc.psum_tensor("ps", [P, 8, 512], F32))

        def bank(b):
            return ps[:, b, :]

        def pair(b):
            return ps[:, b:b + 2, :].rearrange("p b n -> p (b n)")

        const_pool = sem("const_pool")
        small_in = sem("small_in")
        misc_in = sem("misc_in")
        ada_in = [sem(f"ada_in{s}") for s in range(4)]
        piece_in = [sem(f"piece_in{b}") for b in range(PIECES)]
        bg_in = sem("bg_in")
        acc_s = sem("acc_s")
        mrow_s = sem("mrow_s")
        mcol_mm = sem("mcol_mm")
        x_in = [sem(f"x_in{t}") for t in range(NT)]
        w_in_s = [sem(f"w_in_s{b}") for b in range(3)]
        w_out_s = sem("w_out_s")
        stg_t = sem("stg_t")
        colv_s = sem("colv_s")
        sil_s = sem("sil_s")
        ada_mm = sem("ada_mm")
        mods_s = sem("mods_s")
        row_mm = sem("row_mm")
        row_s = sem("row_s")
        dchain = sem("dchain")
        achain = sem("achain")
        pchain = sem("pchain")
        ss_s = sem("ss_s")
        ms_s = sem("ms_s")
        sq_s = sem("sq_s")
        rstd_s = sem("rstd_s")
        xn_s = sem("xn_s")
        ht_mm = sem("ht_mm")
        ht_s = sem("ht_s")
        hta_s = sem("hta_s")
        misc_mm = sem("misc_mm")
        misc_ev = sem("misc_ev")
        uz_s = sem("uz_s")
        proj_mm = sem("proj_mm")
        ev_s = sem("ev_s")
        outs_mm = sem("outs_mm")
        outs_ev = sem("outs_ev")
        stored = sem("stored")
        outs_st = sem("outs_st")
        pool_st = sem("pool_st")
        wpool_s = sem("wpool_s")
        dstep = sem("dstep")
        pool_turn = sem("pool_turn")
        pooled = sem("pooled")
        vodd_s = sem("vodd_s")
        qbd_s = sem("qbd_s")
        sc_mm = sem("sc_mm")
        mx_s = sem("mx_s")
        ex_s = sem("ex_s")
        pr_s = sem("pr_s")
        pt_mm = sem("pt_mm")
        pta_s = sem("pta_s")
        ptb_s = sem("ptb_s")
        pv_mm = sem("pv_mm")
        o_s = sem("o_s")
        mix_mm = sem("mix_mm")
        ssm_s = sem("ssm_s")
        msm_s = sem("msm_s")
        sqm_s = sem("sqm_s")
        res_s = sem("res_s")
        x1_s = sem("x1_s")
        ssx_s = sem("ssx_s")
        msx_s = sem("msx_s")
        sqx_s = sem("sqx_s")
        h2a_s = sem("h2a_s")
        h2_s = sem("h2_s")
        h2_st = [sem(f"h2_st{b}") for b in range(2)]
        h2t_mm = sem("h2t_mm")
        h2t_s = sem("h2t_s")
        log_mm = sem("log_mm")
        score_s = sem("score_s")
        wsh_s = sem("wsh_s")
        wsh_hi = sem("wsh_hi")
        wsh_lo = sem("wsh_lo")
        xh_s = sem("xh_s")
        xl_s = sem("xl_s")
        ath_s = sem("ath_s")
        x1_st = [sem(f"x1_st{b}") for b in range(3)]
        shg_mm = sem("shg_mm")
        shs_s = sem("shs_s")
        sha_s = sem("sha_s")
        sht_mm = sem("sht_mm")
        sht_s = sem("sht_s")
        shd_mm = sem("shd_mm")
        shy_s = sem("shy_s")
        shy_st = [sem(f"shy_st{b}") for b in range(2)]
        maskb_s = sem("maskb_s")
        rank_mm = sem("rank_mm")
        tables = sem("tables")
        gu_slot = [sem(f"gu_slot{s}") for s in range(RING)]
        dn_slot = [sem(f"dn_slot{s}") for s in range(RING)]
        gu_ready = sem("gu_ready")
        dn_ready = sem("dn_ready")
        round_gu = sem("round_gu")
        round_d = sem("round_d")
        lo_gu = sem("lo_gu")
        lo_d = sem("lo_d")
        oh_s = sem("oh_s")
        slot_mm = sem("slot_mm")
        idx_s = sem("idx_s")
        gathered = [sem("gathered_even"), sem("gathered_odd")]
        xt_mm = sem("xt_mm")
        xt_s = sem("xt_s")
        xtl_s = sem("xtl_s")
        gu_mm = sem("gu_mm")
        silu_s = sem("silu_s")
        act_s = sem("act_s")
        at_mm = sem("at_mm")
        at_s = sem("at_s")
        atl_s = sem("atl_s")
        slot_col = sem("slot_col")
        dn_mm = sem("dn_mm")
        yw_s = sem("yw_s")
        added = sem("added")
        y_in = [sem(f"y_in{t}") for t in range(NT)]
        fin_ss = sem("fin_ss")
        fin_ms = sem("fin_ms")
        fin_sq = sem("fin_sq")
        fin_g = sem("fin_g")
        fin_s = [sem("fin_even"), sem("fin_odd")]

        def chained(eng, s):
            n = [0]

            def link(ins):
                n[0] += 1
                ins.then_inc(s, 1)
                eng.wait_ge(s, n[0])
            return link

        def rows_of(prompt, sample, t):
            return prompt[0, P * t:P * (t + 1), :] if t < SEQ // P else sample[0, :, :]

        ada_view = w_ada[0].rearrange("(k p) n -> p k n", p=P)
        gate_v = w_gate[0].rearrange("e (p k) n -> e p (k n)", k=KD)
        up_v = w_up[0].rearrange("e (p k) n -> e p (k n)", k=KD)
        down_v = w_down[0].rearrange("e (k p) n -> e p k n", p=P)

        groups = []
        for ct in range(NG):
            for a, n_ in BLOCKS:
                groups.append(("ct", ct, a, n_))
        N_U = len(groups)
        for g in range(3):
            groups.append(("v", g, 0, 0))
        N_V = len(groups)
        for ct in range(NG, 9):
            for a, n_ in BLOCKS:
                groups.append(("ct", ct, a, n_))
        N_PROJ = len(groups)
        for g in range(NG):
            for a, n_ in BLOCKS:
                groups.append(("pool", g, a, n_))
        VECS = [(2, 0, 1), (3, 2, None), (4, 1, 2), (5, 3, 3)]
        LAST_U = N_V + 10
        ROWS_AT = [6, N_U, N_V + 3, N_V + 9]

        def evac_group(eng, n, kind, c, a, n_):
            src = bank(n % 4)
            def copy(out, in_):
                return eng.activation(out, in_, ACT.Copy)
            if kind == "v":
                if c < 2:
                    return copy(vt[:, 4 * c:4 * c + 4, :], src.rearrange("p (t n) -> p t n", t=4))
                return copy(vt[0:DEC, 9, :], src[0:DEC, 0:KV])
            if kind == "pool":
                out, sc = hT[:, c, a:a + n_], colv[:, 96 + c:97 + c]
                return eng.activation(out, src[:, 0:n_], ACT.Copy, scale=sc)
            if c < NG:
                to = HIST + a if a < SEQ else US + HIST
                return copy(u[:, c, to:to + n_], src[:, 0:n_])
            if c < 8:
                return copy(q[:, c - 4, a:a + n_], src[:, 0:n_])
            to = a if a < SEQ else SEQ + WIN
            return copy(kT[:, to:to + n_], src[:, 0:n_])

        NCH = len(CHUNKS)

        def raw_of(e, m):
            return raw[m][:, bass.ds(((e + 1) & (RING - 1)) * WSLOT, MAT)]

        def lo_of(e, m, n=1):
            return lor[:, bass.ds(((e + 1) & (RING - 1)) * WSLOT + m * MAT, n * MAT)]

        def hi_of(e, m, n=1):
            if m == 2:
                return hi_dn[:, bass.ds((e & (HIS - 1)) * WSLOT, MAT)]
            return hi_gu[:, bass.ds((e & (HIS - 1)) * WSLOT + m * MAT, n * MAT)]

        def split_rest(eng, e, m):
            return eng.tensor_tensor(lo_of(e, m), raw_of(e, m), hi_of(e, m).bitcast(F32), ALU.subtract)

        def raw_at(m, s):
            return raw[m][:, s * WSLOT:s * WSLOT + MAT]

        def sh_raw(m):
            return raw_at(m, 3)

        def sh_lo(m):
            return lor[:, 3 * WSLOT + m * MAT:3 * WSLOT + (m + 1) * MAT]

        def sh_hi(m):
            return hi_dn[:, 0:MAT] if m == 2 else hi_gu[:, m * MAT:(m + 1) * MAT]

        LAST_GROUPS = [(0, 1), (1, 3), (3, 6), (6, NT)]

        def tiles(eng, tile, last):
            with eng.Fori(0, NE // 2 - 1) as p:
                tile(p * 2 + 1, 1)
                tile(p * 2 + 2, 0)
            with eng.Fori(0, GROUPS) as g:
                with eng.If(g * GROUP + (NE - 1) <= last):
                    with eng.Fori(0, GROUP // 2) as p:
                        for odd in (1, 0):
                            i = g * GROUP + p * 2 + (NE - odd)
                            with eng.If(i <= last):
                                tile(i, odd)

        def last_tile(eng, last, step):
            for odd in range(2):
                with eng.If((last & 1) == odd):
                    step(last, odd)

        block = ctx.enter_context(nc.Block())

        @block.sync
        def _(sp):
            sp.dma_start(stg[0:48, :], b_ada[0].rearrange("(r n) -> r n", n=P)).then_inc(small_in, 16)
            sp.dma_start(stg[48:80, :], norm_gains[0].rearrange("g (r n) -> (g r) n", n=P)).then_inc(small_in, 16)
            sp.dma_start(stg[80:88, :], c_prompt[0].rearrange("(r n) -> r n", n=P)).then_inc(small_in, 16)
            sp.dma_start(stg[88:96, :], c_sample[0].rearrange("(r n) -> r n", n=P)).then_inc(small_in, 16)
            sp.dma_start(stg[96:100, :], pool_scale[0].rearrange("(r n) -> r n", n=P)).then_inc(small_in, 16)
            for b in range(4):
                sp.dma_start(ada[b], ada_view[:, :, 512 * b:512 * (b + 1)]).then_inc(ada_in[b], 16)
            for t in range(6):
                sp.dma_start(xb[t][0:ROWS[t], :], rows_of(x_prompt, x_sample, t)).then_inc(x_in[t], 16)
            w_in_v = w_in[0].rearrange("(k p) n -> p k n", p=P)
            sp.dma_start(w1[:, :, 0:PW], w_in_v[:, :, 0:PW]).then_inc(w_in_s[0], 16)
            sp.dma_start(w1[:, :, INW - KV:INW], w_in_v[:, :, INW - KV:INW]).then_inc(w_in_s[1], 16)
            sp.dma_start(w1[:, :, PW:INW - KV], w_in_v[:, :, PW:INW - KV]).then_inc(w_in_s[2], 16)
            for t in range(6, NT):
                sp.wait_ge(ht_mm, t - 5)
                sp.dma_start(xb[t - 6][0:ROWS[t], :], rows_of(x_prompt, x_sample, t)).then_inc(x_in[t], 16)
            sp.dma_start(wpool, w_pool[0].rearrange("g c d -> c g d")).then_inc(wpool_s, 16)
            sp.dma_start(vt[:, 8, :], cache_v[0, 0].rearrange("s h d -> s (h d)")).then_inc(vodd_s, 16)
            for i, (v, kind, gain_row) in enumerate(VECS):
                if i >= 1:
                    sp.wait_ge(row_s, 2 * i)
                sp.dma_start(brow, b_ada[0:1, D * v:D * (v + 1)].to_broadcast([P, D])).then_inc(bg_in, 16)
                if gain_row is not None:
                    sp.dma_start(grow, norm_gains[0, gain_row:gain_row + 1, :].to_broadcast([P, D])).then_inc(bg_in, 16)
                for k in range(KD):
                    m = KD * i + k
                    if m >= PIECES:
                        sp.wait_ge(acc_s, 2 * (m - PIECES + 1))
                    sp.dma_start(piece[m % PIECES], ada_view[:, k, D * v:D * (v + 1)]).then_inc(piece_in[m % PIECES], 16)
            sp.wait_ge(ev_s, N_V)
            sp.dma_start(vodd[0:64, 0:8, :], vt[64:128, 0:8, :]).then_inc(vodd_s, 16)
            sp.dma_start(vodd[64:128, 0:7, :], vt[0:64, 1:8, :]).then_inc(vodd_s, 16)
            sp.dma_start(v_p[0, 0].rearrange("s h d -> s (h d)"), vt[:, 7, :]).then_inc(stored, 16)
            sp.dma_start(v_s[0, 0, DEC:WIN].rearrange("s h d -> s (h d)"), vt[0:DEC, 9, :]).then_inc(stored, 16)
            sp.wait_ge(proj_mm, N_PROJ)
            sp.dma_start(wo[:, 0:NG, :], w_out[0, 0:PW].rearrange("(k p) n -> p k n", p=P)).then_inc(w_out_s, 16)
            for h in range(2):
                src = w_out[0, PW + 256 * h:PW + 256 * (h + 1)].rearrange("(j d) n -> d j n", d=HD)
                sp.dma_start(wo[64 * h:64 * h + 64, NG:NG + NJ, :], src).then_inc(w_out_s, 16)
            def load_gate_up(g, s):
                for m, v in enumerate((gate_v, up_v)):
                    src = v.rearrange("(g s) p n -> s g p n", s=RING)[s, bass.ds(g, 1)].rearrange("a p n -> (a p) n")
                    sp.dma_start(raw_at(m, (s + 1) % RING), src).then_inc(gu_slot[s], 16)

            def load_down(g, s):
                src = down_v.rearrange("(g s) p k n -> s g p k n", s=RING)[s, bass.ds(g, 1)].rearrange("a p k n -> (a p) k n")
                sp.dma_start(raw_at(2, (s + 1) % RING).rearrange("p (k n) -> p k n", k=KF), src).then_inc(dn_slot[s], 16)

            def load_expert(g, s):
                load_gate_up(g, s)
                load_down(g, s)

            sp.wait_ge(pv_mm, NCH)
            sp.wait_ge(outs_st, 64)
            for t in range(3):
                sp.dma_start(xf(t)[0:ROWS[t], :], rows_of(x_prompt, x_sample, t)).then_inc(x_in[t], 16)
            sp.dma_start(raw_at(0, 3), ws_gate[0].rearrange("(p k) n -> p (k n)", k=KD)).then_inc(wsh_s, 16)
            sp.dma_start(raw_at(1, 3), ws_up[0].rearrange("(p k) n -> p (k n)", k=KD)).then_inc(wsh_s, 16)
            sp.dma_start(raw_at(2, 3).rearrange("p (k n) -> p k n", k=KF), ws_down[0].rearrange("(k p) n -> p k n", p=P)).then_inc(wsh_s, 16)
            for t in range(NT):
                sp.wait_ge(x1_s, t + 1)
                sp.dma_start(x1_rows[P * t:P * t + ROWS[t], :], xf(t)[0:ROWS[t], :]).then_inc(x1_st[t % 3], 16)
                if 1 <= t < NT - 2:
                    u_ = t + 2
                    sp.wait_ge(x1_st[u_ % 3], 16 * (u_ // 3))
                    sp.wait_ge(h2a_s, t)
                    sp.dma_start(xf(u_)[0:ROWS[u_], :], rows_of(x_prompt, x_sample, u_)).then_inc(x_in[u_], 16)
                sp.wait_ge(h2_s, t + 1)
                sp.dma_start(h2_rows[P * t:P * t + ROWS[t], :], h2p[t % 2][0:ROWS[t], :]).then_inc(h2_st[t % 2], 16)
            sp.wait_ge(mix_mm, NT)
            sp.wait_ge(h2t_mm, NT)
            sp.wait_ge(h2_st[0], 16 * ((NT + 1) // 2))
            sp.wait_ge(h2_st[1], 16 * (NT // 2))
            sp.wait_ge(h2_s, NT)
            load_expert(0, 0)
            load_expert(0, 1)
            for t in range(NT):
                sp.wait_ge(shy_s, t + 1)
                sp.dma_start(y_acc[P * t:P * t + ROWS[t], :], shy[t % 2][0:ROWS[t], :]).then_inc(shy_st[t % 2], 16)
                if t in (4, 5):
                    sp.wait_ge(gu_slot[t - 4], 32)
                    sp.sem_inc(gu_ready, 1)
                    sp.wait_ge(dn_slot[t - 4], 16)
                    sp.sem_inc(dn_ready, 1)
            for b in range(2):
                sp.wait_ge(shy_st[b], 16 * ((NT + 1 - b) // 2))
            sp.wait_ge(shd_mm, NT)
            sp.wait_ge(tables, 1)
            for b in range(2):
                sp.wait_ge(gathered[b], 16)
            load_expert(0, 2)
            load_expert(0, 3)
            sp.wait_ge(gu_slot[2], 32)
            sp.sem_inc(gu_ready, 1)
            sp.wait_ge(dn_slot[2], 16)
            sp.sem_inc(dn_ready, 1)
            sp.wait_ge(gu_slot[RING - 1], 32)
            sp.sem_inc(gu_ready, 1)
            with sp.Fori(1, NE // RING) as g:
                for s in range(RING):
                    last_of = sp.value_load(lasti[0:1, :].rearrange("a (g s) -> a s g", s=RING)[:, s, bass.ds(g - 1, 1)],
                                            min_val=0, max_val=MAX_TILES - 1)
                    sp.wait_ge(gu_mm, last_of + 1)
                    load_gate_up(g, s)
                    if s == 0:
                        sp.wait_ge(dn_slot[RING - 1], g * 16)
                    else:
                        sp.wait_ge(dn_slot[s - 1], g * 16 + 16)
                    sp.sem_inc(dn_ready, 1)
                    sp.wait_ge(dn_mm, last_of + 1)
                    load_down(g, s)
                    sp.wait_ge(gu_slot[s], g * 32 + 32)
                    sp.sem_inc(gu_ready, 1)
            sp.wait_ge(dn_slot[RING - 1], 16 * NE // RING)
            sp.sem_inc(dn_ready, 1)

            for t in range(NT):
                if D * t % WSLOT == 0:
                    e = NE - RING + D * t // WSLOT
                    last_of = sp.value_load(lasti[0:1, e:e + 1], min_val=e, max_val=MAX_TILES - 1)
                    sp.wait_ge(dn_mm, last_of + 1)
                sp.dma_start(x1_t(t)[0:ROWS[t], :], x1_rows[P * t:P * t + ROWS[t], :]).then_inc(y_in[t], 16)
            last = sp.value_load(lasti[0:1, NE - 1:NE], min_val=NE - 1, max_val=MAX_TILES - 1)
            sp.wait_ge(added, 16 * (last + 3))
            for t in range(NT):
                sp.dma_start(y_t(t)[0:ROWS[t], :], y_acc[P * t:P * t + ROWS[t], :]).then_inc(y_in[t], 16)
            for t in range(NT):
                sp.wait_ge(fin_s[t % 2], t // 2 + 1)
                sp.dma_start(rows_of(y_prompt, y_sample, t), x1_t(t)[0:ROWS[t], :]).then_inc(stored, 16)
            sp.wait_ge(stored, 16 * (2 + NT))
            sp.wait_ge(pool_st, 32)

        @block.gpsimd
        def _(pool):
            link = chained(pool, pchain)
            pool.dma_start(sink[0:64, :], attn_sinks[0:1, 0:NJ].to_broadcast([64, NJ])).then_inc(misc_in, 16)
            pool.dma_start(sink[64:128, :], attn_sinks[0:1, NJ:2 * NJ].to_broadcast([64, NJ])).then_inc(misc_in, 16)
            pool.dma_start(rbias[:, :], router_bias[0:1, :].to_broadcast([P, NE])).then_inc(misc_in, 16)
            pool.dma_start(wrt[:, :, :].rearrange("p k n -> p (k n)"), w_router[0].rearrange("(p k) n -> p (k n)", k=KD)).then_inc(misc_in, 16)
            pool.dma_start(stin[:, :], state_pool[0, 0]).then_inc(misc_in, 16)
            pool.dma_start(ckin[:, :], cache_k[0, 0].rearrange("s h d -> s (h d)")).then_inc(misc_in, 16)
            pool.dma_start(k_s[0, 0, 0:DEC], cache_k[0, 0, DEC:WIN]).then_inc(pool_st, 16)
            pool.dma_start(v_s[0, 0, 0:DEC], cache_v[0, 0, DEC:WIN]).then_inc(pool_st, 16)
            for r in (0, P // 2):
                pool.dma_start(y_acc[N + r:N + r + P // 2, :], x_prompt[0, r:r + P // 2, :]).then_inc(added, 16)
            link(pool.memset(ident[:, :], 0.0))
            pool.affine_select(out=ident[:, :], in_=ident[:, :], compare_op=ALU.not_equal, fill=1.0, base=0,
                               pattern=[[-1, P]], channel_multiplier=1).then_inc(const_pool, 1)
            pool.memset(ones[:, :], 1.0)
            pool.memset(onesb[:, :], 1.0)
            link(pool.memset(triub[:, :], 1.0))
            pool.affine_select(out=triub[:, :], in_=triub[:, :], compare_op=ALU.is_gt, fill=0.0, base=0,
                               pattern=[[1, P]], channel_multiplier=-1)
            low = dict(allow_small_or_imprecise_dtypes=True)
            pool.iota(iota1[:, :], [[1, P]], base=1, channel_multiplier=0, **low)
            pool.iota(base[:, :], [[P, TAB]], base=0, channel_multiplier=0, **low)
            pool.iota(padcol[:, :], [[0, 1]], base=N + 1, channel_multiplier=1, **low)
            pool.iota(prow[:, :], [[0, 1]], base=1, channel_multiplier=1, **low)
            pool.iota(iotae[:, :], [[1, NE]], base=0, channel_multiplier=0, **low)
            pool.iota(rec[:, :], [[1, 16]], base=1, channel_multiplier=0, **low)
            link(pool.memset(lower8[:, :, :], 1.0))
            pool.affine_select(out=lower8[:, :, :], in_=lower8[:, :, :], compare_op=ALU.is_gt, fill=0.0, base=0,
                               pattern=[[1, EG], [-1, EG]], channel_multiplier=0)
            pool.memset(wtab[:, :], 0.0).then_inc(const_pool, 1)
            pool.wait_ge(const_pool, 2)
            pool.wait_ge(ada_mm, 4)
            pool.memset(u[:, :, 0:HIST], 0.0).then_inc(uz_s, 1)

            pool.wait_ge(row_mm, 4)
            for b in range(2):
                ins = pool.memset(qbd[b], 0.0)
            ins.then_inc(uz_s, 1)
            pool.wait_ge(uz_s, 2)
            pool.wait_ge(ev_s, N_PROJ - 3)
            for n, (qc, _, _, _, _) in enumerate(CHUNKS):
                if n >= 2:
                    pool.wait_ge(sc_mm, n - 1)
                for h in range(2):
                    r = slice(64 * h, 64 * h + 64)
                    pool.tensor_copy(qbd[n % 2][r, :, r], q[r, :, qc:qc + CHUNK]).then_inc(qbd_s, 1)
                    pool.wait_ge(qbd_s, 2 * n + h + 1)

            def rest(out, of, hi):
                return pool.tensor_tensor(out, of, hi.bitcast(F32), ALU.subtract)

            def sh_x(t):
                r = slice(0, ROWS[t])
                pool.wait_ge(xh_s, t + 1)
                rest(Xl[t % 2][:, :, r], hT[:, :, P * t:P * t + ROWS[t]], Xh[t % 2][:, :, r]).then_inc(xl_s, 1)

            for t in range(NT):
                r, c = slice(0, ROWS[t]), t // (SEQ // P)
                if t == NT - 1:
                    sh_x(0)
                pool.wait_ge(x_in[t], 32)
                pool.wait_ge(res_s, t + 1)
                pool.tensor_tensor(xf(t)[r, :], xf(t)[r, :], tmpf[r, :], ALU.add).then_inc(x1_s, 1)
                pool.wait_ge(h2a_s, t + 1)
                if t >= 2:
                    pool.wait_ge(h2_st[t % 2], 16 * (t // 2))
                    pool.wait_ge(h2t_mm, t - 1)
                pool.tensor_tensor(h2p[t % 2][r, :].rearrange("p (k q) -> p q k", k=KD),
                                   junkf[r, :].rearrange("p (q k) -> p q k", k=KD),
                                   rowsb[r, 2, c, :].rearrange("p (q k) -> p q k", k=KD), ALU.add).then_inc(h2_s, 1)
                if t == 5:
                    pool.wait_ge(wsh_hi, 2)
                    pool.tensor_tensor(sh_lo(1), sh_raw(1), sh_hi(1).bitcast(F32), ALU.subtract).then_inc(wsh_lo, 1)

            def sh_act(t):
                r = slice(0, ROWS[t])
                pool.wait_ge(ath_s, t + 1)
                rest(aTsl[:, :, r], actTs[:, :, r], aTsh[:, :, r]).then_inc(sht_s, 1)

            sh_x(1)
            for t in range(NT):
                r = slice(0, ROWS[t])
                if t >= 1:
                    sh_act(t - 1)
                pool.wait_ge(shs_s, 2 * (t + 1))
                if t >= 1:
                    pool.wait_ge(sht_mm, t)
                pool.tensor_tensor(acts[r, :], sgs[r, :], ups[r, :], ALU.mult).then_inc(sha_s, 1)
                if t + 2 < NT:
                    sh_x(t + 2)
            pool.wait_ge(xl_s, NT)
            for b in range(2):
                ins = pool.memset(xg[b], 0.0)
            ins.then_inc(uz_s, 1)
            sh_act(NT - 1)

            gather_bound, add_bound = pool.to_reg(N - 1), pool.to_reg(N + P - 1)

            def gather(i, b):
                pool.wait_ge(idx_s, i + 1)
                pool.sem_inc(pool_turn, 1)
                pool.indirect_dma_start(out=xg[b], out_offset=None, in_=h2_rows,
                                        in_offset=bass.IndirectOffsetOnAxis(ap=idxg[b][:, 0:1], axis=0),
                                        bounds_check=gather_bound, oob_is_err=False).then_inc(gathered[b], 16)

            def scatter_add(i, b):
                pool.wait_ge(added, 16 * (i + 2))
                pool.wait_ge(yw_s, i + 2)
                pool.sem_inc(pool_turn, 1)
                pool.indirect_dma_start(out=y_acc, out_offset=bass.IndirectOffsetOnAxis(ap=idxs[b][:, 0:1], axis=0),
                                        in_=yw[b], in_offset=None, bounds_check=add_bound,
                                        compute_op=ALU.add).then_inc(added, 16)

            def down_rest(e):
                pool.wait_ge(round_d, e + 1)
                split_rest(pool, e, 2).then_inc(lo_d, 1)

            pool.wait_ge(uz_s, 3)
            gather(0, 0)
            gather(1, 1)
            pool.wait_ge(xt_mm, 1)
            gather(2, 0)
            down_rest(0)
            pool.wait_ge(xt_mm, 2)
            gather(3, 1)
            for b in range(2):
                pool.wait_ge(shy_st[b], 16 * ((NT + 1 - b) // 2))
            pool.wait_ge(added, 32)
            pool.wait_ge(tables, 1)
            last = pool.value_load(lasti[0:1, NE - 1:NE], min_val=NE - 1, max_val=MAX_TILES - 1)

            def tile(i, odd):
                f = pool.value_load(ftab[0:1, bass.ds(i, 1)], min_val=0, max_val=2)
                e = pool.value_load(etab[0:1, bass.ds(i, 1)], min_val=0, max_val=NE - 1)
                with pool.If(f > 0):
                    down_rest(e)
                pool.wait_ge(xt_mm, i + 2)
                gather(i + AHEAD, 1 - odd)
                scatter_add(i - 1, 1 - odd)
            tiles(pool, tile, last)
            last_tile(pool, last, scatter_add)

            for t in range(0, NT, 2):
                r = slice(0, ROWS[t])
                pool.wait_ge(fin_g, t + 1)
                pool.tensor_tensor(x1_t(t)[r, :], x1_t(t)[r, :], y_t(t)[r, :], ALU.add).then_inc(fin_s[0], 1)

        @block.scalar
        def _(act):
            link = chained(act, achain)
            act.wait_ge(colv_s, 1)
            act.activation(sil[:, :, :].rearrange("p k c -> p c k"), colv[:, 80:96].rearrange("p (c k) -> p c k", c=2),
                           ACT.Silu).then_inc(sil_s, 1)
            def modulate(t):
                c = t // (SEQ // P)
                act.wait_ge(ht_mm, t + 1)
                for k in range(KD // 2, KD):
                    ins = act.activation(hT[:, k, P * t:P * t + ROWS[t]], pair(2 * (t % 2))[:, P * k:P * k + ROWS[t]],
                                         ACT.Identity, scale=a1[:, k, c:c + 1], bias=mods[:, k, c:c + 1])
                ins.then_inc(hta_s, 1)

            act.wait_ge(ms_s, 1)
            for g in range(3):
                three = range(3 * g, 3 * g + 3)
                for t in three:
                    r = slice(0, ROWS[t])
                    act.wait_ge(x_in[t], 16)
                    ins = act.activation(pair(4)[r, :], xb[t % 6][r, :], ACT.Square, accum_out=ss[r, t:t + 1])
                    if t < 3 * g + 2:
                        link(ins)
                    else:
                        ins.then_inc(ss_s, 1)
                act.wait_ge(ms_s, g + 2)
                act.activation(rstd[:, 3 * g:3 * g + 3], ss[:, 3 * g:3 * g + 3], ACT.Sqrt).then_inc(sq_s, 1)
                act.wait_ge(rstd_s, g + 1)
                for t in three:
                    r = slice(0, ROWS[t])
                    act.activation(xb[t % 6][r, :], xb[t % 6][r, :], ACT.Copy, scale=rstd[r, t:t + 1]).then_inc(xn_s, 1)
                if g == 0:
                    for b in range(4):
                        act.wait_ge(ada_mm, b + 1)
                        act.activation(mrow[:, 512 * b:512 * (b + 1)], bank(b)[0:2, :], ACT.Copy).then_inc(mrow_s, 1)
                    act.wait_ge(mods_s, 1)
                for t in three:
                    modulate(t)

            for n, (kind, c, a, n_) in enumerate(groups):
                act.wait_ge(proj_mm, n + 1)
                evac_group(act, n, kind, c, a, n_).then_inc(ev_s, 1)
                if n == N_PROJ - 1:
                    act.wait_ge(outs_mm, 2)
                    act.wait_ge(row_s, 8)
                    act.activation(outst_p[:, 0, :], bank(4)[0:HIST, :], ACT.Copy)
                    act.activation(outst_p[:, 1, :], bank(5)[0:HIST, :], ACT.Copy)
                    act.activation(outst_k[:, 0, :], bank(6)[:, 0:KV], ACT.Copy)
                    act.activation(outst_k[0:DEC, 1, :], bank(6)[0:DEC, KV:2 * KV], ACT.Copy).then_inc(outs_ev, 1)
                    act.wait_ge(outs_ev, 1)
                    act.dma_start(pool_p[0, 0], outst_p[:, 0, :]).then_inc(outs_st, 16)
                    act.dma_start(pool_s[0, 0], outst_p[:, 1, :]).then_inc(outs_st, 16)
                    act.dma_start(k_p[0, 0].rearrange("s h d -> s (h d)"), outst_k[:, 0, :]).then_inc(outs_st, 16)
                    act.dma_start(k_s[0, 0, DEC:WIN].rearrange("s h d -> s (h d)"), outst_k[0:DEC, 1, :]).then_inc(outs_st, 16)

            def exps(n):
                b, nk = n % 3, CHUNKS[n][2]
                act.wait_ge(mx_s, n + 1)
                if n >= 3:
                    act.wait_ge(pt_mm, n - 2)
                act.activation(small[:, b, 3, :], small[:, b, 2, :], ACT.Exp)
                for j in range(NJ):
                    src = ps[:, 2 * (n % 2) + j // 2, 192 * (j % 2):192 * (j % 2) + nk]
                    ins = act.activation(probs[b][:, j, 0:nk], src, ACT.Exp, bias=small[:, b, 1, j:j + 1],
                                         scale=HD ** -0.5, accum_out=small[:, b, 4, j:j + 1])
                ins.then_inc(ex_s, 1)

            def copy_pta(n):
                act.wait_ge(pt_mm, n + 1)
                if n >= 2:
                    act.wait_ge(pv_mm, n - 1)
                nk = CHUNKS[n][2]
                if nk >= 128:
                    act.activation(pta[n % 2], bank(4).rearrange("p (j n) -> p j n", j=NJ), ACT.Copy).then_inc(pta_s, 1)
                else:
                    act.sem_inc(pta_s, 1)

            def copy_o(n):
                act.wait_ge(pv_mm, n + 1)
                qc = CHUNKS[n][0]
                act.activation(hT[:, NG:NG + NJ, qc:qc + CHUNK],
                               bank(6 + n % 2)[:, 0:NJ * CHUNK].rearrange("p (j n) -> p j n", j=NJ), ACT.Copy).then_inc(o_s, 1)

            for m in range(NCH + 3):
                if m < NCH:
                    exps(m)
                if 2 <= m <= NCH + 1:
                    copy_pta(m - 2)
                if m >= 3:
                    copy_o(m - 3)

            def h2t_copy(t):
                act.wait_ge(h2t_mm, t + 1)
                act.activation(hT[:, :, P * t:P * t + ROWS[t]],
                               pair(4).rearrange("p (k n) -> p k n", k=KD)[:, :, 0:ROWS[t]], ACT.Copy).then_inc(h2t_s, 1)

            def round_x(t):
                r = slice(0, ROWS[t])
                act.wait_ge(h2t_s, t + 1)
                if t >= 2:
                    act.wait_ge(shg_mm, t - 1)
                act.activation(Xh[t % 2][:, :, r], hT[:, :, P * t:P * t + ROWS[t]], ACT.Copy).then_inc(xh_s, 1)

            for t in range(NT):
                r = slice(0, ROWS[t])
                if t == NT - 1:
                    round_x(0)
                act.wait_ge(mix_mm, t + 1)
                if t >= 1:
                    act.wait_ge(h2_s, t)
                act.activation(junkf[r, :], pair(2 * (t % 2))[r, :], ACT.Square, accum_out=ss1[r, t:t + 1]).then_inc(ssm_s, 1)
                if t >= 1:
                    h2t_copy(t - 1)
                if 3 <= t < 6:
                    act.wait_ge(wsh_s, 48)
                    act.activation(sh_hi(t - 3), sh_raw(t - 3), ACT.Copy).then_inc(wsh_hi, 1)
                act.wait_ge(msm_s, t + 1)
                act.activation(r1[r, t:t + 1], ss1[r, t:t + 1], ACT.Sqrt).then_inc(sqm_s, 1)
                act.wait_ge(x1_s, t + 1)
                act.activation(junkf[r, :], xf(t)[r, :], ACT.Square, accum_out=ss2[r, t:t + 1]).then_inc(ssx_s, 1)
                act.wait_ge(msx_s, t + 1)
                act.activation(r2[r, t:t + 1], ss2[r, t:t + 1], ACT.Sqrt).then_inc(sqx_s, 1)
            h2t_copy(NT - 1)
            def round_gate_up(e):
                act.wait_ge(gu_ready, e + 1)
                for m in range(2):
                    act.activation(hi_of(e, m), raw_of(e, m), ACT.Copy).then_inc(round_gu, 1)

            def round_down(e):
                act.wait_ge(dn_ready, e + 1)
                act.activation(hi_of(e, 2), raw_of(e, 2), ACT.Copy).then_inc(round_d, 1)

            def sh_silu(t):
                r = slice(0, ROWS[t])
                act.wait_ge(shg_mm, t + 1)
                if t >= 1:
                    act.wait_ge(sha_s, t)
                act.activation(sgs[r, :], bank(2)[r, 0:DE], ACT.Silu).then_inc(shs_s, 1)
                act.activation(ups[r, :], bank(2)[r, DE:2 * DE], ACT.Copy).then_inc(shs_s, 1)

            def sh_tail(t):
                r = slice(0, ROWS[t])
                act.wait_ge(shd_mm, t + 1)
                if t >= 2:
                    act.wait_ge(shy_st[t % 2], 16 * (t // 2))
                act.activation(shy[t % 2][r, :], pair(0)[r, :], ACT.Copy).then_inc(shy_s, 1)

            def at_copy(t):
                r = slice(0, ROWS[t])
                act.wait_ge(sht_mm, t + 1)
                src = bank(3)[:, 0:DE].rearrange("p (k n) -> p k n", k=KF)[:, :, r]
                act.activation(actTs[:, :, r], src, ACT.Copy)
                act.activation(aTsh[:, :, r], src, ACT.Copy).then_inc(ath_s, 1)

            sh_silu(0)
            for b in range(3):
                act.wait_ge(x1_st[b], 16 * 3)
            act.wait_ge(h2a_s, NT)
            round_x(1)
            act.wait_ge(log_mm, NT)
            act.wait_ge(misc_ev, 3)
            act.activation(score[:, 0:8, :], bank(6).rearrange("p (t e) -> p t e", e=NE), ACT.Sigmoid)
            act.activation(score[0:DEC, 8, :], bank(7)[0:DEC, 0:NE], ACT.Sigmoid).then_inc(score_s, 1)

            for t in range(NT):
                if t >= 1:
                    at_copy(t - 1)
                    sh_silu(t)
                if t + 2 < NT:
                    round_x(t + 2)
                if t >= 1:
                    sh_tail(t - 1)
            at_copy(NT - 1)
            act.wait_ge(shg_mm, NT)
            round_gate_up(0)
            sh_tail(NT - 1)

            def round_next(i):
                f = act.value_load(ftab[0:1, bass.ds(i + 1, 1)], min_val=0, max_val=2)
                e = act.value_load(etab[0:1, bass.ds(i + 1, 1)], min_val=0, max_val=NE - 1)
                with act.If(f > 1):
                    round_gate_up(e + 1)

            def xt_copy(i):
                act.wait_ge(xt_mm, i + 1)
                act.activation(xTh, pair(0).rearrange("p (k n) -> p k n", k=KD), ACT.Copy).then_inc(xt_s, 1)

            def silu_of(i):
                act.wait_ge(gu_mm, i + 1)
                act.activation(sg, bank(4)[:, 0:DE], ACT.Silu).then_inc(silu_s, 1)

            def at_copy(i):
                act.wait_ge(at_mm, i + 1)
                act.activation(aTh, bank(5)[:, 0:DE].rearrange("p (k n) -> p k n", k=KF), ACT.Copy).then_inc(at_s, 1)

            def y_of(i, b):
                act.wait_ge(slot_col, i + 1)
                act.wait_ge(dn_mm, i + 1)
                act.activation(yw[b], pair(2), ACT.Copy, scale=wcol[b][:, 0:1]).then_inc(yw_s, 1)

            act.wait_ge(tables, 1)
            act.wait_ge(shd_mm, NT)
            xt_copy(0)
            round_gate_up(1)
            round_down(0)
            silu_of(0)
            xt_copy(1)
            round_next(0)
            at_copy(0)
            last = act.value_load(lasti[0:1, NE - 1:NE], min_val=NE - 1, max_val=MAX_TILES - 1)

            def tile(i, odd):
                f = act.value_load(ftab[0:1, bass.ds(i, 1)], min_val=0, max_val=2)
                e = act.value_load(etab[0:1, bass.ds(i, 1)], min_val=0, max_val=NE - 1)
                with act.If(f > 0):
                    round_down(e)
                act.wait_ge(gu_mm, i + 1)
                act.wait_ge(act_s, i)
                act.activation(sg, bank(4)[:, 0:DE], ACT.Silu).then_inc(silu_s, 1)
                xt_copy(i + 1)
                round_next(i)
                y_of(i - 1, 1 - odd)
                at_copy(i)
            tiles(act, tile, last)
            last_tile(act, last, y_of)

            for g, (t0, t1) in enumerate(LAST_GROUPS):
                for t in range(t0, t1):
                    r = slice(0, ROWS[t])
                    act.wait_ge(y_in[t], 32)
                    ins = act.activation(pair(4)[r, :], y_t(t)[r, :], ACT.Square, accum_out=ss3[r, t:t + 1])
                    if t < t1 - 1:
                        link(ins)
                    else:
                        ins.then_inc(fin_ss, 1)
                act.wait_ge(fin_ms, g + 1)
                act.activation(r3[:, t0:t1], ss3[:, t0:t1], ACT.Sqrt).then_inc(fin_sq, 1)

        @block.vector
        def _(dve):
            link = chained(dve, dchain)
            dve.memset(ss1[:, :], 1.0)
            dve.memset(ss3[:, :], 1.0)
            dve.memset(ss2[:, :], 1.0)
            dve.memset(ss[:, :], 1.0).then_inc(ms_s, 1)
            dve.wait_ge(stg_t, 1)
            dve.tensor_copy(colv[:, :], bank(7)[:, 0:100]).then_inc(colv_s, 1)
            dve.wait_ge(const_pool, 2)
            link(dve.reciprocal(rec[:, :], rec[:, :]))
            def mean_eps(s):
                return dve.tensor_scalar(s, s, 1.0 / D, EPS, ALU.mult, ALU.add)

            def rms_of_three(g):
                dve.wait_ge(ss_s, g + 1)
                mean_eps(ss[:, 3 * g:3 * g + 3]).then_inc(ms_s, 1)
                dve.wait_ge(sq_s, g + 1)
                dve.reciprocal(rstd[:, 3 * g:3 * g + 3], rstd[:, 3 * g:3 * g + 3]).then_inc(rstd_s, 1)
            rms_of_three(0)
            dve.wait_ge(mcol_mm, 1)
            dve.wait_ge(colv_s, 1)
            link(dve.tensor_tensor(mods[:, :, :], bank(6)[:, 0:4 * KD].rearrange("p (r c) -> p r c", c=2),
                                   colv[:, 0:2 * KD].unsqueeze(2).to_broadcast([P, 2 * KD, 2]), ALU.add))
            dve.scalar_tensor_tensor(a1[:, :, :], mods[:, KD:2 * KD, :], 1.0,
                                     colv[:, 48:48 + KD].unsqueeze(2).to_broadcast([P, KD, 2]), ALU.add, ALU.mult)\
                .then_inc(mods_s, 1)
            dve.wait_ge(mods_s, 1)
            for t in range(NT):
                c = t // (SEQ // P)
                if t in (3, 6):
                    rms_of_three(t // 3)
                dve.wait_ge(ht_mm, t + 1)
                src = pair(2 * (t % 2))
                for k in range(KD // 2):
                    ins = dve.tensor_scalar(hT[:, k, P * t:P * t + ROWS[t]], src[:, P * k:P * k + ROWS[t]],
                                            a1[:, k, c:c + 1], mods[:, k, c:c + 1], ALU.mult, ALU.add)
                ins.then_inc(ht_s, 1)
            dve.wait_ge(misc_mm, 1)
            dve.tensor_copy(u[:, :, US:US + HIST], bank(4)[:, 0:NG * HIST].rearrange("p (g n) -> p g n", g=NG))
            dve.tensor_copy(kT[:, SEQ:SEQ + WIN], bank(5)[:, 0:WIN]).then_inc(misc_ev, 1)

            def pooling():
                dve.wait_ge(ev_s, N_U)
                dve.wait_ge(outs_mm, 1)
                dve.wait_ge(uz_s, 1)
                for g, w in enumerate(WINDOWS):
                    cur, s = u[:, g, :], 1
                    for b in range(g + 1):
                        nxt, lo = sums[b % 2], 2 * s - 1
                        link(dve.tensor_tensor(nxt[:, lo:UL], cur[:, lo:UL], cur[:, lo - s:UL - s], ALU.add))
                        cur, s = nxt, 2 * s
                    first = slice(HIST, HIST + w - 1)
                    link(dve.tensor_tensor(fix[:, 0:w - 1], cur[:, first], rec[:, 0:w - 1], ALU.mult))
                    link(dve.tensor_tensor(fix[:, 0:w - 1], fix[:, 0:w - 1], u[:, g, first], ALU.subtract))
                    link(dve.scalar_tensor_tensor(u[:, g, HIST:UL], cur[:, HIST:UL], 1.0 / w, u[:, g, HIST:UL],
                                                  ALU.mult, ALU.subtract))
                    dve.tensor_copy(u[:, g, first], fix[:, 0:w - 1]).then_inc(pooled, 1)
                    dve.wait_ge(pooled, g + 1)

            for i, (_, kind, gain_row) in enumerate(VECS):
                for k in range(KD):
                    m = KD * i + k
                    dve.wait_ge(piece_in[m % PIECES], 16 * (m // PIECES + 1))
                    for c in range(2):
                        if k == 0:
                            dve.tensor_scalar(acc[c], piece[m % PIECES], sil[:, k, c:c + 1], None, ALU.mult).then_inc(acc_s, 1)
                        else:
                            dve.wait_ge(acc_s, 2 * m + c - 1)
                            dve.scalar_tensor_tensor(acc[c], piece[m % PIECES], sil[:, k, c:c + 1], acc[c],
                                                     ALU.mult, ALU.add).then_inc(acc_s, 1)
                dve.wait_ge(bg_in, 16 * sum(1 + (g is not None) for _, _, g in VECS[:i + 1]))
                dve.wait_ge(row_mm, i + 1)
                for c in range(2):
                    row = rowsb[:, kind, c, :]
                    link(dve.tensor_tensor(row, pair(6 if c == 0 else 4), brow, ALU.add))
                    if kind == 1:
                        dve.scalar_tensor_tensor(row, row, 1.0, grow, ALU.add, ALU.mult).then_inc(row_s, 1)
                    elif gain_row is not None:
                        dve.tensor_tensor(row, row, grow, ALU.mult).then_inc(row_s, 1)
                    else:
                        dve.sem_inc(row_s, 1)
            pooling()

            def maxima(n):
                b, nk = n % 3, CHUNKS[n][2]
                dve.wait_ge(sc_mm, n + 1)
                if n >= 3:
                    dve.wait_ge(pr_s, n - 2)
                s = ps[:, 2 * (n % 2):2 * (n % 2) + 2, 0:384].rearrange("p a (c n) -> p a c n", c=2)[:, :, :, 0:nk]
                v = small[:, b, :, :]
                link(dve.tensor_reduce(v[:, 0, :], s, AX.X, ALU.max))
                link(dve.scalar_tensor_tensor(v[:, 0, :], v[:, 0, :], HD ** -0.5, sink[:, :], ALU.mult, ALU.max))
                link(dve.tensor_scalar(v[:, 1, :], v[:, 0, :], -1.0, None, ALU.mult))
                dve.tensor_tensor(v[:, 2, :], sink[:, :], v[:, 1, :], ALU.add).then_inc(mx_s, 1)

            def normalise(n):
                b, nk = n % 3, CHUNKS[n][2]
                v = small[:, b, :, :]
                dve.wait_ge(ex_s, n + 1)
                link(dve.tensor_tensor(v[:, 5, :], v[:, 3, :], v[:, 4, :], ALU.add))
                link(dve.reciprocal(v[:, 6, :], v[:, 5, :]))
                dve.tensor_tensor(probs[b][:, :, 0:nk], probs[b][:, :, 0:nk],
                                  v[:, 6, :].unsqueeze(2).to_broadcast([P, NJ, nk]), ALU.mult).then_inc(pr_s, 1)

            def copy_ptb(n):
                dve.wait_ge(pt_mm, n + 1)
                if n >= 2:
                    dve.wait_ge(pv_mm, n - 1)
                if CHUNKS[n][2] % 128:
                    dve.tensor_copy(ptb[n % 2], bank(5)[0:64, :].rearrange("p (j n) -> p j n", j=NJ)).then_inc(ptb_s, 1)
                else:
                    dve.sem_inc(ptb_s, 1)

            dve.wait_ge(misc_in, 16 * 6)
            for m in range(NCH + 2):
                if m < NCH:
                    maxima(m)
                if 1 <= m <= NCH:
                    normalise(m - 1)
                if 2 <= m <= NCH + 1:
                    copy_ptb(m - 2)

            dve.wait_ge(row_s, 8)
            for t in range(NT):
                r, c = slice(0, ROWS[t]), t // (SEQ // P)
                dve.wait_ge(ssm_s, t + 1)
                mean_eps(ss1[r, t:t + 1]).then_inc(msm_s, 1)
                dve.wait_ge(sqm_s, t + 1)
                link(dve.reciprocal(r1[r, t:t + 1], r1[r, t:t + 1]))
                dve.scalar_tensor_tensor(tmpf[r, :], pair(2 * (t % 2))[r, :], r1[r, t:t + 1], rowsb[r, 0, c, :],
                                         ALU.mult, ALU.mult).then_inc(res_s, 1)
                dve.wait_ge(ssx_s, t + 1)
                mean_eps(ss2[r, t:t + 1]).then_inc(msx_s, 1)
                dve.wait_ge(sqx_s, t + 1)
                link(dve.reciprocal(r2[r, t:t + 1], r2[r, t:t + 1]))
                dve.scalar_tensor_tensor(junkf[r, :], xf(t)[r, :], r2[r, t:t + 1], rowsb[r, 1, c, :],
                                         ALU.mult, ALU.mult).then_inc(h2a_s, 1)
                if t in (4, 6):
                    m = t - 4
                    dve.wait_ge(wsh_hi, m + 1)
                    dve.tensor_tensor(sh_lo(m), sh_raw(m), sh_hi(m).bitcast(F32), ALU.subtract).then_inc(wsh_lo, 1)

            dve.wait_ge(h2_s, NT)
            dve.wait_ge(log_mm, NT)
            dve.memset(score[:, 8, :], 0.0).then_inc(misc_ev, 2)
            dve.wait_ge(score_s, 1)
            bias9 = rbias[:, :].unsqueeze(1).to_broadcast([P, NT, NE])
            link(dve.tensor_tensor(sel, score, bias9, ALU.add))
            for t in range(NT):
                for g in range(EG):
                    ins = dve.max(g8[:, t, g, :], sel[:, t, EG * g:EG * g + 8])
            link(ins)
            link(dve.tensor_tensor(gs[:, :, :], g8[:, :, :, 0], g8[:, :, :, 1], ALU.add))
            half = NT * EG * EG
            above = rtmp.bitcast(BF16)[:, 0:half].rearrange("p (t i j) -> p t i j", t=NT, i=EG)
            equal = rtmp.bitcast(BF16)[:, half:2 * half].rearrange("p (t i j) -> p t i j", t=NT, i=EG)
            of_j = gs[:, :, :].unsqueeze(2).to_broadcast([P, NT, EG, EG])
            of_i = gs[:, :, :].unsqueeze(3).to_broadcast([P, NT, EG, EG])
            dve.tensor_tensor(above, of_j, of_i, ALU.is_gt)
            link(dve.tensor_tensor(equal, of_j, of_i, ALU.is_equal))
            link(dve.tensor_tensor(equal, equal, lower8[:, :, :].unsqueeze(1).to_broadcast([P, NT, EG, EG]), ALU.mult))
            link(dve.tensor_tensor(above, above, equal, ALU.add))
            link(dve.tensor_reduce(gm[:, :, :], above, AX.X, ALU.add))
            link(dve.tensor_scalar(gm[:, :, :], gm[:, :, :], TOPG - 0.5, -1.0, ALU.is_lt, ALU.add))
            link(dve.tensor_scalar(gm[:, :, :], gm[:, :, :], 3.0e38, None, ALU.mult))
            link(dve.tensor_tensor(sel.rearrange("p t (g e) -> p t g e", g=EG), sel.rearrange("p t (g e) -> p t g e", g=EG),
                                   gm[:, :, :].unsqueeze(3).to_broadcast([P, NT, EG, 8]), ALU.add))
            for t in range(NT):
                ins = dve.max(top8[:, t, :], sel[:, t, :])
            link(ins)
            for t in range(NT):
                ins = dve.max_index(ix8[:, t, :], top8[:, t, :], sel[:, t, :])
            link(ins)
            link(dve.tensor_copy(ixf[:, :, :], ix8[:, :, :]))
            hit = rtmp.bitcast(BF16).rearrange("p (t e k) -> p t e k", t=NT, e=NE)
            link(dve.tensor_tensor(hit, iotae[:, :].unsqueeze(1).unsqueeze(3).to_broadcast([P, NT, NE, TOPK]),
                                   ixf[:, :, 0:TOPK].unsqueeze(2).to_broadcast([P, NT, NE, TOPK]), ALU.is_equal))
            link(dve.tensor_reduce(mask, hit, AX.X, ALU.add))
            link(dve.memset(mask[DEC:P, NT - 1, :], 0.0))
            dve.tensor_copy(maskb, mask).then_inc(maskb_s, 1)
            wn = sel
            link(dve.tensor_tensor(wn, mask, score, ALU.mult))
            link(dve.tensor_reduce(den[:, :], wn, AX.X, ALU.add))
            link(dve.memset(den[DEC:P, NT - 1:NT], 1.0))
            link(dve.reciprocal(den[:, :], den[:, :]))
            link(dve.scalar_tensor_tensor(wn, wn, SCALE_R, den[:, :].unsqueeze(2).to_broadcast([P, NT, NE]),
                                          ALU.mult, ALU.mult))
            link(dve.tensor_copy(wp[:, :, :, 2], wn))
            link(dve.tensor_tensor(wn, wn, wp[:, :, :, 2], ALU.subtract))
            link(dve.tensor_copy(wp[:, :, :, 3], wn))
            link(dve.tensor_tensor(wp[:, :, :, 4], wn, wp[:, :, :, 3], ALU.subtract))
            dve.tensor_copy(wp[:, :, :, 0], base[:, 0:NT].unsqueeze(2).to_broadcast([P, NT, NE]))
            link(dve.tensor_scalar(wp[:, :, :, 1], mask, 0.0, prow[:, 0:1], ALU.mult, ALU.add))
            dve.wait_ge(rank_mm, 1)
            dve.memset(ntl[:, :], 1.0)
            link(dve.tensor_copy(cnt[:, :], bank(7)[:, NE:2 * NE]))
            for j in range(1, NT):
                link(dve.scalar_tensor_tensor(ntl[:, :], cnt[:, :], float(P * j), ntl[:, :], ALU.is_gt, ALU.add))
            link(dve.tensor_tensor_scan(tend[:, :], ones[:, 0:NE], ntl[:, :], 0.0, ALU.mult, ALU.add))
            link(dve.tensor_tensor(tst[:, :], tend[:, :], ntl[:, :], ALU.subtract))
            link(dve.tensor_scalar(tst[:, :], tst[:, :], float(P), 1.0, ALU.mult, ALU.add))
            start9 = tst[:, :].unsqueeze(1).to_broadcast([P, NT, NE])
            dve.tensor_tensor(sel[:, 0:8, :], bank(6).rearrange("p (t e) -> p t e", e=NE), start9[:, 0:8, :], ALU.add)
            link(dve.tensor_tensor(sel[:, 8:9, :], bank(7)[:, 0:NE].unsqueeze(1), start9[:, 8:9, :], ALU.add))
            link(dve.tensor_tensor(pos.rearrange("p e t -> p t e"), sel, mask, ALU.mult))
            dve.tensor_scalar(lasti[:, :], tend[0:1, :], -1.0, None, ALU.add)
            link(dve.tensor_scalar(cnt, tend[:, :], float(P), None, ALU.mult))
            ef = score[0:1, 0:4, :].rearrange("p t e -> p (t e)")[:, 0:TAB]
            step = NT * NE * TOPK // NE
            for a in range(0, TAB, step):
                m = min(step, TAB - a)
                past = rtmp[0:1, :].bitcast(BF16)[:, 0:m * NE].rearrange("p (i e) -> p i e", e=NE)
                link(dve.tensor_tensor(past, cnt[0:1, :].unsqueeze(1).to_broadcast([1, m, NE]),
                                       base[0:1, a:a + m].unsqueeze(2).to_broadcast([1, m, NE]), ALU.is_le))
                link(dve.tensor_reduce(ef[:, a:a + m], past, AX.X, ALU.add))
            link(dve.tensor_scalar(ef, ef, float(NE - 1), None, ALU.min))
            first = rtmp[0:1, 0:TAB]
            link(dve.memset(first[:, 0:1], 1.0))
            link(dve.tensor_tensor(first[:, 1:TAB], ef[:, 1:TAB], ef[:, 0:TAB - 1], ALU.is_gt))
            link(dve.tensor_scalar(rtmp[0:1, TAB:2 * TAB], ef, float(NE - 1), 1.0, ALU.is_lt, ALU.add))
            dve.tensor_tensor(ftab[:, :], first, rtmp[0:1, TAB:2 * TAB], ALU.mult)
            dve.tensor_copy(etab[:, :], ef).then_inc(tables, 1)
            dve.wait_ge(tables, 1)
            dve.wait_ge(xl_s, NT)

            def one_hot(i, e=None):
                if e is None:
                    e = dve.value_load(etab[0:1, bass.ds(i, 1)], min_val=0, max_val=NE - 1)
                dve.scalar_tensor_tensor(oh, pos[:, bass.ds(e, 1), :].rearrange("p a t -> p t a").to_broadcast([P, NT, P]),
                                         base[:, bass.ds(i, 1)], iota1[:, :].unsqueeze(1).to_broadcast([P, NT, P]),
                                         ALU.subtract, ALU.is_equal).then_inc(oh_s, 1)

            def slots(i, b, first=False):
                s = bank(6)
                if not first:
                    dve.wait_ge(gathered[b], 8 * (i - b))
                dve.wait_ge(slot_mm, i + 1)
                dve.tensor_reduce(sl[:, 0:1], s[:, 0:2], AX.X, ALU.add)
                dve.tensor_reduce(wtab[:, bass.ds(i, 1)], s[:, 2:5], AX.X, ALU.add).then_inc(dstep, 1)
                dve.wait_ge(dstep, 2 * i + 1)
                dve.tensor_scalar(sl[:, 1:2], sl[:, 0:1], 0.0, padcol[:, 0:1], ALU.is_equal, ALU.mult).then_inc(dstep, 1)
                dve.wait_ge(dstep, 2 * i + 2)
                dve.scalar_tensor_tensor(itab[:, bass.ds(i, 1)], sl[:, 0:1], -1.0, sl[:, 1:2], ALU.add, ALU.add)
                dve.scalar_tensor_tensor(idxg[b][:, 0:1], sl[:, 0:1], -1.0, sl[:, 1:2], ALU.add, ALU.add).then_inc(idx_s, 1)

            def act_of(i):
                dve.wait_ge(silu_s, i + 1)
                dve.tensor_tensor(act_m, sg, bank(4)[:, DE:2 * DE], ALU.mult).then_inc(act_s, 1)

            def mat_rest(e, m):
                dve.wait_ge(round_gu, 2 * e + m + 1)
                split_rest(dve, e, m).then_inc(lo_gu, 1)

            def gate_up_rest(e):
                for m in range(2):
                    mat_rest(e, m)

            def xt_rest(i):
                dve.wait_ge(xt_s, i + 1)
                dve.tensor_tensor(xTl, pair(0).rearrange("p (k n) -> p k n", k=KD), xTh.bitcast(F32), ALU.subtract)\
                    .then_inc(xtl_s, 1)

            def at_rest(i):
                dve.wait_ge(at_s, i + 1)
                dve.tensor_tensor(aTl, bank(5)[:, 0:DE].rearrange("p (k n) -> p k n", k=KF), aTh.bitcast(F32), ALU.subtract)\
                    .then_inc(atl_s, 1)

            def slot_columns(i, b):
                dve.tensor_copy(wcol[b][:, 0:1], wtab[:, bass.ds(i, 1)])
                dve.tensor_copy(idxs[b][:, 0:1], itab[:, bass.ds(i, 1)]).then_inc(slot_col, 1)

            dve.sem_inc(yw_s, 1)
            one_hot(0)
            slots(0, 0, first=True)
            one_hot(1)
            slots(1, 1, first=True)
            gate_up_rest(0)
            xt_rest(0)
            one_hot(2)
            gate_up_rest(1)
            act_of(0)
            xt_rest(1)
            slots(2, 0)
            one_hot(3)
            slots(3, 1)
            one_hot(4)
            last = dve.value_load(lasti[0:1, NE - 1:NE], min_val=NE - 1, max_val=MAX_TILES - 1)

            def rests(i):
                f = dve.value_load(ftab[0:1, bass.ds(i + 1, 1)], min_val=0, max_val=2)
                e = dve.value_load(etab[0:1, bass.ds(i + 1, 1)], min_val=0, max_val=NE - 1)
                with dve.If(f > 1):
                    mat_rest(e + 1, 0)
                at_rest(i)
                with dve.If(f > 1):
                    mat_rest(e + 1, 1)
            rests(0)

            def tile(i, odd):
                act_of(i)
                xt_rest(i + 1)
                e = dve.value_load(etab[0:1, bass.ds(i + AHEAD + 1, 1)], min_val=0, max_val=NE - 1)
                slots(i + AHEAD, 1 - odd)
                dve.wait_ge(added, 16 * i)
                slot_columns(i - 1, 1 - odd)
                one_hot(i + AHEAD + 1, e)
                rests(i)
            tiles(dve, tile, last)
            dve.wait_ge(added, 16 * (last + 1))
            last_tile(dve, last, slot_columns)

            for g, (t0, t1) in enumerate(LAST_GROUPS):
                dve.wait_ge(fin_ss, g + 1)
                mean_eps(ss3[:, t0:t1]).then_inc(fin_ms, 1)
                dve.wait_ge(fin_sq, g + 1)
                link(dve.reciprocal(r3[:, t0:t1], r3[:, t0:t1]))
                for t in range(t0, t1):
                    r, c = slice(0, ROWS[t]), t // (SEQ // P)
                    dve.scalar_tensor_tensor(y_t(t)[r, :], y_t(t)[r, :], r3[r, t:t + 1], rowsb[r, 3, c, :],
                                             ALU.mult, ALU.mult).then_inc(fin_g, 1)
                    if t % 2:
                        dve.wait_ge(fin_g, t + 1)
                        dve.tensor_tensor(x1_t(t)[r, :], x1_t(t)[r, :], y_t(t)[r, :], ALU.add).then_inc(fin_s[t % 2], 1)

        @block.tensor
        def _(pe):
            pe.wait_ge(const_pool, 1)
            pe.wait_ge(small_in, 16 * 5)
            pe.transpose(bank(7)[:, 0:100], stg[:, :], ident[0:100, 0:100]).then_inc(stg_t, 1)

            def transposes(t):
                r = slice(0, ROWS[t])
                pe.wait_ge(xn_s, t + 1)
                if t >= 2:
                    pe.wait_ge(ht_s, t - 1)
                    pe.wait_ge(hta_s, t - 1)
                for k in range(KD):
                    ins = pe.transpose(pair(2 * (t % 2))[:, P * k:P * k + ROWS[t]], xb[t % 6][r, P * k:P * (k + 1)],
                                       ident[r, r])
                ins.then_inc(ht_mm, 1)

            pe.wait_ge(sil_s, 1)
            for b in range(4):
                pe.wait_ge(ada_in[b], 16)
                for k in range(KD):
                    ins = pe.matmul(bank(b)[0:2, :], sil[:, k, :], ada[b][:, k, :], start=(k == 0), stop=(k == KD - 1))
                ins.then_inc(ada_mm, 1)
            pe.wait_ge(mrow_s, 4)
            for r_ in range(2 * KD):
                ins = pe.transpose(bank(6)[:, 2 * r_:2 * r_ + 2], mrow[:, P * r_:P * (r_ + 1)], ident[0:2, 0:2])
            ins.then_inc(mcol_mm, 1)
            for t in range(NT):
                transposes(t)

            pe.wait_ge(misc_in, 16 * 6)
            pe.wait_ge(rstd_s, 3)
            for g in range(NG):
                pe.transpose(bank(4)[:, HIST * g:HIST * (g + 1)], stin[:, P * g:P * (g + 1)], ident[0:HIST, 0:HIST])
            pe.transpose(bank(5)[:, 0:WIN], ckin[:, :], ident[:, :]).then_inc(misc_mm, 1)

            def ada_rows(i):
                pe.wait_ge(acc_s, 2 * KD * (i + 1))
                if i >= 1:
                    pe.wait_ge(row_s, 2 * i)
                for c in range(2):
                    for half in range(2):
                        ins = pe.matmul(bank((6 if c == 0 else 4) + half), ones[:, :], acc[c][:, 512 * half:512 * (half + 1)],
                                        start=True, stop=True)
                ins.then_inc(row_mm, 1)

            pe.wait_ge(w_in_s[0], 16)
            pe.wait_ge(misc_ev, 1)
            for n, (kind, c, a, n_) in enumerate(groups):
                if n == 0:
                    pe.wait_ge(ht_s, NT)
                    pe.wait_ge(hta_s, NT)
                if n == N_U:
                    pe.wait_ge(w_in_s[1], 16)
                if n == N_V:
                    pe.wait_ge(w_in_s[2], 16)
                if n in ROWS_AT:
                    ada_rows(ROWS_AT.index(n))
                if n >= 4:
                    pe.wait_ge(ev_s, n - 3)
                out = bank(n % 4)
                if kind == "ct":
                    for k in range(KD):
                        ins = pe.matmul(out[:, 0:n_], w1[:, k, P * c:P * (c + 1)], hT[:, k, a:a + n_], start=(k == 0), stop=(k == KD - 1))
                elif kind == "v":
                    for t in range(4 * c, min(4 * c + 4, NT)):
                        o = out[0:ROWS[t], P * (t % 4):P * (t % 4) + KV]
                        for k in range(KD):
                            ins = pe.matmul(o, hT[:, k, P * t:P * t + ROWS[t]], w1[:, k, INW - KV:INW],
                                            start=(k == 0), stop=(k == KD - 1))
                else:
                    pe.wait_ge(pooled, c + 1)
                    pe.wait_ge(wpool_s, 16)
                    o = HIST + a if a < SEQ else US + HIST
                    ins = pe.matmul(out[:, 0:n_], wpool[:, c, :], u[:, c, o:o + n_], start=True, stop=True)
                ins.then_inc(proj_mm, 1)
                if n == LAST_U:
                    pe.wait_ge(ev_s, N_U)
                    pe.wait_ge(row_s, 8)
                    for g in range(NG):
                        pe.transpose(bank(4)[0:HIST, P * g:P * (g + 1)], u[:, g, US - HIST:US], ident[:, :])
                        ins = pe.transpose(bank(5)[0:HIST, P * g:P * (g + 1)], u[:, g, UL - HIST:UL], ident[:, :])
                    ins.then_inc(outs_mm, 1)
                if n == N_PROJ - 1:
                    pe.wait_ge(ev_s, N_PROJ)
                    pe.transpose(bank(6)[:, 0:KV], kT[:, SEQ - WIN:SEQ], ident[:, :])
                    pe.transpose(bank(6)[0:DEC, KV:2 * KV], kT[:, SEQ + WIN:KL], ident[:, :]).then_inc(outs_mm, 1)

            def scores(n):
                b, (qc, kc, nk, _, _) = n % 2, CHUNKS[n]
                pe.wait_ge(qbd_s, 2 * (n + 1))
                if n >= 2:
                    pe.wait_ge(ex_s, n - 1)
                for j in range(NJ):
                    ins = pe.matmul(ps[:, 2 * b + j // 2, 192 * (j % 2):192 * (j % 2) + nk], qbd[b][:, j, :],
                                    kT[:, kc:kc + nk], start=True, stop=True)
                ins.then_inc(sc_mm, 1)

            def prob_t(n):
                b, nk = n % 3, CHUNKS[n][2]
                pe.wait_ge(pr_s, n + 1)
                if n >= 1:
                    pe.wait_ge(pta_s, n)
                    pe.wait_ge(ptb_s, n)
                for j in range(NJ):
                    if nk >= 128:
                        ins = pe.transpose(bank(4)[:, P * j:P * (j + 1)], probs[b][:, j, 0:128], ident[:, :])
                    if nk % 128:
                        ins = pe.transpose(bank(5)[0:64, P * j:P * (j + 1)], probs[b][:, j, nk - 64:nk], ident[:, :])
                ins.then_inc(pt_mm, 1)

            def pv(n):
                b, (_, _, nk, where, tile) = n % 2, CHUNKS[n]
                v = vodd if where == "odd" else vt
                pe.wait_ge(pta_s, n + 1)
                pe.wait_ge(ptb_s, n + 1)
                if n >= 2:
                    pe.wait_ge(o_s, n - 1)
                for h in range(2):
                    r = slice(64 * h, 64 * h + 64)
                    out = bank(6 + b)[r, 0:NJ * CHUNK]
                    if nk >= 128:
                        ins = pe.matmul(out, v[:, tile, r], pta[b][:, :, r], start=True, stop=(nk == 128))
                    if nk % 128:
                        ins = pe.matmul(out, v[0:64, tile + 1, r], ptb[b][:, :, r], start=(nk == 64), stop=True)
                ins.then_inc(pv_mm, 1)

            pe.wait_ge(ev_s, len(groups))
            pe.wait_ge(outs_ev, 1)
            pe.wait_ge(vodd_s, 48)
            for m in range(NCH + 3):
                if m < NCH:
                    scores(m)
                if 2 <= m <= NCH + 1:
                    prob_t(m - 2)
                if m >= 3:
                    pv(m - 3)

            pe.wait_ge(o_s, NCH)
            pe.wait_ge(w_out_s, 48)

            def mix(t):
                if t >= 2:
                    pe.wait_ge(res_s, t - 1)
                for half in range(2):
                    for k in range(KD):
                        ins = pe.matmul(bank(2 * (t % 2) + half)[0:ROWS[t], :], hT[:, k, P * t:P * t + ROWS[t]],
                                        wo[:, k, 512 * half:512 * half + 512], start=(k == 0), stop=(k == KD - 1))
                ins.then_inc(mix_mm, 1)

            def h2_t(t):
                r = slice(0, ROWS[t])
                pe.wait_ge(h2_s, t + 1)
                if t >= 1:
                    pe.wait_ge(h2t_s, t)
                for k in range(KD):
                    ins = pe.transpose(pair(4)[:, P * k:P * k + ROWS[t]], h2p[t % 2][r, P * k:P * (k + 1)], ident[r, r])
                ins.then_inc(h2t_mm, 1)

            def logits(t):
                pe.wait_ge(h2t_s, t + 1)
                out = bank(6 + t // 8)[0:ROWS[t], NE * (t % 8):NE * (t % 8 + 1)]
                for k in range(KD):
                    ins = pe.matmul(out, hT[:, k, P * t:P * t + ROWS[t]], wrt[:, k, :], start=(k == 0), stop=(k == KD - 1))
                ins.then_inc(log_mm, 1)

            for t in range(NT):
                mix(t)
                if t >= 1:
                    h2_t(t - 1)
                if t >= 2:
                    logits(t - 2)
            logits(NT - 2)

            def passes(out, at_h, at_l, w_h, w_l, k, first, last):
                pe.matmul(out, at_h[:, k, :], w_h, start=first, stop=False)
                pe.matmul(out, at_h[:, k, :], w_l, start=False, stop=False)
                return pe.matmul(out, at_l[:, k, :], w_h, start=False, stop=last)

            def swiglu_in(b, xh, xl, wh, wl):
                gh, gl = [w.rearrange("p (m k n) -> p m k n", m=2, k=KD) for w in (wh, wl)]
                for k in range(KD):
                    ins = passes(bank(b), xh, xl, gh[:, :, k, :], gl[:, :, k, :], k, k == 0, k == KD - 1)
                return ins

            def swiglu_out(b, ah, al, wh, wl):
                for half in range(2):
                    c = slice(512 * half, 512 * half + 512)
                    dh, dl = [w.rearrange("p (k n) -> p k n", k=KF) for w in (wh, wl)]
                    for k in range(KF):
                        ins = passes(bank(b + half), ah, al, dh[:, k, c], dl[:, k, c], k, k == 0, k == KF - 1)
                return ins

            at_lo = 3 * WSLOT

            def sh_in(t):
                pe.wait_ge(xl_s, t + 1)
                if t >= 1:
                    pe.wait_ge(shs_s, 2 * t)
                swiglu_in(2, Xh[t % 2], Xl[t % 2], hi_gu[:, 0:2 * MAT], lor[:, at_lo:at_lo + 2 * MAT]).then_inc(shg_mm, 1)


            def sh_out(t):
                pe.wait_ge(sht_s, t + 1)
                if t >= 1:
                    pe.wait_ge(shy_s, t)
                swiglu_out(0, aTsh, aTsl, hi_dn[:, 0:MAT], lor[:, at_lo + 2 * MAT:at_lo + 3 * MAT]).then_inc(shd_mm, 1)

            def sh_t(t):
                r = slice(0, ROWS[t])
                pe.wait_ge(sha_s, t + 1)
                if t >= 1:
                    pe.wait_ge(shd_mm, t)
                for k in range(KF):
                    ins = pe.transpose(bank(3)[:, P * k:P * k + ROWS[t]], acts[r, P * k:P * (k + 1)], ident[r, r])
                ins.then_inc(sht_mm, 1)

            pe.wait_ge(wsh_lo, 3)
            pe.wait_ge(res_s, NT - 1)
            sh_in(0)
            h2_t(NT - 1)
            logits(NT - 1)
            pe.wait_ge(res_s, NT)
            for t in range(NT):
                if t >= 1:
                    sh_t(t - 1)
                    sh_in(t)
                if t >= 1:
                    sh_out(t - 1)
                if t == 4:
                    pe.wait_ge(maskb_s, 1)
                    for tt in range(NT + 1):
                        out = bank(6)[:, NE * tt:NE * (tt + 1)] if tt < 8 else bank(7)[:, NE * (tt - 8):NE * (tt - 7)]
                        for s in range(min(tt + 1, NT)):
                            ins = pe.matmul(out, (triub if s == tt else onesb)[:, :], maskb[:, s, :],
                                            start=(s == 0), stop=(s == min(tt, NT - 1)))
                    ins.then_inc(rank_mm, 1)

            def expert(i):
                return pe.value_load(etab[0:1, bass.ds(i, 1)], min_val=0, max_val=NE - 1)

            def slots(i, e=None, first=False):
                e = expert(i) if e is None else e
                if not first:
                    pe.wait_ge(idx_s, i)
                pe.wait_ge(oh_s, i + 1)
                for t in range(NT):
                    ins = pe.matmul(bank(6)[:, 0:5], oh[:, t, :], wp[:, t, bass.ds(e, 1), :].rearrange("p a c -> p (a c)"),
                                    start=(t == 0), stop=(t == NT - 1))
                ins.then_inc(slot_mm, 1)

            def x_t(i, b):
                pe.wait_ge(gathered[b], 8 * (i - b) + 16)
                for k in range(KD):
                    ins = pe.transpose(pair(0)[:, P * k:P * (k + 1)], xg[b][:, P * k:P * (k + 1)], ident[:, :])
                ins.then_inc(xt_mm, 1)

            def expert_in(i, e):
                pe.wait_ge(lo_gu, 2 * e + 2)
                pe.wait_ge(xtl_s, i + 1)
                swiglu_in(4, xTh, xTl, hi_of(e, 0, 2), lo_of(e, 0, 2)).then_inc(gu_mm, 1)

            def act_t(i):
                pe.wait_ge(act_s, i + 1)
                for k in range(KF):
                    ins = pe.transpose(bank(5)[:, P * k:P * (k + 1)], act_m[:, P * k:P * (k + 1)], ident[:, :])
                ins.then_inc(at_mm, 1)

            def expert_out(i, e):
                pe.wait_ge(yw_s, i + 1)
                pe.wait_ge(lo_d, e + 1)
                pe.wait_ge(atl_s, i + 1)
                swiglu_out(2, aTh, aTl, hi_of(e, 2), lo_of(e, 2)).then_inc(dn_mm, 1)

            sh_t(NT - 1)
            pe.wait_ge(tables, 1)
            slots(0, first=True)
            sh_out(NT - 1)
            slots(1)
            pe.wait_ge(shy_s, NT)
            x_t(0, 0)
            expert_in(0, expert(0))
            x_t(1, 1)
            slots(2)
            slots(3)
            last = pe.value_load(lasti[0:1, NE - 1:NE], min_val=NE - 1, max_val=MAX_TILES - 1)

            def tile(i, odd):
                e_out, e_in, e_next = expert(i - 1), expert(i), expert(i + AHEAD)
                act_t(i - 1)
                expert_in(i, e_in)
                x_t(i + 1, 1 - odd)
                slots(i + AHEAD, e_next)
                expert_out(i - 1, e_out)
            tiles(pe, tile, last)
            act_t(last)
            expert_out(last, expert(last))


_INS = ["x_prompt", "x_sample", "c_prompt", "c_sample", "state_pool", "cache_k", "cache_v", "w_ada", "b_ada",
        "norm_gains", "w_in", "w_pool", "pool_scale", "attn_sinks", "w_out", "w_router", "router_bias",
        "w_gate", "w_up", "w_down", "ws_gate", "ws_up", "ws_down"]
_OUTS = [(1, SEQ, D), (1, DEC, D), (1, 1, HIST, PW), (1, 1, WIN, 2, HD), (1, 1, WIN, 2, HD),
         (1, 1, HIST, PW), (1, 1, WIN, 2, HD), (1, 1, WIN, 2, HD)]


def kernel(**inputs):
    import numpy as _np
    import concourse.bacc as _bacc
    from concourse import mybir as _mybir
    from concourse.bass_utils import run_bass_kernel_spmd as _run

    nc = _bacc.Bacc("TRN2", target_bir_lowering=False, num_devices=1)
    arrays, args = {}, []
    for name in _INS:
        a = _np.asarray(inputs[name])
        if name == "w_in":
            qcols = a[..., PW:PW + 512].reshape(1, D, 2, NJ, HD).transpose(0, 1, 3, 2, 4).reshape(1, D, 512)
            a = _np.concatenate([a[..., :PW], qcols, a[..., PW + 512:]], axis=-1)
        a = _np.ascontiguousarray(a)
        arrays[f"in_{name}_dram"] = a
        args.append(nc.dram_tensor(f"in_{name}_dram", a.shape, _mybir.dt.from_np(a.dtype), kind="ExternalInput").ap())
    for i, shape in enumerate(_OUTS):
        args.append(nc.dram_tensor(f"out_{i}_dram", shape, F32, kind="ExternalOutput").ap())
    build(nc, *args)
    r = _run(nc, [arrays], core_ids=[0])
    return tuple(r.results[0][f"out_{i}_dram"] for i in range(len(_OUTS)))
```
